# Optimizing a Trainium2 kernel written in Bass

```python
import jax, jax.numpy as jnp
from jax import lax
import numpy as np

D_MODEL = 1024
BATCH = 1
SEQ = 256
DEPTH = 1

RET_HEADS = 4
RET_DK = 128
RET_DV = 256
RET_CHUNK = 128
ROPE_BASE = 10000.0
MOBA_HEADS = 8
MOBA_DH = 64
MOBA_BLOCK = 256
MOBA_TOPK = 3
MOBA_QBLOCK = 64
FFN_HIDDEN = ((8 * D_MODEL + 3 * 256 - 1) // (3 * 256)) * 256

RET_QK = RET_HEADS * RET_DK
RET_V = RET_HEADS * RET_DV
MOBA_W = MOBA_HEADS * MOBA_DH
IN_SPLITS = (RET_QK, RET_QK, RET_V, RET_V, MOBA_W, MOBA_W, MOBA_W, D_MODEL, D_MODEL)
IN_COLS = sum(IN_SPLITS)

RMS_EPS = 1e-6
GN_EPS = 1e-5
NEG = -1e30


def rmsnorm(x, w):
    xf = x.astype(jnp.float32)
    y = xf * lax.rsqrt(jnp.mean(xf * xf, axis=-1, keepdims=True) + RMS_EPS)
    return (y * w.astype(jnp.float32)).astype(x.dtype)

def rotary(x, pos):
    half = x.shape[-1] // 2
    inv = ROPE_BASE ** (-jnp.arange(half, dtype=jnp.float32) / half)
    ang = pos.astype(jnp.float32)[:, None] * inv[None, :]
    cos = jnp.cos(ang)[None, :, None, :].astype(x.dtype)
    sin = jnp.sin(ang)[None, :, None, :].astype(x.dtype)
    x1, x2 = x[..., :half], x[..., half:]
    return jnp.concatenate([x1 * cos - x2 * sin, x2 * cos + x1 * sin], axis=-1)

def retention(q, k, v):
    B, S, H, _ = q.shape
    dv = v.shape[-1]
    C = RET_CHUNK
    NC = S // C
    dt = q.dtype

    def chunks(t):
        return t.reshape(B, NC, C, H, t.shape[-1]).transpose(0, 3, 1, 2, 4)

    qc, kc, vc = chunks(q), chunks(k), chunks(v)
    lg = jnp.log1p(-jnp.exp2(-5.0 - jnp.arange(H, dtype=jnp.float32)))
    idx = jnp.arange(C, dtype=jnp.float32)
    diff = idx[:, None] - idx[None, :]
    dmat = jnp.where(diff >= 0, jnp.exp(jnp.maximum(diff, 0.0)[None] * lg[:, None, None]), 0.0).astype(dt)
    xi = jnp.exp((idx + 1.0)[None, :] * lg[:, None]).astype(dt)
    zeta = jnp.exp((C - 1.0 - idx)[None, :] * lg[:, None]).astype(dt)
    g_chunk = jnp.exp(C * lg).astype(dt)

    scores = jnp.einsum('bhcnd,bhcmd->bhcnm', qc, kc) * dmat[None, :, None]
    o_inner = jnp.einsum('bhcnm,bhcme->bhcne', scores, vc)
    upd = jnp.einsum('bhcmd,bhcme->bhcde', kc * zeta[None, :, None, :, None], vc)
    upd = jnp.moveaxis(upd, 2, 0)

    def step(state, u):
        return g_chunk[None, :, None, None] * state + u, state

    _, r_prev = lax.scan(step, jnp.zeros_like(upd[0]), upd)
    r_prev = jnp.moveaxis(r_prev, 0, 2)
    o_cross = jnp.einsum('bhcnd,bhcde->bhcne', qc * xi[None, :, None, :, None], r_prev)
    o = (o_inner + o_cross).transpose(0, 2, 3, 1, 4).reshape(B, S, H, dv)
    of = o.astype(jnp.float32)
    mu = jnp.mean(of, axis=-1, keepdims=True)
    var = jnp.mean(jnp.square(of - mu), axis=-1, keepdims=True)
    o = ((of - mu) * lax.rsqrt(var + GN_EPS)).astype(dt)
    return o.reshape(B, S, H * dv)

def gather_blocks(blocks, sel):
    return jax.vmap(jax.vmap(lambda bl, ix: bl[ix]))(blocks, sel)

def moba_attention(q, k, v):
    B, S, H, dh = q.shape
    BLK, QB = MOBA_BLOCK, MOBA_QBLOCK
    sp = ((S + BLK - 1) // BLK) * BLK
    pad = ((0, 0), (0, sp - S), (0, 0), (0, 0))
    qh = jnp.pad(q, pad).transpose(0, 2, 1, 3)
    kh = jnp.pad(k, pad).transpose(0, 2, 1, 3)
    vh = jnp.pad(v, pad).transpose(0, 2, 1, 3)
    nb = sp // BLK
    kb = kh.reshape(B, H, nb, BLK, dh)
    vb = vh.reshape(B, H, nb, BLK, dh)
    kbar = jnp.mean(kb, axis=3)
    topk = min(MOBA_TOPK, nb)
    scale = dh ** -0.5
    n_qb = sp // QB

    def one_block(qi):
        start = qi * QB
        blk = start // BLK
        qb = lax.dynamic_slice_in_dim(qh, start, QB, axis=2)
        gate = jnp.einsum('bhqd,bhnd->bhqn', qb, kbar).astype(jnp.float32)
        gate = jnp.where(jnp.arange(nb)[None, None, None, :] < blk, gate, NEG)
        _, sel = lax.top_k(gate, topk)
        valid = sel < blk
        ks = gather_blocks(kb, sel)
        vs = gather_blocks(vb, sel)
        s_sel = jnp.einsum('bhqd,bhqkjd->bhqkj', qb, ks).astype(jnp.float32) * scale
        s_sel = jnp.where(valid[..., None], s_sel, NEG).reshape(B, H, QB, topk * BLK)
        k_own = lax.dynamic_index_in_dim(kb, blk, axis=2, keepdims=False)
        v_own = lax.dynamic_index_in_dim(vb, blk, axis=2, keepdims=False)
        s_own = jnp.einsum('bhqd,bhjd->bhqj', qb, k_own).astype(jnp.float32) * scale
        qpos = start + jnp.arange(QB)
        kpos = blk * BLK + jnp.arange(BLK)
        s_own = jnp.where(kpos[None, :] <= qpos[:, None], s_own, NEG)
        p = jax.nn.softmax(jnp.concatenate([s_sel, s_own], axis=-1), axis=-1)
        p_sel = p[..., :topk * BLK].reshape(B, H, QB, topk, BLK).astype(v.dtype)
        p_own = p[..., topk * BLK:].astype(v.dtype)
        return (jnp.einsum('bhqkj,bhqkjd->bhqd', p_sel, vs)
                + jnp.einsum('bhqj,bhjd->bhqd', p_own, v_own))

    out = lax.map(one_block, jnp.arange(n_qb))
    out = out.transpose(1, 0, 3, 2, 4).reshape(B, sp, H * dh)
    return out[:, :S]

def first_inputs(seed: int = 0) -> dict:
    key = jax.random.key(seed)
    ks = jax.random.split(key, 12)

    def w(k, shape, fan_in):
        return jax.random.normal(k, shape, jnp.float32) * fan_in ** -0.5

    def gain(k, shape):
        return 1.0 + 0.02 * jax.random.normal(k, shape, jnp.float32)

    return {
        "x": jax.random.normal(ks[0], (BATCH, SEQ, D_MODEL), jnp.float32),
        "norm1_w": gain(ks[1], (DEPTH, D_MODEL)),
        "w_in": w(ks[2], (DEPTH, D_MODEL, IN_COLS), D_MODEL),
        "q_norm_w": gain(ks[3], (DEPTH, MOBA_DH)),
        "k_norm_w": gain(ks[4], (DEPTH, MOBA_DH)),
        "w_ret_out": w(ks[5], (DEPTH, RET_V, D_MODEL), RET_V),
        "w_moba_out": w(ks[6], (DEPTH, MOBA_W, D_MODEL), MOBA_W),
        "w_o": w(ks[7], (DEPTH, D_MODEL, D_MODEL), D_MODEL),
        "norm2_w": gain(ks[8], (DEPTH, D_MODEL)),
        "w_ffn_gate": w(ks[9], (DEPTH, D_MODEL, FFN_HIDDEN), D_MODEL),
        "w_ffn_up": w(ks[10], (DEPTH, D_MODEL, FFN_HIDDEN), D_MODEL),
        "w_ffn_down": w(ks[11], (DEPTH, FFN_HIDDEN, D_MODEL), FFN_HIDDEN),
    }

def first_block(x, norm1_w, w_in, q_norm_w, k_norm_w, w_ret_out, w_moba_out, w_o,
              norm2_w, w_ffn_gate, w_ffn_up, w_ffn_down):
    B, S, _ = x.shape
    pos = jnp.arange(S)
    split_points = [int(v) for v in np.cumsum(IN_SPLITS)[:-1]]
    for l in range(DEPTH):
        h = rmsnorm(x, norm1_w[l])
        proj = h @ w_in[l]
        rq, rk, rv, rg, mq, mk, mv, ga, gb = jnp.split(proj, split_points, axis=-1)

        rq = rotary(rq.reshape(B, S, RET_HEADS, RET_DK), pos)
        rk = rotary(rk.reshape(B, S, RET_HEADS, RET_DK), pos) * (RET_DK ** -0.5)
        rv = rv.reshape(B, S, RET_HEADS, RET_DV)
        ret = jax.nn.silu(rg) * retention(rq, rk, rv)
        a = ret @ w_ret_out[l]

        mq = rmsnorm(mq.reshape(B, S, MOBA_HEADS, MOBA_DH), q_norm_w[l])
        mk = rmsnorm(mk.reshape(B, S, MOBA_HEADS, MOBA_DH), k_norm_w[l])
        mv = mv.reshape(B, S, MOBA_HEADS, MOBA_DH)
        b = moba_attention(mq, mk, mv) @ w_moba_out[l]

        mix = jax.nn.sigmoid(ga) * a + jax.nn.sigmoid(gb) * b
        x = x + mix @ w_o[l]

        h2 = rmsnorm(x, norm2_w[l])
        f = (jax.nn.silu(h2 @ w_ffn_gate[l]) * (h2 @ w_ffn_up[l])) @ w_ffn_down[l]
        x = x + f
    return x


DEPTH_2 = 2

N_A = DEPTH_2 // 2
N_B = DEPTH_2 - N_A
PLE_DIM = 256
FOX_HEADS = 16
FOX_HEAD_DIM = D_MODEL // FOX_HEADS
FOX_IN = 3 * D_MODEL + FOX_HEADS
FOX_GATE_BIAS = 3.0
MLA_HEADS = 16
QK_NOPE_DIM = 128
QK_ROPE_DIM = 64
V_HEAD_DIM = 128
Q_LORA_RANK = 384
KV_LORA_RANK = 256
ROPE_THETA = 10000.0
D_FF = 2816
BLOCK_Q = 128
LN_EPS = 1e-5
ALPHA = (2 * DEPTH_2) ** 0.25
BETA = (8 * DEPTH_2) ** -0.25


def layer_norm(x, g, b):
    xf = x.astype(jnp.float32)
    mu = jnp.mean(xf, axis=-1, keepdims=True)
    xc = xf - mu
    var = jnp.mean(xc * xc, axis=-1, keepdims=True)
    y = xc * lax.rsqrt(var + LN_EPS) * g.astype(jnp.float32) + b.astype(jnp.float32)
    return y.astype(x.dtype)

def rms_norm(x, g):
    xf = x.astype(jnp.float32)
    y = xf * lax.rsqrt(jnp.mean(xf * xf, axis=-1, keepdims=True) + RMS_EPS) * g.astype(jnp.float32)
    return y.astype(x.dtype)

def post_norm(x, delta, g, b):
    return layer_norm(ALPHA * x + delta, g, b)

def swiglu(x, w_in, w_out):
    h = x @ w_in
    gate, up = h[..., :D_FF], h[..., D_FF:]
    return (jax.nn.silu(gate) * up) @ w_out

def rope_tables(seq_len):
    half = QK_ROPE_DIM // 2
    inv = ROPE_THETA ** (-jnp.arange(half, dtype=jnp.float32) * (2.0 / QK_ROPE_DIM))
    ang = jnp.arange(seq_len, dtype=jnp.float32)[:, None] * inv[None, :]
    return jnp.cos(ang), jnp.sin(ang)

def rope(x, cos, sin):
    half = x.shape[-1] // 2
    xf = x.astype(jnp.float32)
    x1, x2 = xf[..., :half], xf[..., half:]
    return jnp.concatenate([x1 * cos - x2 * sin, x2 * cos + x1 * sin], axis=-1).astype(x.dtype)

def causal_block_attention(score_fn, v):
    B, S, H, Dv = v.shape
    n_blocks = S // BLOCK_Q
    k_pos = jnp.arange(S)

    def one_block(blk):
        start = blk * BLOCK_Q
        s = score_fn(start)
        q_pos = start + jnp.arange(BLOCK_Q)
        s = jnp.where(k_pos[None, :] <= q_pos[:, None], s, -jnp.inf)
        w = jax.nn.softmax(s, axis=-1).astype(v.dtype)
        return jnp.einsum('bhqk,bkhd->bqhd', w, v)

    o = lax.map(one_block, jnp.arange(n_blocks))
    return jnp.moveaxis(o, 0, 1).reshape(B, S, H, Dv)

def fox_mixer(x, w_in, b_f, w_o):
    B, S, _ = x.shape
    h = x @ w_in
    q = h[..., :D_MODEL].reshape(B, S, FOX_HEADS, FOX_HEAD_DIM)
    k = h[..., D_MODEL:2 * D_MODEL].reshape(B, S, FOX_HEADS, FOX_HEAD_DIM)
    v = h[..., 2 * D_MODEL:3 * D_MODEL].reshape(B, S, FOX_HEADS, FOX_HEAD_DIM)
    f_logit = h[..., 3 * D_MODEL:].astype(jnp.float32) + b_f.astype(jnp.float32)
    cum = jnp.cumsum(jax.nn.log_sigmoid(f_logit), axis=1).transpose(0, 2, 1)
    scale = FOX_HEAD_DIM ** -0.5

    def scores(start):
        qb = lax.dynamic_slice_in_dim(q, start, BLOCK_Q, axis=1)
        cb = lax.dynamic_slice_in_dim(cum, start, BLOCK_Q, axis=2)
        s = jnp.einsum('bqhd,bkhd->bhqk', qb, k).astype(jnp.float32) * scale
        return s + cb[:, :, :, None] - cum[:, :, None, :]

    o = causal_block_attention(scores, v)
    return o.reshape(B, S, D_MODEL) @ w_o

def shared_kv(x, w_down, kv_norm, w_up, cos, sin):
    B, S, _ = x.shape
    h = x @ w_down
    c_kv = rms_norm(h[..., :KV_LORA_RANK], kv_norm)
    k_rope = rope(h[..., KV_LORA_RANK:], cos, sin)
    kv = jnp.einsum('bsc,chd->bshd', c_kv, w_up)
    return kv[..., :QK_NOPE_DIM], k_rope, kv[..., QK_NOPE_DIM:]

def mla_mixer(x, w_dq, q_norm, w_uq, w_o, k_nope, k_rope, v, cos, sin):
    B, S, _ = x.shape
    c_q = rms_norm(x @ w_dq, q_norm)
    q = jnp.einsum('bsc,chd->bshd', c_q, w_uq)
    q_nope = q[..., :QK_NOPE_DIM]
    q_rope = rope(q[..., QK_NOPE_DIM:], cos[:, None, :], sin[:, None, :])
    scale = (QK_NOPE_DIM + QK_ROPE_DIM) ** -0.5

    def scores(start):
        qn = lax.dynamic_slice_in_dim(q_nope, start, BLOCK_Q, axis=1)
        qr = lax.dynamic_slice_in_dim(q_rope, start, BLOCK_Q, axis=1)
        s = jnp.einsum('bqhd,bkhd->bhqk', qn, k_nope) + jnp.einsum('bqhr,bkr->bhqk', qr, k_rope)
        return s.astype(jnp.float32) * scale

    o = causal_block_attention(scores, v)
    return o.reshape(B, S, MLA_HEADS * V_HEAD_DIM) @ w_o

def second_inputs(seed: int = 0) -> dict:
    key = jax.random.key(seed)
    ks = iter(jax.random.split(key, 32))
    f32 = jnp.float32

    def nrm(shape, fan_in, scale=1.0):
        return jax.random.normal(next(ks), shape, f32) * (scale * fan_in ** -0.5)

    def gain(shape):
        return 1.0 + 0.02 * jax.random.normal(next(ks), shape, f32)

    def small(shape, s=0.02):
        return s * jax.random.normal(next(ks), shape, f32)

    x = jax.random.normal(next(ks), (BATCH, SEQ, D_MODEL), f32)
    p = jax.random.normal(next(ks), (DEPTH_2, BATCH, SEQ, PLE_DIM), f32)
    ffn1_w_in = nrm((DEPTH_2, D_MODEL, 2 * D_FF), D_MODEL)
    ffn1_w_out = nrm((DEPTH_2, D_FF, D_MODEL), D_FF, BETA)
    ffn2_w_in = nrm((DEPTH_2, D_MODEL, 2 * D_FF), D_MODEL)
    ffn2_w_out = nrm((DEPTH_2, D_FF, D_MODEL), D_FF, BETA)
    ln_g = gain((DEPTH_2, 4, D_MODEL))
    ln_b = small((DEPTH_2, 4, D_MODEL))
    ple_w_gate = nrm((DEPTH_2, D_MODEL, D_MODEL), D_MODEL)
    ple_b_gate = small((DEPTH_2, D_MODEL))
    ple_w_proj = nrm((DEPTH_2, PLE_DIM, D_MODEL), PLE_DIM, BETA)
    fox_w_in = nrm((N_A, D_MODEL, FOX_IN), D_MODEL)
    fox_w_in = fox_w_in.at[:, :, 2 * D_MODEL:3 * D_MODEL].multiply(BETA)
    fox_b_f = FOX_GATE_BIAS + 0.5 * jax.random.normal(next(ks), (N_A, FOX_HEADS), f32)
    fox_w_o = nrm((N_A, D_MODEL, D_MODEL), D_MODEL, BETA)
    mla_w_dq = nrm((N_B, D_MODEL, Q_LORA_RANK), D_MODEL)
    mla_q_norm = gain((N_B, Q_LORA_RANK))
    mla_w_uq = nrm((N_B, Q_LORA_RANK, MLA_HEADS, QK_NOPE_DIM + QK_ROPE_DIM), Q_LORA_RANK)
    mla_w_o = nrm((N_B, MLA_HEADS * V_HEAD_DIM, D_MODEL), MLA_HEADS * V_HEAD_DIM, BETA)
    kv_w_down = nrm((D_MODEL, KV_LORA_RANK + QK_ROPE_DIM), D_MODEL)
    kv_norm = gain((KV_LORA_RANK,))
    kv_w_up = nrm((KV_LORA_RANK, MLA_HEADS, QK_NOPE_DIM + V_HEAD_DIM), KV_LORA_RANK)
    kv_w_up = kv_w_up.at[:, :, QK_NOPE_DIM:].multiply(BETA)
    return {'x': x, 'p': p,
            'ffn1_w_in': ffn1_w_in, 'ffn1_w_out': ffn1_w_out,
            'ffn2_w_in': ffn2_w_in, 'ffn2_w_out': ffn2_w_out,
            'ln_g': ln_g, 'ln_b': ln_b,
            'ple_w_gate': ple_w_gate, 'ple_b_gate': ple_b_gate, 'ple_w_proj': ple_w_proj,
            'fox_w_in': fox_w_in, 'fox_b_f': fox_b_f, 'fox_w_o': fox_w_o,
            'mla_w_dq': mla_w_dq, 'mla_q_norm': mla_q_norm, 'mla_w_uq': mla_w_uq, 'mla_w_o': mla_w_o,
            'kv_w_down': kv_w_down, 'kv_norm': kv_norm, 'kv_w_up': kv_w_up}

def second_block(x, p, ffn1_w_in, ffn1_w_out, ffn2_w_in, ffn2_w_out, ln_g, ln_b,
              ple_w_gate, ple_b_gate, ple_w_proj, fox_w_in, fox_b_f, fox_w_o,
              mla_w_dq, mla_q_norm, mla_w_uq, mla_w_o, kv_w_down, kv_norm, kv_w_up):
    S = x.shape[1]
    cos, sin = rope_tables(S)
    k_nope = k_rope = v_shared = None
    for i in range(DEPTH_2):
        if i == N_A:
            k_nope, k_rope, v_shared = shared_kv(x, kv_w_down, kv_norm, kv_w_up, cos, sin)
        x = post_norm(x, 0.5 * swiglu(x, ffn1_w_in[i], ffn1_w_out[i]), ln_g[i, 0], ln_b[i, 0])
        if i < N_A:
            mix = fox_mixer(x, fox_w_in[i], fox_b_f[i], fox_w_o[i])
        else:
            j = i - N_A
            mix = mla_mixer(x, mla_w_dq[j], mla_q_norm[j], mla_w_uq[j], mla_w_o[j],
                            k_nope, k_rope, v_shared, cos, sin)
        x = post_norm(x, mix, ln_g[i, 1], ln_b[i, 1])
        x = post_norm(x, 0.5 * swiglu(x, ffn2_w_in[i], ffn2_w_out[i]), ln_g[i, 2], ln_b[i, 2])
        gate = jax.nn.sigmoid((x @ ple_w_gate[i] + ple_b_gate[i]).astype(jnp.float32)).astype(x.dtype)
        x = post_norm(x, gate * (p[i] @ ple_w_proj[i]), ln_g[i, 3], ln_b[i, 3])
    return x


def setup_inputs(seed=0):
    out = dict(first_inputs(seed))
    for name, value in second_inputs(seed + 1).items():
        if name != "x":
            out[name + "_2"] = value
    return out


def reference(
    x, norm1_w, w_in, q_norm_w, k_norm_w, w_ret_out, w_moba_out, w_o, norm2_w, w_ffn_gate,
    w_ffn_up, w_ffn_down, p_2, ffn1_w_in_2, ffn1_w_out_2, ffn2_w_in_2, ffn2_w_out_2, ln_g_2,
    ln_b_2, ple_w_gate_2, ple_b_gate_2, ple_w_proj_2, fox_w_in_2, fox_b_f_2, fox_w_o_2,
    mla_w_dq_2, mla_q_norm_2, mla_w_uq_2, mla_w_o_2, kv_w_down_2, kv_norm_2, kv_w_up_2,
):
    x = first_block(
        x, norm1_w, w_in, q_norm_w, k_norm_w, w_ret_out, w_moba_out, w_o, norm2_w, w_ffn_gate,
        w_ffn_up, w_ffn_down,
    )
    return second_block(
        x, p_2, ffn1_w_in_2, ffn1_w_out_2, ffn2_w_in_2, ffn2_w_out_2, ln_g_2, ln_b_2,
        ple_w_gate_2, ple_b_gate_2, ple_w_proj_2, fox_w_in_2, fox_b_f_2, fox_w_o_2, mla_w_dq_2,
        mla_q_norm_2, mla_w_uq_2, mla_w_o_2, kv_w_down_2, kv_norm_2, kv_w_up_2,
    )


_drawn_inputs = setup_inputs


def setup_inputs(seed=0):
    import zlib

    import numpy as np

    out = dict(_drawn_inputs(seed))
    spreads = {}
    factors = {'norm1_w': 3.536,
     'q_norm_w': 8.0,
     'k_norm_w': 8.0,
     'norm2_w': 4.273,
     'ple_b_gate_2': 8.0,
     'fox_b_f_2': 44.36,
     'mla_q_norm_2': 8.0,
     'kv_norm_2': 8.0}
    for name, (base, spread) in spreads.items():
        noise = np.random.default_rng([zlib.crc32(name.encode()), seed]).standard_normal(out[name].shape)
        drawn = base * np.exp(spread * noise) if base else spread * noise
        out[name] = __import__('jax').numpy.asarray(drawn.astype(out[name].dtype))
    for name, factor in factors.items():
        out[name] = (out[name] * factor).astype(out[name].dtype)
    return out
```

```python
from contextlib import ExitStack
import math

import numpy as np
import concourse.bass as bass
from concourse import mybir

P = 128
T = 2
S = T * P
D = 1024
KD = D // P
CH = 512
RING = 3
UNIT = 2048
F_HID = 2816
HB = 256
FI = F_HID // HB
RET_H, RET_DK, RET_DV = 4, 128, 256
MOBA_H, MOBA_DH = 8, 64
FOX_H, FOX_DH = 16, 64
MLA_H, NOPE, ROPE_D, VD = 16, 128, 64, 128
QL, KVL = 384, 256
PLE = 256
RMS_EPS, LN_EPS, GN_EPS = 1e-6, 1e-5, 1e-5
ALPHA = float((2 * 2) ** 0.25)
NEG = -1e30

F32 = mybir.dt.float32
F32R = mybir.dt.float32r
I32 = mybir.dt.int32
ALU = mybir.AluOpType
ACT = mybir.ActivationFunctionType
AX_X = mybir.AxisListType.X


def shape_constants():
    c = {}
    c["ident"] = np.eye(P, dtype=np.float32)
    i = np.arange(P)
    causal = np.where(i[None, :] <= i[:, None], 0.0, NEG)
    c["mask"] = np.concatenate([causal, np.zeros((P, P)), causal], 1)
    lg = np.log1p(-np.exp2(-5.0 - np.arange(RET_H)))
    dec = np.zeros((P, RET_H, 3, P))
    for h in range(RET_H):
        diff = i[None, :] - i[:, None]
        own = np.where(diff >= 0, np.exp(np.maximum(diff, 0) * lg[h]), 0.0)
        dec[:, h, 0] = own
        dec[:, h, 1] = np.exp((diff + P) * lg[h])
        dec[:, h, 2] = own
    c["decay"] = (dec * RET_DK ** -0.5).reshape(P, RET_H * 3 * P)
    pos = np.arange(S).reshape(T, P).T

    def rope(half, base):
        inv = (base ** (-np.arange(half, dtype=np.float32) / np.float32(half))).astype(np.float32)
        ang = (pos[:, :, None].astype(np.float32) * inv).astype(np.float32)
        return np.cos(ang.astype(np.float64)), np.sin(ang.astype(np.float64))

    for name, half in (("rope_ret", RET_DK // 2), ("rope_mla", ROPE_D // 2)):
        cos, sin = rope(half, np.float32(10000.0))
        c[name] = np.concatenate([cos, cos, -sin, sin], 2).reshape(P, T * 4 * half)
    c["upper"] = (i[:, None] <= i[None, :]).astype(np.float32)
    sel = np.zeros((FOX_H, FOX_H, P))
    sel[np.arange(FOX_H), np.arange(FOX_H), :] = -math.sqrt(FOX_DH)
    c["sel"] = sel.reshape(FOX_H, FOX_H * P)
    return {n: np.ascontiguousarray(a, dtype=np.float32) for n, a in c.items()}


def weight_units(w):
    units, at = [], {}

    def add(stage, kt, n, halves):
        at.setdefault(stage, []).append(len(units))
        units.append((stage, kt, n, halves))

    def dense(stage, m, k0, kts, c0, n):
        rows = m[k0 * P:(k0 + kts) * P, c0:c0 + n].rearrange("(k p) n -> p k n", p=P)
        a = (kts + 1) // 2
        if kts == 1:
            b = n // 2
            add(stage, kts, n, [((0, 1), (0, b), rows[:, :, 0:b]), ((0, 1), (b, n), rows[:, :, b:n])])
        else:
            add(stage, kts, n, [((0, a), (0, n), rows[:, 0:a, :]), ((a, kts), (0, n), rows[:, a:kts, :])])

    def chunks(stage, m, k, c0, count, n=CH, per=4):
        for c in range(count):
            for k0 in range(0, k, per):
                dense(f"{stage}{c}", m, k0, min(per, k - k0), c0 + c * n, n)

    def ffn(f):
        for _ in range(3 * FI):
            add(f"ffn{f}", 0, 0, None)

    w_in = w["w_in"]
    for name, c0, count in (("rq", 0, 1), ("rk", 512, 1), ("rv", 1024, 2), ("mq", 3072, 1), ("mk", 3584, 1),
                            ("mv", 4096, 1), ("rg", 2048, 2)):
        chunks(name, w_in, KD, c0, count)
    chunks("ret_out", w["w_ret_out"], KD, 0, 2)
    chunks("ga", w_in, KD, 4608, 2)
    chunks("moba_out", w["w_moba_out"], 4, 0, 2)
    chunks("gb", w_in, KD, 5632, 2)
    chunks("w_o", w["w_o"], KD, 0, 2)
    ffn(0)
    ffn(1)
    dense("fox_f", w["fox_w_in"], 0, KD, 3 * D, FOX_H)
    chunks("fox_in", w["fox_w_in"], KD, 0, 6)
    chunks("fox_o", w["fox_w_o"], KD, 0, 2)
    ffn(2)
    dense("ple_p0", w["ple_w_proj"][0], 0, 2, 0, D)
    chunks("ple_g0", w["ple_w_gate"][0], KD, 0, 2)
    chunks("kv_down", w["kv_w_down"], KD, 0, 1, n=KVL + ROPE_D)
    for c in range(4):
        dense("kv_up", w["kv_w_up"], 0, 2, c * D, D)
    ffn(3)
    chunks("dq", w["mla_w_dq"], KD, 0, 1, n=QL)
    for g in range(MLA_H // 2):
        dense("uq", w["mla_w_uq"], 0, 3, g * 384, 384)
    chunks("mla_o", w["mla_w_o"], MLA_H, 0, 2)
    ffn(4)
    dense("ple_p1", w["ple_w_proj"][1], 0, 2, 0, D)
    chunks("ple_g1", w["ple_w_gate"][1], KD, 0, 2)
    return units, at


def build(nc, dram, marks):
    found = {}
    units, unit_at = weight_units(dram)
    N_UNITS = len(units)
    ffn_w = [(dram["w_ffn_gate"], dram["w_ffn_up"], dram["w_ffn_down"])]
    for l in range(2):
        for n in (1, 2):
            m = dram[f"ffn{n}_w_in"][l]
            ffn_w.append((m[:, 0:F_HID], m[:, F_HID:2 * F_HID], dram[f"ffn{n}_w_out"][l]))

    with ExitStack() as ctx:
        def sb(name, cols, dt=F32):
            return ctx.enter_context(nc.sbuf_tensor(name, [P, cols], dt))

        sems = {}

        def sem(name):
            sems[name] = ctx.enter_context(nc.semaphore(name))
            return sems[name]

        w_raw = [sb(f"w_raw{s}", UNIT) for s in range(RING)]
        w_hi = [sb(f"w_hi{s}", UNIT, F32R) for s in range(RING)]
        w_lo = [sb(f"w_lo{s}", UNIT, F32R) for s in range(RING)]
        x = sb("x", T * D)[:, :].rearrange("p (t n) -> p t n", t=T)
        xTh = sb("xTh", 16 * S, F32R)[:, :].rearrange("p (k n) -> p k n", k=16)
        xTl = sb("xTl", 16 * S, F32R)[:, :].rearrange("p (k n) -> p k n", k=16)
        cTh = sb("cTh", 3 * S, F32R)[:, :].rearrange("p (k n) -> p k n", k=3)
        cTl = sb("cTl", 3 * S, F32R)[:, :].rearrange("p (k n) -> p k n", k=3)
        hTh = sb("hTh", 2 * S, F32R)[:, :].rearrange("p (k n) -> p k n", k=2)
        hTl = sb("hTl", 2 * S, F32R)[:, :].rearrange("p (k n) -> p k n", k=2)
        hid = sb("hid", T * HB)[:, :].rearrange("p (t n) -> p t n", t=T)
        tanh = sb("tanh", T * CH)[:, :].rearrange("p (t n) -> p t n", t=T)
        gb = sb("gb", 2 * D)[:, :].rearrange("p (a n) -> p a n", a=2)
        pin = sb("pin", T * PLE)[:, :].rearrange("p (t n) -> p t n", t=T)
        ident = sb("ident", P)[:, :]
        mask = sb("mask", 3 * P)[:, :]
        decay = sb("decay", RET_H * 3 * P)[:, :].rearrange("p (h n) -> p h n", h=RET_H)
        rope_ret = sb("rope_ret", T * 256)[:, :].rearrange("p (t n) -> p t n", t=T)
        rope_mla = sb("rope_mla", T * 128)[:, :].rearrange("p (t n) -> p t n", t=T)
        upper = sb("upper", P)[:, :]
        ones = sb("ones", P)[:, :]
        head_w = sb("head_w", 2 * MOBA_DH)[:, :].rearrange("p (a n) -> p a n", a=2)
        fox_b = sb("fox_b", FOX_H)[:, :]
        stats = sb("stats", 64)[:, :]
        mv_ = sb("mean_var", 2 * 16)[:, :].rearrange("p (a n) -> p a n", n=2)
        rs_v, rs_y, rs_a, rs_b = (sb(f"rsqrt_{n}", 32)[:, :] for n in "vyab")
        negmax = sb("negmax", 8)[:, :]
        psum_e = sb("exp_sum", 8)[:, :]
        rsum = sb("exp_rsum", 4)[:, :]

        ARENA = 14336
        arena = sb("arena", ARENA)[:, :]

        class Carve:
            def __init__(self):
                self.at = 0

            def __call__(self, cols):
                self.at += cols
                assert self.at <= ARENA, self.at
                return arena[:, self.at - cols:self.at]

            def tiles(self, a, n):
                return self(a * n).rearrange("p (a n) -> p a n", a=a)

        common = Carve()
        sm = common.tiles(2, 384)
        pr = common.tiles(2, 384)
        pT = common.tiles(2, 384)
        shared_end = common.at

        def carve():
            c = Carve()
            c.at = shared_end
            return c

        c1 = carve()
        rqk = c1.tiles(4, 512)
        rqT = c1.tiles(4, S)
        rkT = c1.tiles(4, S)
        rv = c1.tiles(T, D)
        mqk = c1.tiles(4, 512)
        mqT = c1.tiles(4, S)
        mkT = c1.tiles(4, S)
        mv = c1.tiles(T, 512)
        mo = mqk.rearrange("p (b t) n -> p b t n", b=2)[:, 0]
        rtmp = arena[:, 0:512]
        c1b = carve()
        ro = c1b.tiles(T, D)
        ra = c1b.tiles(T, D)
        mix = c1b.tiles(T, D)
        cf = carve()
        fqk = cf.tiles(T, 512)
        fqT = cf.tiles(8, S)
        fkT = cf.tiles(8, S)
        fv = cf.tiles(T, D)
        fsel = cf(FOX_H * P).rearrange("p (h n) -> p h n", h=FOX_H)
        cumT = cf(S)
        fg = cf.tiles(6, 32)
        cb = cf.tiles(T, FOX_H)
        fo = cf.tiles(T, D)
        cm = carve()
        kT = cm.tiles(MLA_H, S)
        vv = cm.tiles(T, MLA_H * VD)
        krT = cm(S)
        norm_c = cm(QL)
        cq = cm.tiles(T, QL)
        kr = cm.tiles(T, 2 * ROPE_D)
        qs = cm.tiles(T, 384)
        qT = cm.tiles(3, S)
        mlo = cm.tiles(T, 2 * VD)
        cp = carve()
        pp = cp.tiles(T, D)
        pz = cp.tiles(T, CH)
        pb = cp(D)

        bank = [ctx.enter_context(nc.psum_tensor(f"bank{b}", [P, CH], F32))[:, :] for b in range(4)]
        acc_t = ctx.enter_context(nc.psum_tensor("acc", [P, T, D], F32))
        acc = acc_t[:, :, :]
        bank += [acc[:, b // 2, (b % 2) * CH:(b % 2 + 1) * CH] for b in range(4)]

        w_loaded = [sem(f"w_loaded{s}") for s in range(RING)]
        w_hi_done, w_lo_done, w_used = sem("w_hi_done"), sem("w_lo_done"), sem("w_used")
        pe_done, act_done, dve_done = sem("pe_done"), sem("act_done"), sem("dve_done")
        const_loaded, gb_loaded, out_stored = sem("const_loaded"), sem("gb_loaded"), sem("out_stored")
        p_loaded, aux_loaded, ones_set = sem("p_loaded"), sem("aux_loaded"), sem("ones_set")
        gu0_full = sem("gu0_full")
        tanh_done = sem("tanh_done")
        hid_part, hid_done = sem("hid_part"), sem("hid_done")
        hT_full = sem("hT_full")
        hT_hi, hT_lo = sem("hT_hi"), sem("hT_lo")
        acc_full = sem("acc_full")

        counts = {"pe_done": 0, "act_done": 0, "dve_done": 0}
        seen = {}

        def mark(name, *label):
            counts[name] += 1
            if label:
                assert label not in found, label
                found[label] = (name, counts[name])
            return 1

        def note(label, name, value):
            assert label not in found, label
            found[label] = (name, value)

        def need(eng, *label):
            if not marks:
                return
            name, value = marks[label]
            if seen.get((eng, name), 0) < value:
                seen[(eng, name)] = value
                ENG[eng].wait_ge(sems[name], value)

        ENG = {}
        block = ctx.enter_context(nc.Block())

        def bcast_rows(src, n):
            return src.rearrange("(a n) -> a n", a=1).broadcast_to([P, n])

        @block.sync
        def _(sp):
            def store_x(t):
                sp.dma_start(dram["out"][t * P:(t + 1) * P, :], x[:, t, :]).then_inc(out_stored, 16)

            ENG["sp"] = sp

            def load(u):
                _, kt, n, halves = units[u]
                slot = w_raw[u % RING][:, 0:kt * n].rearrange("p (k n) -> p k n", k=kt)
                if u >= RING:
                    sp.wait_ge(w_lo_done, u - RING + 1)
                for (k0, k1), (n0, n1), src in halves:
                    sp.dma_start(slot[:, k0:k1, n0:n1], src).then_inc(w_loaded[u % RING], 16)

            def load_ffn(f):
                u0 = unit_at[f"ffn{f}"][0]
                gate, up, down = ffn_w[f]

                def gate_up(u_slot, need_lo, half, i):
                    if need_lo is not None:
                        sp.wait_ge(w_lo_done, need_lo)
                    slot = w_raw[u_slot][:, :].rearrange("p (k g n) -> p g k n", k=4, g=2)
                    for g, m in enumerate((gate, up)):
                        src = m[half * 512:(half + 1) * 512, :].rearrange("(k p) n -> p k n", p=P)
                        sp.dma_start(slot[:, g], src[:, :, bass.ds(i * HB, HB)]).then_inc(w_loaded[u_slot], 16)

                def down_rows(u_slot, need_lo, i):
                    sp.wait_ge(w_lo_done, need_lo)
                    slot = w_raw[u_slot][:, :].rearrange("p (k n) -> p k n", k=2)
                    for k in range(2):
                        sp.dma_start(slot[:, k], down[bass.ds(i * HB + k * P, P), :]).then_inc(w_loaded[u_slot], 16)

                gate_up(u0 % RING, u0 - 2 if u0 > 2 else None, 0, 0)
                gate_up((u0 + 1) % RING, u0 - 1, 1, 0)
                with sp.Fori(1, FI) as i:
                    gate_up((u0 + 2) % RING, i * 3 + (u0 - 3), 0, i)
                    gate_up(u0 % RING, i * 3 + (u0 - 2), 1, i)
                    down_rows((u0 + 1) % RING, i * 3 + (u0 - 1), i - 1)
                u = u0 + 3 * FI - 1
                down_rows(u % RING, u - 2, FI - 1)

            u = 0
            while u < N_UNITS:
                if units[u][3] is None:
                    load_ffn(int(units[u][0][3:]))
                    u += 3 * FI
                else:
                    load(u)
                    u += 1
            for t in range(T):
                need("sp", "norm", 9, t)
                store_x(t)
            sp.wait_ge(out_stored, 16 * T)

        norm_src = [(dram["norm1_w"], None), (dram["norm2_w"], None)] + \
                   [(dram["ln_g"][l, j], dram["ln_b"][l, j]) for l in range(2) for j in range(4)]

        @block.gpsimd
        def _(pool):
            ENG["pool"] = pool
            pool.memset(ones, 1.0).then_inc(ones_set, 1)

            def load_p(l):
                pool.dma_start(pin, dram["p"][l].rearrange("(t p) n -> p t n", p=P)).then_inc(p_loaded, 16)

            for site, (g, b) in enumerate(norm_src):
                if site:
                    need("pool", "norm", site - 1, 1)
                pool.dma_start(gb[:, 0, :], bcast_rows(g, D)).then_inc(gb_loaded, 16)
                pool.dma_start(gb[:, 1, :], bcast_rows(b if b is not None else g, D)).then_inc(gb_loaded, 16)
                if site == 0:
                    load_p(0)
                if site == 2:
                    pool.dma_start(fsel[0:FOX_H], dram["sel"].rearrange("p (h n) -> p h n", h=FOX_H))\
                        .then_inc(aux_loaded, 16)
                if site == 5:
                    pool.dma_start(pb, bcast_rows(dram["ple_b"][0], D)).then_inc(aux_loaded, 16)
                    need("pool", "pT", 0)
                    load_p(1)
                if site == 6:
                    pool.dma_start(norm_c[:, 0:KVL], bcast_rows(dram["kv_norm"], KVL)).then_inc(aux_loaded, 16)
                    need("pool", "ckv", 1)
                    pool.dma_start(norm_c, bcast_rows(dram["q_norm"], QL)).then_inc(aux_loaded, 16)
                if site == 9:
                    pool.dma_start(pb, bcast_rows(dram["ple_b"][1], D)).then_inc(aux_loaded, 16)

        CONSTS = [("ident", ident), ("x", x), ("head_q", head_w[:, 0]), ("head_k", head_w[:, 1]),
                  ("rope_ret", rope_ret), ("mask", mask), ("decay", decay), ("rope_mla", rope_mla),
                  ("upper", upper), ("fox_b", fox_b)]
        const_src = {n: dram[n] for n in ("ident", "mask", "upper")}
        const_src["x"] = dram["x"].rearrange("(t p) n -> p t n", p=P)
        const_src["decay"] = dram["decay"].rearrange("p (h n) -> p h n", h=RET_H)
        for n in ("rope_ret", "rope_mla"):
            const_src[n] = dram[n].rearrange("p (t n) -> p t n", t=T)
        const_src["head_q"] = bcast_rows(dram["q_norm_w"], MOBA_DH)
        const_src["head_k"] = bcast_rows(dram["k_norm_w"], MOBA_DH)
        const_src["fox_b"] = bcast_rows(dram["fox_b_f"], FOX_H)
        N_CONST = 16 * len(CONSTS)

        def site_ready(site, t):
            return {"ret": ("gated", 1, t), "moba": ("o", "moba", MOBA_H - 1), "mix": ("mix", 1, t),
                    "fox": ("o", "fox", FOX_H - 1), "raw": ("ffn_out", 0, t)}.get(site, ("norm", site, t))

        @block.tensor
        def _(pe):
            ENG["pe"] = pe
            freed = {b: None for b in range(8)}

            def take(b, label):
                if freed[b]:
                    need("pe", *freed[b])
                freed[b] = label

            def transposes(b, free, label, pairs):
                take(b, free)
                for c, src in pairs:
                    mm = pe.matmul(bank[b][:, c:c + P], src, ident, is_transpose=True, start=True, stop=True)
                mm.then_inc(pe_done, mark("pe_done", *label))

            def mm3(out, ah, al, bh, bl, first, last):
                pe.matmul(out, ah, bh, start=first, stop=False)
                pe.matmul(out, ah, bl, start=False, stop=False)
                return pe.matmul(out, al, bh, start=False, stop=last)

            def chunk(stage, banks, free, src=None, slot0=0, part=None):
                ah, al = src or (xTh, xTl)
                us = unit_at[stage] if part is None else [unit_at[stage][part[0]]]
                name = (stage,) if part is None else (stage, part[0] * 2 + (part[1] > 0))
                total = sum(units[u][1] for u in us)
                for t in range(T):
                    take(banks[t], (free, *name, t))
                k = 0
                for u in us:
                    _, kt, n, _ = units[u]
                    c0, cn, ends = (0, n, True) if part is None else part[1:]
                    pe.wait_ge(w_lo_done, u + 1)
                    wh, wl = (w[u % RING][:, 0:kt * n].rearrange("p (k n) -> p k n", k=kt) for w in (w_hi, w_lo))
                    for j in range(kt):
                        for t in range(T):
                            a, tok = slot0 + k, slice(t * P, (t + 1) * P)
                            mm = mm3(bank[banks[t]][:, 0:cn], ah[:, a, tok], al[:, a, tok],
                                     wh[:, j, c0:c0 + cn], wl[:, j, c0:c0 + cn], k == 0, k == total - 1)
                            if t == 0 and k == total - 1:
                                mm.then_inc(pe_done, mark("pe_done", "full", *name, 0))
                        k += 1
                    if ends:
                        mm.then_inc(w_used, 1)
                        if k == total:
                            note(("full", *name, 1), "w_used", u + 1)
                    else:
                        mm.then_inc(pe_done, mark("pe_done", "full", *name, 1))

            def to_xT(site, src, count, b0=0):
                for t in range(T):
                    for q in range(count // 4):
                        need("pe", *site_ready(site, t))
                        transposes((b0 + t * (count // 4) + q) % 4, ("xT", site, t, q), ("T", site, t, q),
                                   [(j * P, src[:, t, (4 * q + j) * P:(4 * q + j + 1) * P]) for j in range(4)])

            def need_xT(site, count=KD):
                for t in range(T):
                    for q in range(count // 4):
                        need("pe", "xT", site, t, q)

            def ffn(f):
                u0 = unit_at[f"ffn{f}"][0]
                g0 = f * FI
                assert 3 * FI == len(unit_at[f"ffn{f}"])

                def gate_up(slot, u1, half, first, last):
                    pe.wait_ge(w_lo_done, u1)
                    wh, wl = (w[slot][:, :].rearrange("p (k n) -> p k n", k=4) for w in (w_hi, w_lo))
                    for j in range(4):
                        k = half * 4 + j
                        for t in range(T):
                            tok = slice(t * P, (t + 1) * P)
                            mm = mm3(bank[t], xTh[:, k, tok], xTl[:, k, tok], wh[:, j], wl[:, j], k == 0, k == 7)
                            if k == 7 and t == 0:
                                mm.then_inc(gu0_full, 1)
                    mm.then_inc(w_used, 1)

                def transpose_hid(i):
                    pe.wait_ge(hid_done, (i + (g0 + 1)) * T)
                    for k in range(2):
                        for t in range(T):
                            mm = pe.matmul(bank[2 + k][:, t * P:(t + 1) * P], hid[:, t, k * P:(k + 1) * P],
                                           ident, is_transpose=True, start=True, stop=True)
                        mm.then_inc(hT_full, 1)

                def down(slot, u1, i, first, last):
                    pe.wait_ge(w_lo_done, u1)
                    pe.wait_ge(hT_lo, (i + (g0 + 1)) * 2)
                    wh, wl = (w[slot][:, :].rearrange("p (k n) -> p k n", k=2) for w in (w_hi, w_lo))
                    for k in range(2):
                        for t in range(T):
                            tok = slice(t * P, (t + 1) * P)
                            for n in range(2):
                                cols = slice(n * CH, (n + 1) * CH)
                                mm = mm3(acc[:, t, cols], hTh[:, k, tok], hTl[:, k, tok], wh[:, k, cols],
                                         wl[:, k, cols], first and k == 0, last and k == 1)
                    mm.then_inc(w_used, 1)

                for b in range(8):
                    take(b, ("ffn_out", f, 1))
                gate_up(u0 % RING, u0 + 1, 0, True, False)
                gate_up((u0 + 1) % RING, u0 + 2, 1, False, True)
                transpose_hid(0)
                gate_up((u0 + 2) % RING, u0 + 3, 0, True, False)
                gate_up(u0 % RING, u0 + 4, 1, False, True)
                down((u0 + 1) % RING, u0 + 5, 0, True, False)
                transpose_hid(1)
                with pe.Fori(2, FI) as i:
                    gate_up((u0 + 2) % RING, i * 3 + u0, 0, True, False)
                    gate_up(u0 % RING, i * 3 + (u0 + 1), 1, False, True)
                    down((u0 + 1) % RING, i * 3 + (u0 + 2), i - 1, False, False)
                    transpose_hid(i)
                u = u0 + 3 * FI - 1
                down(u % RING, u + 1, FI - 1, False, True)
                note(("ffn_full", f), "w_used", u + 1)

            def attention(name, heads, qk, v, dv, base=0):
                def scores(h):
                    take(4 + h % 2, ("soft", name, h))
                    b = bank[4 + h % 2]
                    for t in range(T):
                        out = b[:, 0:P] if t == 0 else b[:, P:3 * P]
                        terms = qk(h, t)
                        for n, (q, k) in enumerate(terms):
                            mm = pe.matmul(out, q, k, start=n == 0, stop=n == len(terms) - 1)
                    mm.then_inc(pe_done, mark("pe_done", "S", name, h))

                def turn(h):
                    need("pe", "exp", name, h)
                    transposes(2 + h % 2, ("pT", name, h), ("PT", name, h),
                               [(c * P, pr[:, h % 2, c * P:(c + 1) * P]) for c in range(3)])

                def weigh(h):
                    take(6 + h % 2, ("o", name, h))
                    need("pe", "pT", name, h)
                    b, p = bank[6 + h % 2], pT[:, h % 2]
                    pe.matmul(b[:, 0:dv], p[:, 0:P], v(h, 0), start=True, stop=True)
                    pe.matmul(b[:, dv:2 * dv], p[:, P:2 * P], v(h, 0), start=True, stop=False)
                    pe.matmul(b[:, dv:2 * dv], p[:, 2 * P:3 * P], v(h, 1), start=False, stop=True)\
                        .then_inc(pe_done, mark("pe_done", "PV", name, h))

                for s in range(len(heads) + 2):
                    if s < len(heads):
                        scores(heads[s])
                    if 1 <= s <= len(heads):
                        turn(heads[s - 1])
                    if s >= 2:
                        weigh(heads[s - 2])

            def tok(t):
                return slice(t * P, (t + 1) * P)

            pe.wait_ge(const_loaded, N_CONST)
            to_xT(0, ra, KD)
            need_xT(0)
            for n, stage in enumerate(("rq0", "rk0", "rv0", "rv1", "mq0", "mk0", "mv0")):
                chunk(stage, ((0, 1), (2, 3))[n % 2], "ev")
            for a, (src, name) in enumerate(((rqk, "rot"), (mqk, "mnorm"))):
                if a == 1:
                    for h in range(RET_H + 1):
                        if h < RET_H:
                            for i in range(2):
                                need("pe", "qkT", "rot", i, 0)
                                need("pe", "qkT", "rot", i, 1)
                            take(4 + h % 2, ("decayed", h))
                            b = bank[4 + h % 2]
                            pe.matmul(b[:, 0:S], rkT[:, h, 0:P], rqT[:, h, :], start=True, stop=True)
                            pe.matmul(b[:, S:S + P], rkT[:, h, P:S], rqT[:, h, P:S], start=True, stop=True)\
                                .then_inc(pe_done, mark("pe_done", "RS", h))
                        if h >= 1:
                            g = h - 1
                            take(6 + g % 2, ("ro", g))
                            need("pe", "decayed", g)
                            b, s = bank[6 + g % 2], pT[:, g % 2]
                            v = [rv[:, t, g * RET_DV:(g + 1) * RET_DV] for t in range(T)]
                            pe.matmul(b[:, 0:RET_DV], s[:, 0:P], v[0], start=True, stop=True)
                            pe.matmul(b[:, RET_DV:], s[:, P:2 * P], v[0], start=True, stop=False)
                            pe.matmul(b[:, RET_DV:], s[:, 2 * P:3 * P], v[1], start=False, stop=True)\
                                .then_inc(pe_done, mark("pe_done", "RO", g))
                for i in range(2):
                    for t in range(T):
                        need("pe", name, i, t)
                        transposes(2 * (t % 2) + i, ("qkT", name, i, t), ("qkTf", name, i, t),
                                   [(j * P, src[:, 2 * i + t, j * P:(j + 1) * P]) for j in range(4)])

            for i in range(2):
                for t in range(T):
                    need("pe", "qkT", "mnorm", i, t)

            def moba_qk(h, t):
                r = slice(64 * (h % 2), 64 * (h % 2) + 64)
                return [(mqT[r, h // 2, tok(t)], mkT[r, h // 2, 0:(t + 1) * P])]

            attention("moba", range(MOBA_H), moba_qk,
                      lambda h, t: mv[:, t, h * MOBA_DH:(h + 1) * MOBA_DH], MOBA_DH)
            chunk("rg0", (0, 1), "ev")
            chunk("rg1", (2, 3), "ev")
            to_xT("ret", ro, KD)
            need_xT("ret")
            chunk("ret_out0", (0, 1), "ev", slot0=8)
            chunk("ret_out1", (2, 3), "ev", slot0=8)
            chunk("ga0", (0, 1), "ev")
            chunk("ga1", (2, 3), "ev")
            to_xT("moba", mo, 4)
            need_xT("moba", 4)
            chunk("moba_out0", (2, 3), "ev", slot0=8)
            chunk("moba_out1", (0, 1), "ev", slot0=8)
            chunk("gb0", (2, 3), "ev")
            chunk("gb1", (0, 1), "ev")
            to_xT("mix", mix, KD)
            need_xT("mix")
            chunk("w_o0", (0, 1), "ev")
            chunk("w_o1", (2, 3), "ev")
            to_xT(1, ra, KD)
            need_xT(1)
            ffn(0)
            for l in range(2):
                if l == 0:
                    to_xT("raw", x, KD)
                    need_xT("raw")
                if l == 1:
                    chunk("kv_down0", (4, 5), "ev")
                    for t in range(T):
                        need("pe", "ckv", t)
                        take(6 + t, ("ckvT", t))
                        for c in range(3):
                            src = cq[:, t, c * P:(c + 1) * P] if c < 2 else kr[:, t, :]
                            mm = pe.matmul(bank[6 + t][:, c * P:(c + 1) * P], src, ident, is_transpose=True,
                                           start=True, stop=True)
                        mm.then_inc(pe_done, mark("pe_done", "ckvTf", t))
                    for t in range(T):
                        need("pe", "ckvT", t)
                    for c in range(MLA_H // 2 + 1):
                        if c < MLA_H // 2:
                            chunk("kv_up", ((0, 1), (2, 3))[c % 2], "ev", src=(cTh, cTl),
                                  part=(c // 2, (c % 2) * CH, CH, c % 2 == 1))
                        if c:
                            for t in range(T):
                                need("pe", "ks", c - 1, t)
                            transposes(4 + c % 2, ("kT", c - 1), ("kTf", c - 1),
                                       [(j * S + t * P, qs[:, t, j * P:(j + 1) * P])
                                        for t in range(T) for j in range(2)])
                ffn(1 + 2 * l)
                to_xT(2 + 4 * l, x, KD)
                need_xT(2 + 4 * l)
                if l == 0:
                    chunk("fox_f", (4, 5), "ev")
                    for c in range(7):
                        if c < 6:
                            chunk(f"fox_in{c}", ((0, 1), (2, 3))[c % 2], "ev")
                        if c == 1:
                            need("pe", "logf")
                            pe.wait_ge(ones_set, 1)
                            ls = [fg[:, 5, t * FOX_H:(t + 1) * FOX_H] for t in range(T)]
                            take(6, ("cb",))
                            pe.matmul(bank[6][:, 0:FOX_H], upper, ls[0], start=True, stop=True)
                            pe.matmul(bank[6][:, FOX_H:2 * FOX_H], ones, ls[0], start=True, stop=False)
                            pe.matmul(bank[6][:, FOX_H:2 * FOX_H], upper, ls[1], start=False, stop=True)\
                                .then_inc(pe_done, mark("pe_done", "cum"))
                            take(7, ("cumT",))
                            pe.matmul(bank[7][0:FOX_H, 0:P], ls[0], upper, start=True, stop=True)
                            pe.matmul(bank[7][0:FOX_H, P:S], ls[0], ones, start=True, stop=False)
                            pe.matmul(bank[7][0:FOX_H, P:S], ls[1], upper, start=False, stop=True)\
                                .then_inc(pe_done, mark("pe_done", "cumTf"))
                        if 1 <= c <= 4:
                            for t in range(T):
                                need("pe", "ev", f"fox_in{c - 1}", t)
                                transposes(4 + t, ("fT", c - 1, t), ("fTf", c - 1, t),
                                           [(j * P, fqk[:, t, j * P:(j + 1) * P]) for j in range(4)])
                    for c in range(4):
                        for t in range(T):
                            need("pe", "fT", c, t)
                    need("pe", "cumT")
                    need("pe", "fv")
                    pe.wait_ge(aux_loaded, 16)

                    def fox_qk(h, t):
                        r = slice(64 * (h % 2), 64 * (h % 2) + 64)
                        keys = slice(0, (t + 1) * P)
                        return [(fqT[r, h // 2, tok(t)], fkT[r, h // 2, keys]),
                                (fsel[0:FOX_H, h, :], cumT[0:FOX_H, keys])]

                    attention("fox", range(FOX_H), fox_qk,
                              lambda h, t: fv[:, t, h * FOX_DH:(h + 1) * FOX_DH], FOX_DH)
                    to_xT("fox", fo, KD)
                    need_xT("fox")
                    chunk("fox_o0", (0, 1), "ev")
                    chunk("fox_o1", (2, 3), "ev")
                else:
                    chunk("dq0", (4, 5), "ev")
                    for t in range(T):
                        need("pe", "cqn", t)
                        take(6 + t, ("cqT", t))
                        for c in range(3):
                            mm = pe.matmul(bank[6 + t][:, c * P:(c + 1) * P], cq[:, t, c * P:(c + 1) * P], ident,
                                           is_transpose=True, start=True, stop=True)
                        mm.then_inc(pe_done, mark("pe_done", "cqTf", t))
                    for t in range(T):
                        need("pe", "cqT", t)

                    def mla_qk(h, t):
                        r = slice(64 * (h % 2), 64 * (h % 2) + 64)
                        keys = slice(0, (t + 1) * P)
                        return [(qT[:, h % 2, tok(t)], kT[:, h, keys]), (qT[r, 2, tok(t)], krT[r, keys])]

                    for g in range(MLA_H // 2):
                        u = unit_at["uq"][g]
                        for t in range(T):
                            take(t, ("qs", g, t))
                        pe.wait_ge(w_lo_done, u + 1)
                        wh, wl = (w[u % RING][:, 0:3 * QL].rearrange("p (k n) -> p k n", k=3) for w in (w_hi, w_lo))
                        for j in range(3):
                            for t in range(T):
                                mm = mm3(bank[t][:, 0:QL], cTh[:, j, tok(t)], cTl[:, j, tok(t)], wh[:, j],
                                         wl[:, j], j == 0, j == 2)
                                if j == 2 and t == 0:
                                    mm.then_inc(pe_done, mark("pe_done", "qf", g, 0))
                        mm.then_inc(w_used, 1)
                        note(("qf", g, 1), "w_used", u + 1)
                        for t in range(T):
                            need("pe", "qs", g, t)
                            transposes(4 + t, ("qT", g, t), ("qTf", g, t),
                                       [(j * P, qs[:, t, j * P:(j + 1) * P]) for j in range(3)])
                        for t in range(T):
                            need("pe", "qT", g, t)
                        attention("mla", (2 * g, 2 * g + 1), mla_qk,
                                  lambda h, t: vv[:, t, h * VD:(h + 1) * VD], VD)
                        for h in range(2 * g, 2 * g + 2):
                            need("pe", "o", "mla", h)
                        transposes(0, ("oT", g), ("oTf", g),
                                   [(j * S + t * P, mlo[:, t, j * VD:(j + 1) * VD]) for t in range(T) for j in range(2)])
                    for g in range(MLA_H // 2):
                        need("pe", "oT", g)
                    chunk("mla_o0", (0, 1), "ev")
                    chunk("mla_o1", (2, 3), "ev")
                to_xT(3 + 4 * l, x, KD)
                need_xT(3 + 4 * l)
                ffn(2 + 2 * l)
                pe.wait_ge(p_loaded, 16 * (l + 1))
                transposes(0, ("pT", l), ("pTf", l),
                           [(j * S + t * P, pin[:, t, j * P:(j + 1) * P]) for t in range(T) for j in range(2)])
                need("pe", "pT", l)
                for c in range(2):
                    chunk(f"ple_p{l}", ((4, 5), (6, 7))[c], "ev", src=(cTh, cTl), part=(0, c * CH, CH, c == 1))
                to_xT(4 + 4 * l, x, KD)
                need_xT(4 + 4 * l)
                chunk(f"ple_g{l}0", (0, 1), "ev")
                chunk(f"ple_g{l}1", (2, 3), "ev")
                if l == 0:
                    to_xT(5, x, KD)
                    need_xT(5)

        @block.scalar
        def _(act):
            ENG["act"] = act
            for name, dst in CONSTS:
                act.dma_start(dst, const_src[name]).then_inc(const_loaded, 16)
            split = [0]

            def split_to(n):
                while split[0] < min(n, N_UNITS):
                    u = split[0]
                    cols = units[u][1] * units[u][2] or UNIT
                    act.wait_ge(w_loaded[u % RING], 32 * (u // RING + 1))
                    if u >= RING:
                        act.wait_ge(w_used, u - RING + 1)
                    nc.scalar.activation(w_hi[u % RING][:, 0:cols], w_raw[u % RING][:, 0:cols], ACT.Copy)\
                        .then_inc(w_hi_done, 1)
                    split[0] += 1

            def ahead(stage, part=None):
                us = unit_at[stage]
                split_to((us[-1] if part is None else us[part]) + RING)

            def go(label, out, in_, func=ACT.Copy, **kw):
                nc.scalar.activation(out, in_, func, **kw).then_inc(act_done, mark("act_done", *label))

            def xT_evac(site, count=KD, slot0=0, b0=0, scale=1.0):
                for t in range(T):
                    for q in range(count // 4):
                        need("act", "T", site, t, q)
                        b = (b0 + t * (count // 4) + q) % 4
                        go(("xTh", site, t, q), xTh[:, slot0 + 4 * q:slot0 + 4 * q + 4, t * P:(t + 1) * P],
                           bank[b].rearrange("p (k n) -> p k n", k=4), scale=scale)

            def ffn(f):
                u0 = unit_at[f"ffn{f}"][0]
                g0 = f * FI

                def split_unit(slot, loaded, used):
                    act.wait_ge(w_loaded[slot], loaded)
                    act.wait_ge(w_used, used)
                    nc.scalar.activation(w_hi[slot][:, :], w_raw[slot][:, :], ACT.Copy).then_inc(w_hi_done, 1)

                def half_tanh(i, last_used):
                    act.wait_ge(gu0_full, i + (g0 + 1))
                    nc.scalar.activation(tanh[:, 0, 0:HB], bank[0][:, 0:HB], ACT.Tanh, scale=0.5)\
                        .then_inc(tanh_done, 1)
                    act.wait_ge(w_used, last_used)
                    nc.scalar.activation(tanh[:, 1, 0:HB], bank[1][:, 0:HB], ACT.Tanh, scale=0.5)\
                        .then_inc(tanh_done, 1)

                def hT_round(i):
                    for k in range(2):
                        act.wait_ge(hT_full, i * 2 + (2 * g0 + k + 1))
                        nc.scalar.activation(hTh[:, k, :], bank[2 + k][:, 0:S], ACT.Copy).then_inc(hT_hi, 1)

                split_to(u0 + 3)
                half_tanh(0, u0 + 2)
                split_to(u0 + 4)
                hT_round(0)
                with act.Fori(1, FI) as i:
                    s, n = (u0 + 4) % RING, (u0 + 4) // RING
                    split_unit(s, i * 32 + 32 * n, i * 3 + (u0 - 1))
                    half_tanh(i, i * 3 + (u0 + 1))
                    s, n = (u0 + 5) % RING, (u0 + 5) // RING
                    split_unit(s, i * 32 + 32 * n, i * 3 + u0)
                    s, n = (u0 + 6) % RING, (u0 + 6) // RING
                    split_unit(s, i * 32 + 32 * n, i * 3 + (u0 + 1))
                    hT_round(i)
                split[0] = u0 + 3 * FI + 1
                split_to(u0 + 3 * FI + 2)

            def attention(name, heads, scale):
                def exps(h):
                    need("act", "soft", name, h)
                    for t in range(T):
                        c = slice(0, P) if t == 0 else slice(P, 3 * P)
                        go(("exp", name, h) if t else (), pr[:, h % 2, c], sm[:, h % 2, c], ACT.Exp,
                           bias=negmax[:, 2 * (h % 4) + t:2 * (h % 4) + t + 1], scale=scale,
                           accum_out=psum_e[:, 2 * (h % 4) + t:2 * (h % 4) + t + 1])

                def turned(h):
                    need("act", "PT", name, h)
                    go(("pT", name, h), pT[:, h % 2], bank[2 + h % 2][:, 0:3 * P])

                for s in range(len(heads) + 1):
                    if s < len(heads):
                        exps(heads[s])
                    if s >= 1:
                        turned(heads[s - 1])

            act.wait_ge(const_loaded, N_CONST)
            for t in range(T):
                go(("ssq", 0, t), tanh[:, 0, :], x[:, t, 0:CH], ACT.Square, accum_out=stats[:, 2 * t:2 * t + 1])
                act.wait_ge(act_done, counts["act_done"])
                go(("ssq", 1, t), tanh[:, 0, :], x[:, t, CH:D], ACT.Square,
                   accum_out=stats[:, 2 * t + 1:2 * t + 2])
                act.wait_ge(act_done, counts["act_done"])
            split_to(3)
            xT_evac(0)
            ahead("rq0")
            ahead("rk0")
            for n, stage in enumerate(("rv0", "rv1")):
                ahead(stage)
                for t in range(T):
                    need("act", "full", stage, t)
                    go(("ev", stage, t), rv[:, t, n * CH:(n + 1) * CH], bank[2 * n + t])
            for n, stage in enumerate(("mq0", "mk0")):
                ahead(stage)
                for t in range(T):
                    need("act", "full", stage, t)
                    go(("ev", stage, t), mqk[:, 2 * n + t], bank[2 * n + t])
                    act.wait_ge(act_done, counts["act_done"])
                    if n * T + t:
                        need("act", "mss", n * T + t - 1)
                    go(("msq", n, t), tanh[:, 0], mqk[:, 2 * n + t], ACT.Square)
            ahead("mv0")
            for t in range(T):
                need("act", "full", "mv0", t)
                go(("ev", "mv0", t), mv[:, t], bank[t])
            for i in range(2):
                for t in range(T):
                    need("act", "qkTf", "rot", i, t)
                    go(("qkT", "rot", i, t), (rqT, rkT)[i][:, :, t * P:(t + 1) * P],
                       bank[2 * (t % 2) + i].rearrange("p (k n) -> p k n", k=4))
            for h in range(RET_H):
                need("act", "rstats", h)
                go(("ro", h), ro[:, :, h * RET_DV:(h + 1) * RET_DV],
                   bank[6 + h % 2].rearrange("p (t n) -> p t n", t=T))
            for i in range(2):
                for t in range(T):
                    need("act", "qkTf", "mnorm", i, t)
                    go(("qkT", "mnorm", i, t), (mqT, mkT)[i][:, :, t * P:(t + 1) * P],
                       bank[2 * (t % 2) + i].rearrange("p (k n) -> p k n", k=4))
            attention("moba", range(MOBA_H), MOBA_DH ** -0.5)

            def gate(stage, b, free_of):
                ahead(stage)
                for t in range(T):
                    need("act", "full", stage, t)
                    if free_of:
                        need("act", *free_of, t)
                    go(("tanh", stage, t), tanh[:, t], bank[b + t], ACT.Tanh, scale=0.5)

            gate("rg0", 0, None)
            gate("rg1", 2, ("ev", "rg0"))
            xT_evac("ret", slot0=8)
            for n in range(2):
                ahead(f"ret_out{n}")
                for t in range(T):
                    need("act", "full", f"ret_out{n}", t)
                    go(("ev", f"ret_out{n}", t), ra[:, t, n * CH:(n + 1) * CH], bank[2 * n + t])
            gate("ga0", 0, ("ev", "rg1"))
            gate("ga1", 2, ("ev", "ga0"))
            xT_evac("moba", 4, slot0=8)
            for n in range(2):
                ahead(f"moba_out{n}")
                for t in range(T):
                    need("act", "full", f"moba_out{n}", t)
                    need("act", "ev", "ga1", t)
                    go(("ev", f"moba_out{n}", t), ra[:, t, n * CH:(n + 1) * CH], bank[2 - 2 * n + t])
            gate("gb0", 2, ("ev", "ga1"))
            gate("gb1", 0, ("ev", "gb0"))
            xT_evac("mix", scale=0.5)
            ahead("w_o0")
            ahead("w_o1")
            need("act", "upd", 1)
            for t in range(T):
                for c in range(2):
                    go(("ssq1", c, t), tanh[:, 0, :], x[:, t, c * CH:(c + 1) * CH], ACT.Square,
                       accum_out=stats[:, 2 * t + c:2 * t + c + 1])
                    act.wait_ge(act_done, counts["act_done"])
            xT_evac(1)
            ffn(0)
            for l in range(2):
                if l == 0:
                    xT_evac("raw")
                if l == 1:
                    ahead("kv_down0")
                    for t in range(T):
                        need("act", "full", "kv_down0", t)
                        go(("kvsq", t), tanh[:, t, 0:KVL], bank[4 + t][:, 0:KVL], ACT.Square,
                           accum_out=stats[:, t:t + 1])
                    for t in range(T):
                        need("act", "ckvTf", t)
                        go(("ckvTh", t), cTh[:, 0:2, t * P:(t + 1) * P],
                           bank[6 + t][:, 0:2 * P].rearrange("p (k n) -> p k n", k=2))
                        go(("krT", t), krT[:, t * P:(t + 1) * P], bank[6 + t][:, 2 * P:3 * P])
                    for c in range(MLA_H // 2 + 1):
                        if c < MLA_H // 2:
                            if c % 2 == 1:
                                ahead("kv_up", c // 2)
                            for t in range(T):
                                need("act", "full", "kv_up", c, t)
                                if c:
                                    need("act", "kTf", c - 1)
                                go(("ks", c, t), qs[:, t, 0:2 * NOPE].rearrange("p (h n) -> p h n", h=2),
                                   bank[2 * (c % 2) + t].rearrange("p (h n) -> p h n", h=2)[:, :, 0:NOPE])
                        if c:
                            need("act", "kTf", c - 1)
                            go(("kT", c - 1), kT[:, 2 * c - 2:2 * c, :],
                               bank[4 + c % 2].rearrange("p (h n) -> p h n", h=2))
                ffn(1 + 2 * l)
                xT_evac(2 + 4 * l)
                if l == 0:
                    ahead("fox_f")
                    need("act", "fz")
                    go(("fabs",), fg[:, 1], fg[:, 0], ACT.Abs)
                    act.wait_ge(act_done, counts["act_done"])
                    go(("fexp",), fg[:, 2], fg[:, 1], ACT.Exp, scale=-1.0)
                    need("act", "fexp1")
                    go(("fln",), fg[:, 3], fg[:, 3], ACT.Ln)
                    for c in range(4):
                        ahead(f"fox_in{c}")
                        for t in range(T):
                            need("act", "full", f"fox_in{c}", t)
                            if c:
                                need("act", "fTf", c - 1, t)
                            go(("ev", f"fox_in{c}", t), fqk[:, t], bank[2 * (c % 2) + t])
                        if c == 1:
                            need("act", "cumTf")
                            go(("cumT",), cumT[0:FOX_H], bank[7][0:FOX_H, 0:S])
                        for t in range(T):
                            need("act", "fTf", c, t)
                            dst = (fqT, fkT)[c // 2][:, 4 * (c % 2):4 * (c % 2) + 4, t * P:(t + 1) * P]
                            go(("fT", c, t), dst, bank[4 + t].rearrange("p (k n) -> p k n", k=4))
                    for c in (4, 5):
                        ahead(f"fox_in{c}")
                    attention("fox", range(FOX_H), FOX_DH ** -0.5)
                    xT_evac("fox")
                    ahead("fox_o0")
                    ahead("fox_o1")
                else:
                    ahead("dq0")
                    for t in range(T):
                        need("act", "full", "dq0", t)
                        go(("cqsq", t), tanh[:, t, 0:QL], bank[4 + t][:, 0:QL], ACT.Square,
                           accum_out=stats[:, t:t + 1])
                    for t in range(T):
                        need("act", "cqTf", t)
                        go(("cqTh", t), cTh[:, :, t * P:(t + 1) * P],
                           bank[6 + t][:, 0:3 * P].rearrange("p (k n) -> p k n", k=3))
                    for g in range(MLA_H // 2):
                        ahead("uq", g)
                        for t in range(T):
                            need("act", "qf", g, t)
                            if g:
                                need("act", "qTf", g - 1, t)
                            go(("qn", g, t), qs[:, t, 0:2 * NOPE].rearrange("p (h n) -> p h n", h=2),
                               bank[t][:, 0:QL].rearrange("p (h n) -> p h n", h=2)[:, :, 0:NOPE])
                        for t in range(T):
                            need("act", "qTf", g, t)
                            go(("qT", g, t), qT[:, :, t * P:(t + 1) * P],
                               bank[4 + t][:, 0:3 * P].rearrange("p (k n) -> p k n", k=3))
                        attention("mla", (2 * g, 2 * g + 1), (NOPE + ROPE_D) ** -0.5)
                        need("act", "oTf", g)
                        go(("oTh", g), xTh[:, 2 * g:2 * g + 2, :], bank[0].rearrange("p (k n) -> p k n", k=2))
                    ahead("mla_o0")
                    ahead("mla_o1")
                xT_evac(3 + 4 * l)
                ffn(2 + 2 * l)
                need("act", "pTf", l)
                go(("pTh", l), cTh[:, 0:2, :], bank[0].rearrange("p (k n) -> p k n", k=2))
                for c in range(2):
                    if c == 1:
                        ahead(f"ple_p{l}")
                    for t in range(T):
                        need("act", "full", f"ple_p{l}", c, t)
                        go(("ev", f"ple_p{l}", c, t), pp[:, t, c * CH:(c + 1) * CH], bank[4 + 2 * c + t], scale=0.5)
                xT_evac(4 + 4 * l)
                for c in range(2):
                    ahead(f"ple_g{l}{c}")
                    for t in range(T):
                        need("act", "pz", l, c, t)
                        go(("ptanh", l, c, t), tanh[:, t], pz[:, t], ACT.Tanh, scale=0.5)
                if l == 0:
                    xT_evac(5)

        @block.vector
        def _(dve):
            ENG["dve"] = dve
            split = [0]

            def split_to(n):
                while split[0] < min(n, N_UNITS):
                    u = split[0]
                    cols = units[u][1] * units[u][2] or UNIT
                    dve.wait_ge(w_hi_done, u + 1)
                    lo(u % RING, cols)
                    split[0] += 1

            def lo(slot, cols=UNIT):
                nc.vector.tensor_tensor(w_lo[slot][:, 0:cols], w_raw[slot][:, 0:cols],
                                        w_hi[slot][:, 0:cols].bitcast(F32), ALU.subtract).then_inc(w_lo_done, 1)

            def ahead(stage, part=None):
                us = unit_at[stage]
                split_to((us[-1] if part is None else us[part]) + RING)

            def did(ins, *label):
                ins.then_inc(dve_done, mark("dve_done", *label))

            def settle():
                dve.wait_ge(dve_done, counts["dve_done"])

            def rsqrt(n, label=()):
                v, y, a, b = (r[:, 0:n] for r in (rs_v, rs_y, rs_a, rs_b))
                settle()
                did(nc.vector.tensor_scalar(a.bitcast(I32), v.bitcast(I32), 1, None, ALU.logical_shift_right))
                settle()
                did(nc.vector.tensor_scalar(y.bitcast(I32), a.bitcast(I32), -1.0, float(0x5F3759DF), ALU.mult, ALU.add))
                for step in range(3):
                    settle()
                    did(nc.vector.tensor_tensor(a, y, y, ALU.mult))
                    settle()
                    did(nc.vector.scalar_tensor_tensor(out=b, in0=a, scalar=-0.5, in1=v, op0=ALU.mult, op1=ALU.mult))
                    settle()
                    did(nc.vector.scalar_tensor_tensor(out=y, in0=b, scalar=1.5, in1=y, op0=ALU.add, op1=ALU.mult),
                        *(label if step == 2 else ()))
                settle()

            def xT_evac(site, count=KD, slot0=0, b0=0, scale=None):
                for t in range(T):
                    for q in range(count // 4):
                        need("dve", "xTh", site, t, q)
                        b = (b0 + t * (count // 4) + q) % 4
                        sl = (slice(None), slice(slot0 + 4 * q, slot0 + 4 * q + 4), slice(t * P, (t + 1) * P))
                        src = bank[b].rearrange("p (k n) -> p k n", k=4)
                        if scale is None:
                            did(nc.vector.tensor_tensor(xTl[sl], src, xTh[sl].bitcast(F32), ALU.subtract),
                                "xT", site, t, q)
                        else:
                            did(nc.vector.scalar_tensor_tensor(out=xTl[sl], in0=src, scalar=scale,
                                                               in1=xTh[sl].bitcast(F32), op0=ALU.mult,
                                                               op1=ALU.subtract), "xT", site, t, q)

            def rms_rows(site):
                did(nc.vector.tensor_reduce(rs_a[:, 0:T], stats[:, 0:2 * T].rearrange("p (t c) -> p t c", t=T),
                                            AX_X, ALU.add))
                settle()
                did(nc.vector.tensor_scalar(rs_v[:, 0:T], rs_a[:, 0:T], 1.0 / D, RMS_EPS, ALU.mult, ALU.add))
                rsqrt(T)
                for t in range(T):
                    dve.wait_ge(gb_loaded, 32 * (site + 1))
                    did(nc.vector.scalar_tensor_tensor(out=ra[:, t], in0=x[:, t], scalar=rs_y[:, t:t + 1],
                                                       in1=gb[:, 0], op0=ALU.mult, op1=ALU.mult), "norm", site, t)

            def layer_norm(site):
                settle()
                st = stats[:, 0:24].rearrange("p (t c s) -> p t c s", t=T, c=2)
                for t in range(T):
                    for c in range(2):
                        did(nc.vector.bn_stats(st[:, t, c], x[:, t, c * CH:(c + 1) * CH]))
                settle()
                for t in range(T):
                    did(nc.vector.bn_aggr(mv_[:, t], stats[:, 12 * t:12 * t + 12]))
                settle()
                did(nc.vector.tensor_scalar(rs_v[:, 0:T], mv_[:, 0:T, 1], LN_EPS, None, ALU.add))
                rsqrt(T)
                dve.wait_ge(gb_loaded, 32 * (site + 1))
                for t in range(T):
                    did(nc.vector.scalar_tensor_tensor(out=x[:, t], in0=x[:, t], scalar=mv_[:, t, 0:1],
                                                       in1=gb[:, 0], op0=ALU.subtract, op1=ALU.mult))
                    settle()
                    did(nc.vector.scalar_tensor_tensor(out=x[:, t], in0=x[:, t], scalar=rs_y[:, t:t + 1],
                                                       in1=gb[:, 1], op0=ALU.mult, op1=ALU.add), "norm", site, t)

            def ffn(f, alpha):
                u0 = unit_at[f"ffn{f}"][0]
                g0 = f * FI
                half = 0.5 if f == 0 else 0.25

                def hidden(i):
                    for t in range(T):
                        dve.wait_ge(tanh_done, i * 2 + (2 * g0 + t + 1))
                        nc.vector.scalar_tensor_tensor(out=hid[:, t], in0=tanh[:, t, 0:HB], scalar=1.0,
                                                       in1=bank[t][:, 0:HB], op0=ALU.add, op1=ALU.mult)\
                            .then_inc(hid_part, 1)
                    for t in range(T):
                        dve.wait_ge(hid_part, i * 2 + (2 * g0 + t + 1))
                        nc.vector.scalar_tensor_tensor(out=hid[:, t], in0=hid[:, t], scalar=half,
                                                       in1=bank[t][:, HB:2 * HB], op0=ALU.mult, op1=ALU.mult)\
                            .then_inc(hid_done, 1)

                def hT_rest(i):
                    for k in range(2):
                        dve.wait_ge(hT_hi, i * 2 + (2 * g0 + k + 1))
                        nc.vector.tensor_tensor(hTl[:, k, :], bank[2 + k][:, 0:S], hTh[:, k, :].bitcast(F32),
                                                ALU.subtract).then_inc(hT_lo, 1)

                split_to(u0 + 3)
                hidden(0)
                split_to(u0 + 4)
                hT_rest(0)
                with dve.Fori(1, FI) as i:
                    dve.wait_ge(w_hi_done, i * 3 + (u0 + 2))
                    lo((u0 + 4) % RING)
                    hidden(i)
                    dve.wait_ge(w_hi_done, i * 3 + (u0 + 3))
                    lo((u0 + 5) % RING)
                    dve.wait_ge(w_hi_done, i * 3 + (u0 + 4))
                    lo((u0 + 6) % RING)
                    hT_rest(i)
                split[0] = u0 + 3 * FI + 1
                need("dve", "ffn_full", f)
                for t in range(T):
                    did(nc.vector.scalar_tensor_tensor(out=x[:, t], in0=x[:, t], scalar=alpha, in1=acc[:, t],
                                                       op0=ALU.mult, op1=ALU.add), "ffn_out", f, t)
                split_to(u0 + 3 * FI + 2)

            def attention(name, heads, bias=None, out=None, dv=64):
                def soft(h):
                    need("dve", "S", name, h)
                    if h >= 2:
                        need("dve", "exp", name, h - 2)
                    b = bank[4 + h % 2]
                    if bias is None:
                        did(nc.vector.tensor_tensor(sm[:, h % 2], b[:, 0:3 * P], mask, ALU.add), "soft0", name, h)
                    else:
                        for t in range(T):
                            c = slice(0, P) if t == 0 else slice(P, 3 * P)
                            did(nc.vector.scalar_tensor_tensor(out=sm[:, h % 2, c], in0=b[:, c],
                                                               scalar=bias(h, t), in1=mask[:, c],
                                                               op0=ALU.add, op1=ALU.add))
                    settle()
                    s = 2 * (h % 4)
                    did(nc.vector.tensor_reduce(rs_a[:, 0:1], sm[:, h % 2, 0:P], AX_X, ALU.max))
                    did(nc.vector.tensor_reduce(rs_a[:, 1:2], sm[:, h % 2, P:3 * P], AX_X, ALU.max))
                    settle()
                    did(nc.vector.tensor_scalar(negmax[:, s:s + 2], rs_a[:, 0:2], -SCALE[name], None, ALU.mult),
                        "soft", name, h)

                def gather(h):
                    need("dve", "PV", name, h)
                    s, r = 2 * (h % 4), 2 * (h % 2)
                    did(nc.vector.reciprocal(rsum[:, r:r + 2], psum_e[:, s:s + 2]))
                    settle()
                    for t in range(T):
                        did(nc.vector.tensor_scalar(out(h, t), bank[6 + h % 2][:, t * dv:(t + 1) * dv],
                                                    rsum[:, r + t:r + t + 1], None, ALU.mult),
                            *(("o", name, h) if t else ()))

                for s in range(len(heads) + 2):
                    if s < len(heads):
                        soft(heads[s])
                    if s >= 2:
                        gather(heads[s - 2])

            SCALE = {"moba": MOBA_DH ** -0.5, "fox": FOX_DH ** -0.5, "mla": (NOPE + ROPE_D) ** -0.5}

            dve.wait_ge(const_loaded, N_CONST)
            need("dve", "ssq", 1, 1)
            rms_rows(0)
            split_to(3)
            xT_evac(0)
            for n, stage in enumerate(("rq0", "rk0")):
                ahead(stage)
                for t in range(T):
                    need("dve", "full", stage, t)
                    if n or t:
                        settle()
                    b = bank[2 * n + t].rearrange("p (h a n) -> p h a n", h=RET_H, a=2)
                    r = rope_ret[:, t].rearrange("p (a n) -> p a n", a=4)
                    o = rqk[:, 2 * n + t].rearrange("p (h a n) -> p h a n", h=RET_H, a=2)
                    z = rtmp.rearrange("p (h a n) -> p h a n", h=RET_H, a=2)
                    for a in range(2):
                        did(nc.vector.tensor_tensor(z[:, :, a], b[:, :, 1 - a],
                                                    r[:, 2 + a].unsqueeze(1).broadcast_to([P, RET_H, 64]), ALU.mult))
                        did(nc.vector.tensor_tensor(o[:, :, a], b[:, :, a],
                                                    r[:, a].unsqueeze(1).broadcast_to([P, RET_H, 64]), ALU.mult),
                            *(("ev", stage, t) if a else ()))
                    settle()
                    did(nc.vector.tensor_tensor(rqk[:, 2 * n + t], rqk[:, 2 * n + t], rtmp, ALU.add), "rot", n, t)
            ahead("rv0")
            ahead("rv1")
            for n, stage in enumerate(("mq0", "mk0")):
                ahead(stage)
                for t in range(T):
                    need("dve", "msq", n, t)
                    did(nc.vector.tensor_reduce(rs_b[:, 8 * (2 * n + t):8 * (2 * n + t) + 8],
                                                tanh[:, 0].rearrange("p (h n) -> p h n", n=MOBA_DH), AX_X, ALU.add),
                        "mss", 2 * n + t)
            ahead("mv0")
            settle()
            did(nc.vector.tensor_scalar(rs_v, rs_b, 1.0 / MOBA_DH, RMS_EPS, ALU.mult, ALU.add))
            rsqrt(32)
            for h in range(RET_H + 1):
                if h < RET_H:
                    need("dve", "RS", h)
                    did(nc.vector.tensor_tensor(pT[:, h % 2], bank[4 + h % 2][:, 0:3 * P], decay[:, h], ALU.mult),
                        "decayed", h)
                if h >= 1:
                    g = h - 1
                    need("dve", "RO", g)
                    for t in range(T):
                        did(nc.vector.bn_stats(stats[:, 6 * t:6 * t + 6],
                                               bank[6 + g % 2][:, t * RET_DV:(t + 1) * RET_DV]),
                            *(("rstats", g) if t else ()))
                    settle()
                    for t in range(T):
                        did(nc.vector.bn_aggr(mv_[:, 2 * g + t], stats[:, 6 * t:6 * t + 6]))
                    settle()
            for i in range(2):
                for t in range(T):
                    m = mqk[:, 2 * i + t].rearrange("p (h n) -> p h n", n=MOBA_DH)
                    y = rs_y[:, 8 * (2 * i + t):8 * (2 * i + t) + 8]
                    did(nc.vector.tensor_tensor(m, m, y.unsqueeze(2).broadcast_to([P, MOBA_H, MOBA_DH]), ALU.mult))
                    settle()
                    did(nc.vector.tensor_tensor(m, m, head_w[:, i].unsqueeze(1).broadcast_to([P, MOBA_H, MOBA_DH]),
                                                ALU.mult), "mnorm", i, t)
            did(nc.vector.tensor_scalar(rs_v[:, 0:8], mv_[:, 0:8, 1], GN_EPS, None, ALU.add))
            rsqrt(8)
            need("dve", "ro", RET_H - 1)
            for h in range(RET_H):
                for t in range(T):
                    r = ro[:, t, h * RET_DV:(h + 1) * RET_DV]
                    did(nc.vector.tensor_scalar(r, r, mv_[:, 2 * h + t, 0:1], rs_y[:, 2 * h + t:2 * h + t + 1],
                                                ALU.subtract, ALU.mult))
            attention("moba", range(MOBA_H), out=lambda h, t: mo[:, t, h * MOBA_DH:(h + 1) * MOBA_DH], dv=MOBA_DH)
            for n in range(2):
                ahead(f"rg{n}")
                for t in range(T):
                    need("dve", "tanh", f"rg{n}", t)
                    c = slice(n * CH, (n + 1) * CH)
                    did(nc.vector.scalar_tensor_tensor(out=tanh[:, t], in0=tanh[:, t], scalar=1.0,
                                                       in1=bank[2 * n + t], op0=ALU.add, op1=ALU.mult))
                    settle()
                    did(nc.vector.scalar_tensor_tensor(out=ro[:, t, c], in0=tanh[:, t], scalar=0.5, in1=ro[:, t, c],
                                                       op0=ALU.mult, op1=ALU.mult), "ev", f"rg{n}", t)
                    note(("gated", n, t), "dve_done", counts["dve_done"])
            xT_evac("ret", slot0=8)
            ahead("ret_out0")
            ahead("ret_out1")
            for n in range(2):
                ahead(f"ga{n}")
                for t in range(T):
                    need("dve", "tanh", f"ga{n}", t)
                    c = slice(n * CH, (n + 1) * CH)
                    did(nc.vector.scalar_tensor_tensor(out=mix[:, t, c], in0=tanh[:, t], scalar=1.0,
                                                       in1=ra[:, t, c], op0=ALU.add, op1=ALU.mult),
                        "ev", f"ga{n}", t)
            xT_evac("moba", 4, slot0=8)
            ahead("moba_out0")
            ahead("moba_out1")
            for n in range(2):
                ahead(f"gb{n}")
                for t in range(T):
                    need("dve", "tanh", f"gb{n}", t)
                    c = slice(n * CH, (n + 1) * CH)
                    did(nc.vector.scalar_tensor_tensor(out=tanh[:, t], in0=tanh[:, t], scalar=1.0,
                                                       in1=ra[:, t, c], op0=ALU.add, op1=ALU.mult))
                    settle()
                    did(nc.vector.tensor_tensor(mix[:, t, c], mix[:, t, c], tanh[:, t], ALU.add),
                        "ev", f"gb{n}", t)
                    note(("mix", n, t), "dve_done", counts["dve_done"])
            xT_evac("mix", scale=0.5)

            def update(stage, alpha, label):
                for n in range(2):
                    ahead(f"{stage}{n}")
                    for t in range(T):
                        need("dve", "full", f"{stage}{n}", t)
                        xs = x[:, t, n * CH:(n + 1) * CH]
                        did(nc.vector.scalar_tensor_tensor(out=xs, in0=xs, scalar=alpha, in1=bank[2 * n + t],
                                                           op0=ALU.mult, op1=ALU.add), "ev", f"{stage}{n}", t)
                note(label, "dve_done", counts["dve_done"])

            update("w_o", 1.0, ("upd", 1))
            need("dve", "ssq1", 1, 1)
            rms_rows(1)
            xT_evac(1)
            ffn(0, 1.0)
            for l in range(2):
                if l == 0:
                    xT_evac("raw")
                if l == 1:
                    ahead("kv_down0")
                    for t in range(T):
                        need("dve", "kvsq", t)
                    did(nc.vector.tensor_scalar(rs_v[:, 0:T], stats[:, 0:T], 1.0 / KVL, RMS_EPS, ALU.mult, ALU.add))
                    rsqrt(T)
                    dve.wait_ge(aux_loaded, 48)
                    for t in range(T):
                        did(nc.vector.scalar_tensor_tensor(out=cq[:, t, 0:KVL], in0=bank[4 + t][:, 0:KVL],
                                                           scalar=rs_y[:, t:t + 1], in1=norm_c[:, 0:KVL],
                                                           op0=ALU.mult, op1=ALU.mult))
                        b = bank[4 + t][:, KVL:KVL + ROPE_D].rearrange("p (a n) -> p a n", a=2)
                        r = rope_mla[:, t].rearrange("p (a n) -> p a n", a=4)
                        z = kr[:, t].rearrange("p (c a n) -> p c a n", c=2, a=2)
                        for a in range(2):
                            did(nc.vector.tensor_tensor(z[:, 0, a], b[:, a], r[:, a], ALU.mult))
                            did(nc.vector.tensor_tensor(z[:, 1, a], b[:, 1 - a], r[:, 2 + a], ALU.mult),
                                *(("ev", "kv_down0", t) if a else ()))
                        settle()
                        did(nc.vector.tensor_tensor(kr[:, t, 0:ROPE_D], kr[:, t, 0:ROPE_D], kr[:, t, ROPE_D:], ALU.add))
                        settle()
                        did(nc.vector.tensor_copy(kr[:, t, ROPE_D:], kr[:, t, 0:ROPE_D]), "ckv", t)
                    for t in range(T):
                        need("dve", "krT", t)
                        did(nc.vector.tensor_tensor(cTl[:, 0:2, t * P:(t + 1) * P],
                                                    bank[6 + t][:, 0:2 * P].rearrange("p (k n) -> p k n", k=2),
                                                    cTh[:, 0:2, t * P:(t + 1) * P].bitcast(F32), ALU.subtract),
                            "ckvT", t)
                    for c in range(MLA_H // 2):
                        if c % 2 == 1:
                            ahead("kv_up", c // 2)
                        for t in range(T):
                            need("dve", "ks", c, t)
                            did(nc.vector.tensor_copy(
                                vv[:, t, 2 * c * VD:(2 * c + 2) * VD].rearrange("p (h n) -> p h n", h=2),
                                bank[2 * (c % 2) + t].rearrange("p (h n) -> p h n", h=2)[:, :, NOPE:]),
                                "ev", "kv_up", c, t)
                ffn(1 + 2 * l, ALPHA)
                layer_norm(2 + 4 * l)
                xT_evac(2 + 4 * l)
                if l == 0:
                    ahead("fox_f")
                    for t in range(T):
                        need("dve", "full", "fox_f", t)
                        did(nc.vector.tensor_tensor(fg[:, 0, t * FOX_H:(t + 1) * FOX_H], bank[4 + t][:, 0:FOX_H],
                                                    fox_b, ALU.add), "ev", "fox_f", t)
                    note(("fz",), "dve_done", counts["dve_done"])
                    need("dve", "fexp")
                    did(nc.vector.tensor_scalar(fg[:, 3], fg[:, 2], 1.0, None, ALU.add), "fexp1")
                    need("dve", "fln")
                    did(nc.vector.scalar_tensor_tensor(out=fg[:, 5], in0=fg[:, 0], scalar=0.0, in1=fg[:, 3],
                                                       op0=ALU.min, op1=ALU.subtract), "logf")
                    for c in range(6):
                        ahead(f"fox_in{c}")
                        if c == 1:
                            need("dve", "cum")
                            did(nc.vector.tensor_scalar(cb.rearrange("p t n -> p (t n)"), bank[6][:, 0:2 * FOX_H],
                                                        math.sqrt(FOX_DH), None, ALU.mult), "cb")
                        if c >= 4:
                            for t in range(T):
                                need("dve", "full", f"fox_in{c}", t)
                                did(nc.vector.tensor_copy(fv[:, t, (c - 4) * CH:(c - 3) * CH], bank[2 * (c % 2) + t]),
                                    "ev", f"fox_in{c}", t)
                    note(("fv",), "dve_done", counts["dve_done"])
                    attention("fox", range(FOX_H), bias=lambda h, t: cb[:, t, h:h + 1],
                              out=lambda h, t: fo[:, t, h * FOX_DH:(h + 1) * FOX_DH], dv=FOX_DH)
                    xT_evac("fox")
                    update("fox_o", ALPHA, ("upd", 3))
                else:
                    ahead("dq0")
                    for t in range(T):
                        need("dve", "cqsq", t)
                    did(nc.vector.tensor_scalar(rs_v[:, 0:T], stats[:, 0:T], 1.0 / QL, RMS_EPS, ALU.mult, ALU.add))
                    rsqrt(T)
                    dve.wait_ge(aux_loaded, 64)
                    for t in range(T):
                        did(nc.vector.scalar_tensor_tensor(out=cq[:, t], in0=bank[4 + t][:, 0:QL],
                                                           scalar=rs_y[:, t:t + 1], in1=norm_c,
                                                           op0=ALU.mult, op1=ALU.mult), "cqn", t)
                        note(("ev", "dq0", t), "dve_done", counts["dve_done"])
                    for t in range(T):
                        need("dve", "cqTh", t)
                        did(nc.vector.tensor_tensor(cTl[:, :, t * P:(t + 1) * P],
                                                    bank[6 + t][:, 0:3 * P].rearrange("p (k n) -> p k n", k=3),
                                                    cTh[:, :, t * P:(t + 1) * P].bitcast(F32), ALU.subtract),
                            "cqT", t)
                    for g in range(MLA_H // 2):
                        ahead("uq", g)
                        for t in range(T):
                            need("dve", "qn", g, t)
                            b = bank[t][:, 0:QL].rearrange("p (h n) -> p h n", h=2)[:, :, NOPE:]
                            r = rope_mla[:, t].rearrange("p (a n) -> p a n", a=4)
                            o = qs[:, t, 2 * NOPE:].rearrange("p (h n) -> p h n", h=2)
                            z = kr[:, t].rearrange("p (h n) -> p h n", h=2)
                            for a in range(2):
                                lo_, hi_ = slice(32 * a, 32 * a + 32), slice(32 - 32 * a, 64 - 32 * a)
                                rb = [r[:, q].unsqueeze(1).broadcast_to([P, 2, 32]) for q in (a, 2 + a)]
                                did(nc.vector.tensor_tensor(o[:, :, lo_], b[:, :, lo_], rb[0], ALU.mult))
                                did(nc.vector.tensor_tensor(z[:, :, lo_], b[:, :, hi_], rb[1], ALU.mult))
                            settle()
                            did(nc.vector.tensor_tensor(qs[:, t, 2 * NOPE:], qs[:, t, 2 * NOPE:], kr[:, t], ALU.add),
                                "qs", g, t)
                        attention("mla", (2 * g, 2 * g + 1), out=lambda h, t: mlo[:, t, (h % 2) * VD:(h % 2 + 1) * VD],
                                  dv=VD)
                        need("dve", "oTh", g)
                        did(nc.vector.tensor_tensor(xTl[:, 2 * g:2 * g + 2, :],
                                                    bank[0].rearrange("p (k n) -> p k n", k=2),
                                                    xTh[:, 2 * g:2 * g + 2, :].bitcast(F32), ALU.subtract), "oT", g)
                    update("mla_o", ALPHA, ("upd", 7))
                layer_norm(3 + 4 * l)
                xT_evac(3 + 4 * l)
                ffn(2 + 2 * l, ALPHA)
                need("dve", "pTh", l)
                did(nc.vector.tensor_tensor(cTl[:, 0:2, :], bank[0].rearrange("p (k n) -> p k n", k=2),
                                            cTh[:, 0:2, :].bitcast(F32), ALU.subtract), "pT", l)
                layer_norm(4 + 4 * l)
                ahead(f"ple_p{l}")
                xT_evac(4 + 4 * l)
                dve.wait_ge(aux_loaded, (32, 80)[l])
                for c in range(2):
                    ahead(f"ple_g{l}{c}")
                    cols = slice(c * CH, (c + 1) * CH)
                    for t in range(T):
                        need("dve", "full", f"ple_g{l}{c}", t)
                        if c:
                            need("dve", "ptanh", l, 0, t)
                        did(nc.vector.tensor_tensor(pz[:, t], bank[2 * c + t], pb[:, cols], ALU.add), "pz", l, c, t)
                        note(("ev", f"ple_g{l}{c}", t), "dve_done", counts["dve_done"])
                    for t in range(T):
                        need("dve", "ptanh", l, c, t)
                        need("dve", "ev", f"ple_p{l}", c, t)
                        did(nc.vector.scalar_tensor_tensor(out=tanh[:, t], in0=tanh[:, t], scalar=1.0,
                                                           in1=pp[:, t, cols], op0=ALU.add, op1=ALU.mult))
                        settle()
                        did(nc.vector.scalar_tensor_tensor(out=x[:, t, cols], in0=x[:, t, cols], scalar=ALPHA,
                                                           in1=tanh[:, t], op0=ALU.mult, op1=ALU.add))
                layer_norm(5 + 4 * l)
                if l == 0:
                    xT_evac(5)
    return found


def kernel(**inputs):
    import concourse.bacc as bacc
    from concourse.bass_utils import run_bass_kernel_spmd

    a = {n: np.asarray(v) for n, v in inputs.items()}
    arrays = {"x": a["x"].reshape(S, D)}
    for n in ("norm1_w", "w_in", "q_norm_w", "k_norm_w", "w_ret_out", "w_moba_out", "w_o", "norm2_w", "w_ffn_gate",
              "w_ffn_up", "w_ffn_down"):
        arrays[n] = a[n][0]
    arrays["p"] = a["p_2"].reshape(2, S, PLE)
    for n in ("ffn1_w_in", "ffn1_w_out", "ffn2_w_in", "ffn2_w_out", "ln_g", "ln_b", "ple_w_gate", "ple_w_proj"):
        arrays[n] = a[n + "_2"]
    arrays["ple_b"] = a["ple_b_gate_2"]
    for n in ("fox_w_in", "fox_b_f", "fox_w_o", "mla_w_dq", "mla_w_o"):
        arrays[n] = a[n + "_2"][0]
    arrays["q_norm"] = a["mla_q_norm_2"][0]
    arrays["mla_w_uq"] = a["mla_w_uq_2"].reshape(QL, MLA_H * (NOPE + ROPE_D))
    arrays["kv_w_down"], arrays["kv_norm"] = a["kv_w_down_2"], a["kv_norm_2"]
    arrays["kv_w_up"] = a["kv_w_up_2"].reshape(KVL, MLA_H * (NOPE + VD))
    arrays.update(shape_constants())
    arrays = {f"in_{n}": np.ascontiguousarray(v) for n, v in arrays.items()}

    def program(marks):
        nc = bacc.Bacc("TRN2", target_bir_lowering=False, num_devices=1)
        dram = {n[3:]: nc.dram_tensor(n, v.shape, mybir.dt.from_np(v.dtype), kind="ExternalInput").ap()
                for n, v in arrays.items()}
        dram["out"] = nc.dram_tensor("out_x", (S, D), F32, kind="ExternalOutput").ap()
        return nc, build(nc, dram, marks)

    _, marks = program({})
    nc, again = program(marks)
    assert again == marks
    r = run_bass_kernel_spmd(nc, [arrays], core_ids=[0])
    return r.results[0]["out_x"].reshape(1, S, D)
```

```python
from contextlib import ExitStack
import math

import numpy as np
import concourse.bass as bass
from concourse import mybir

P = 128
T = 2
S = T * P
D = 1024
KD = D // P
CH = 512
RING = 3
UNIT = 2048
F_HID = 2816
HB = 256
FI = F_HID // HB
RET_H, RET_DK, RET_DV = 4, 128, 256
MOBA_H, MOBA_DH = 8, 64
FOX_H, FOX_DH = 16, 64
MLA_H, NOPE, ROPE_D, VD = 16, 128, 64, 128
QL, KVL = 384, 256
PLE = 256
RMS_EPS, LN_EPS, GN_EPS = 1e-6, 1e-5, 1e-5
ALPHA = float((2 * 2) ** 0.25)
NEG = -1e30
POOL_STAGES = ("fox_in1", "fox_in3", "fox_in5", "uq", "mla_oa0", "mla_oa1")

F32 = mybir.dt.float32
F32R = mybir.dt.float32r
I32 = mybir.dt.int32
ALU = mybir.AluOpType
ACT = mybir.ActivationFunctionType
AX_X = mybir.AxisListType.X


def shape_constants():
    c = {}
    c["ident"] = np.eye(P, dtype=np.float32)
    i = np.arange(P)
    c["mask"] = np.where(i[None, :] <= i[:, None], 0.0, NEG)
    lg = np.log1p(-np.exp2(-5.0 - np.arange(RET_H)))
    dec = np.zeros((P, RET_H, 3, P))
    for h in range(RET_H):
        diff = i[None, :] - i[:, None]
        own = np.where(diff >= 0, np.exp(np.maximum(diff, 0) * lg[h]), 0.0)
        dec[:, h, 0] = own
        dec[:, h, 1] = np.exp((diff + P) * lg[h])
        dec[:, h, 2] = own
    c["decay"] = (dec * RET_DK ** -0.5).reshape(P, RET_H * 3 * P)
    pos = np.arange(S).reshape(T, P).T

    def rope(half, base):
        inv = (base ** (-np.arange(half, dtype=np.float32) / np.float32(half))).astype(np.float32)
        ang = (pos[:, :, None].astype(np.float32) * inv).astype(np.float32)
        return np.cos(ang.astype(np.float64)), np.sin(ang.astype(np.float64))

    for name, half in (("rope_ret", RET_DK // 2), ("rope_mla", ROPE_D // 2)):
        cos, sin = rope(half, np.float32(10000.0))
        c[name] = np.concatenate([cos, cos, -sin, sin], 2).reshape(P, T * 4 * half)
    c["upper"] = (i[:, None] <= i[None, :]).astype(np.float32)
    sel = np.zeros((FOX_H, FOX_H, P))
    sel[np.arange(FOX_H), np.arange(FOX_H), :] = -math.sqrt(FOX_DH)
    c["sel"] = sel.reshape(FOX_H, FOX_H * P)
    return {n: np.ascontiguousarray(a, dtype=np.float32) for n, a in c.items()}


def weight_units(w):
    units, at = [], {}

    def add(stage, kt, n, halves):
        at.setdefault(stage, []).append(len(units))
        units.append((stage, kt, n, halves))

    def dense(stage, m, k0, kts, c0, n):
        rows = m[k0 * P:(k0 + kts) * P, c0:c0 + n].rearrange("(k p) n -> p k n", p=P)
        a = (kts + 1) // 2
        if kts == 1:
            b = n // 2
            add(stage, kts, n, [((0, 1), (0, b), rows[:, :, 0:b]), ((0, 1), (b, n), rows[:, :, b:n])])
        else:
            add(stage, kts, n, [((0, a), (0, n), rows[:, 0:a, :]), ((a, kts), (0, n), rows[:, a:kts, :])])

    def chunks(stage, m, k, c0, count, n=CH, per=4, first=0):
        for c in range(count):
            for k0 in range(0, k, per):
                dense(f"{stage}{c + first}", m, k0, min(per, k - k0), c0 + c * n, n)

    def ffn(f):
        for _ in range(3 * FI):
            add(f"ffn{f}", 0, 0, None)

    w_in = w["w_in"]
    for name, c0, count in (("rq", 0, 1), ("rk", 512, 1), ("rv", 1024, 2), ("mq", 3072, 1), ("mk", 3584, 1),
                            ("mv", 4096, 1), ("rg", 2048, 2)):
        chunks(name, w_in, KD, c0, count)
    chunks("ga", w_in, KD, 4608, 2)
    chunks("gb", w_in, KD, 5632, 2)
    chunks("ret_out", w["w_ret_out"], KD, 0, 2)
    chunks("moba_out", w["w_moba_out"], 4, 0, 2)
    chunks("w_o", w["w_o"], KD, 0, 2)
    ffn(0)
    ffn(1)
    dense("fox_f", w["fox_w_in"], 0, KD, 3 * D, FOX_H)
    for c in (0, 2, 4, 1, 3, 5):
        chunks("fox_in", w["fox_w_in"], KD, c * CH, 1, first=c)
    for k0 in (0, 4):
        for c in range(2):
            dense(f"fox_o{c}", w["fox_w_o"], k0, 4, c * CH, CH)
    ffn(2)
    dense("ple_p0", w["ple_w_proj"][0], 0, 2, 0, D)
    chunks("ple_g0", w["ple_w_gate"][0], KD, 0, 2)
    chunks("kv_down", w["kv_w_down"], KD, 0, 1, n=KVL + ROPE_D)
    ffn(3)

    def kv_up(c):
        dense("kv_up", w["kv_w_up"], 0, 2, c * D, D)

    def uq(g):
        dense("uq", w["mla_w_uq"], 0, 3, g * QL, QL)

    for c in range(2):
        kv_up(c)
    chunks("dq", w["mla_w_dq"], KD, 0, 1, n=QL)
    for c in range(2, 4):
        kv_up(c)
    for g in range(7):
        uq(g)
    dense("mla_oa0", w["mla_w_o"], 0, 4, 0, CH)
    uq(7)
    dense("mla_oa0", w["mla_w_o"], 4, 4, 0, CH)
    for k0 in (0, 4):
        dense("mla_oa1", w["mla_w_o"], k0, 4, CH, CH)
    for c in range(2):
        for k0 in (8, 12):
            dense(f"mla_ob{c}", w["mla_w_o"], k0, 4, c * CH, CH)
    ffn(4)
    dense("ple_p1", w["ple_w_proj"][1], 0, 2, 0, D)
    chunks("ple_g1", w["ple_w_gate"][1], KD, 0, 2)
    return units, at


def build(nc, dram, marks):
    found = {}
    units, unit_at = weight_units(dram)
    N_UNITS = len(units)
    ffn_w = [(dram["w_ffn_gate"], dram["w_ffn_up"], dram["w_ffn_down"])]
    for l in range(2):
        for n in (1, 2):
            m = dram[f"ffn{n}_w_in"][l]
            ffn_w.append((m[:, 0:F_HID], m[:, F_HID:2 * F_HID], dram[f"ffn{n}_w_out"][l]))

    with ExitStack() as ctx:
        def sb(name, cols, dt=F32):
            return ctx.enter_context(nc.sbuf_tensor(name, [P, cols], dt))

        sems = {}

        def sem(name):
            sems[name] = ctx.enter_context(nc.semaphore(name))
            return sems[name]

        w_raw = [sb(f"w_raw{s}", UNIT) for s in range(RING)]
        w_hi = [sb(f"w_hi{s}", UNIT, F32R) for s in range(RING)]
        w_lo = [sb(f"w_lo{s}", UNIT, F32R) for s in range(RING)]
        x = sb("x", T * D)[:, :].rearrange("p (t n) -> p t n", t=T)
        xTh = sb("xTh", 16 * S, F32R)[:, :].rearrange("p (k n) -> p k n", k=16)
        fsel = xTh[0:FOX_H, 8:16, :].rearrange("p k (a n) -> p (k a) n", n=P)
        xTl = sb("xTl", 16 * S, F32R)[:, :].rearrange("p (k n) -> p k n", k=16)
        cTh = sb("cTh", 3 * S, F32R)[:, :].rearrange("p (k n) -> p k n", k=3)
        cTl = sb("cTl", 3 * S, F32R)[:, :].rearrange("p (k n) -> p k n", k=3)
        hTh = sb("hTh", 2 * S, F32R)[:, :].rearrange("p (k n) -> p k n", k=2)
        hTl = sb("hTl", 2 * S, F32R)[:, :].rearrange("p (k n) -> p k n", k=2)
        hid = sb("hid", T * HB)[:, :].rearrange("p (t n) -> p t n", t=T)
        tanh = sb("tanh", T * CH)[:, :].rearrange("p (t n) -> p t n", t=T)
        gb = sb("gb", 2 * D)[:, :].rearrange("p (a n) -> p a n", a=2)
        pin = sb("pin", T * PLE)[:, :].rearrange("p (t n) -> p t n", t=T)
        ident = sb("ident", P)[:, :]
        ident_r = sb("ident_r", P, F32R)[:, :]
        mask_r = sb("mask_r", 2 * P, F32R)[:, :]
        decay = sb("decay", RET_H * 3 * P)[:, :].rearrange("p (h n) -> p h n", h=RET_H)
        rope_ret = sb("rope_ret", T * 256)[:, :].rearrange("p (t n) -> p t n", t=T)
        rope_mla = sb("rope_mla", T * 128)[:, :].rearrange("p (t n) -> p t n", t=T)
        upper = sb("upper", P)[:, :]
        ones = sb("ones", P)[:, :]
        head_w = sb("head_w", 2 * MOBA_DH)[:, :].rearrange("p (a n) -> p a n", a=2)
        fox_b = sb("fox_b", FOX_H)[:, :]
        stats = sb("stats", 64)[:, :]
        mv_ = sb("mean_var", 2 * 16)[:, :].rearrange("p (a n) -> p a n", n=2)
        rs_v, rs_y, rs_a, rs_b = (sb(f"rsqrt_{n}", 32)[:, :] for n in "vyab")
        negmax = sb("negmax", 8)[:, :]
        psum_e = sb("exp_sum", 8)[:, :]
        rsum = sb("exp_rsum", 4)[:, :]

        ARENA = 14336
        arena = sb("arena", ARENA)[:, :]

        class Carve:
            def __init__(self):
                self.at = 0

            def __call__(self, cols):
                self.at += cols
                assert self.at <= ARENA, self.at
                return arena[:, self.at - cols:self.at]

            def tiles(self, a, n):
                return self(a * n).rearrange("p (a n) -> p a n", a=a)

        common = Carve()
        pr = common.tiles(2, 384)
        pT = common.tiles(2, 384)
        shared_end = common.at

        def carve():
            c = Carve()
            c.at = shared_end
            return c

        c1 = carve()
        rqk = c1.tiles(4, 512)
        rqT = c1.tiles(4, S)
        rkT = c1.tiles(4, S)
        rv = c1.tiles(T, D)
        mqk = c1.tiles(4, 512)
        mqT = c1.tiles(4, S)
        mkT = c1.tiles(4, S)
        mv = c1.tiles(T, 512)
        mo = mqk.rearrange("p (b t) n -> p b t n", b=2)[:, 0]
        rtmp = arena[:, 0:512]
        c1b = carve()
        ro = c1b.tiles(T, D)
        sga = c1b.tiles(T, D)
        sgb = c1b.tiles(T, D)
        normed = c1b.tiles(T, D)
        cf = carve()
        fqk = cf.tiles(T, 512)
        fqT = cf.tiles(8, S)
        fkT = cf.tiles(8, S)
        fv = cf.tiles(T, D)
        fsel_raw = cf.tiles(FOX_H, P)
        fg = cf.tiles(6, 32)
        fo = cf.tiles(T, D)
        cm = carve()
        kT = cm.tiles(MLA_H, S)
        vv = cm.tiles(T, MLA_H * VD)
        krT = cm(S)
        norm_c = cm(QL)
        cq_ = cm(2 * 512)
        cq = cq_[:, 0:T * QL].rearrange("p (t n) -> p t n", t=T)
        mlo = cq_.rearrange("p (b t n) -> p b t n", b=2, t=T)
        kr = cm.tiles(T, 2 * ROPE_D)
        qs = cm.tiles(T, 384)
        qT = cm(2 * 3 * S).rearrange("p (b k n) -> p b k n", b=2, k=3)
        cp = carve()
        pp = cp.tiles(T, D)
        pz = cp.tiles(T, CH)
        pb = cp(D)

        bank = [ctx.enter_context(nc.psum_tensor(f"bank{b}", [P, CH], F32))[:, :] for b in range(4)]
        acc_t = ctx.enter_context(nc.psum_tensor("acc", [P, T, D], F32))
        acc = acc_t[:, :, :]
        bank += [acc[:, b // 2, (b % 2) * CH:(b % 2 + 1) * CH] for b in range(4)]

        w_loaded = [sem(f"w_loaded{s}") for s in range(RING)]
        w_hi_done, w_used = sem("w_hi_done"), sem("w_used")
        w_lo_done = [sem(f"w_lo_done{s}") for s in range(RING)]
        pe_done, act_done, dve_done = sem("pe_done"), sem("act_done"), sem("dve_done")
        const_loaded, gb_loaded, out_stored = sem("const_loaded"), sem("gb_loaded"), sem("out_stored")
        p_loaded, aux_loaded, ones_set = sem("p_loaded"), sem("aux_loaded"), sem("ones_set")
        gu0_full = sem("gu0_full")
        tanh_done = sem("tanh_done")
        hid_part, hid_done = sem("hid_part"), sem("hid_done")
        hT_full = sem("hT_full")
        hT_hi, hT_lo = sem("hT_hi"), sem("hT_lo")
        acc_full = sem("acc_full")

        counts = {"pe_done": 0, "act_done": 0, "dve_done": 0}
        seen = {}

        def mark(name, *label):
            counts[name] += 1
            if label:
                assert label not in found, label
                found[label] = (name, counts[name])
            return 1

        def note(label, name, value):
            assert label not in found, label
            found[label] = (name, value)

        def need(eng, *label):
            if not marks:
                return
            name, value = marks[label]
            if seen.get((eng, name), 0) < value:
                seen[(eng, name)] = value
                ENG[eng].wait_ge(sems[name], value)

        ENG = {}
        block = ctx.enter_context(nc.Block())

        def bcast_rows(src, n):
            return src.rearrange("(a n) -> a n", a=1).broadcast_to([P, n])

        @block.sync
        def _(sp):
            def store_x(t):
                sp.dma_start(dram["out"][t * P:(t + 1) * P, :], x[:, t, :]).then_inc(out_stored, 16)

            ENG["sp"] = sp

            def load(u):
                _, kt, n, halves = units[u]
                slot = w_raw[u % RING][:, 0:kt * n].rearrange("p (k n) -> p k n", k=kt)
                if u >= RING:
                    sp.wait_ge(w_lo_done[u % RING], u // RING)
                for (k0, k1), (n0, n1), src in halves:
                    sp.dma_start(slot[:, k0:k1, n0:n1], src).then_inc(w_loaded[u % RING], 16)

            def load_ffn(f):
                u0 = unit_at[f"ffn{f}"][0]
                gate, up, down = ffn_w[f]

                def gate_up(u_slot, need_lo, half, i):
                    if need_lo is not None:
                        sp.wait_ge(w_lo_done[u_slot], need_lo)
                    slot = w_raw[u_slot][:, :].rearrange("p (k g n) -> p g k n", k=4, g=2)
                    for g, m in enumerate((gate, up)):
                        src = m[half * 512:(half + 1) * 512, :].rearrange("(k p) n -> p k n", p=P)
                        sp.dma_start(slot[:, g], src[:, :, bass.ds(i * HB, HB)]).then_inc(w_loaded[u_slot], 16)

                def down_rows(u_slot, need_lo, i):
                    sp.wait_ge(w_lo_done[u_slot], need_lo)
                    slot = w_raw[u_slot][:, :].rearrange("p (k n) -> p k n", k=2)
                    for k in range(2):
                        sp.dma_start(slot[:, k], down[bass.ds(i * HB + k * P, P), :]).then_inc(w_loaded[u_slot], 16)

                gate_up(u0 % RING, u0 // RING, 0, 0)
                gate_up((u0 + 1) % RING, (u0 + 1) // RING, 1, 0)
                with sp.Fori(1, FI) as i:
                    gate_up((u0 + 2) % RING, i + (u0 - 1) // RING, 0, i)
                    gate_up(u0 % RING, i + u0 // RING, 1, i)
                    down_rows((u0 + 1) % RING, i + (u0 + 1) // RING, i - 1)
                u = u0 + 3 * FI - 1
                down_rows(u % RING, u // RING, FI - 1)

            u = 0
            while u < N_UNITS:
                if units[u][3] is None:
                    load_ffn(int(units[u][0][3:]))
                    u += 3 * FI
                else:
                    load(u)
                    u += 1
            for t in range(T):
                need("sp", "norm", 9, t, 1)
                store_x(t)
            sp.wait_ge(out_stored, 16 * T)

        norm_src = [(dram["norm1_w"], None), (dram["norm2_w"], None)] + \
                   [(dram["ln_g"][l, j], dram["ln_b"][l, j]) for l in range(2) for j in range(4)]

        @block.gpsimd
        def _(pool):
            ENG["pool"] = pool
            pool.memset(ones, 1.0).then_inc(ones_set, 1)
            for u, unit in enumerate(units):
                if unit[0] in POOL_STAGES:
                    cols, slot = unit[1] * unit[2], u % RING
                    pool.wait_ge(w_hi_done, u + 1)
                    pool.tensor_tensor(w_lo[slot][:, 0:cols], w_raw[slot][:, 0:cols],
                                       w_hi[slot][:, 0:cols].bitcast(F32), ALU.subtract).then_inc(w_lo_done[slot], 1)

        CONSTS = [("ident", ident), ("x", x), ("head_q", head_w[:, 0]), ("head_k", head_w[:, 1]),
                  ("rope_ret", rope_ret), ("mask", pr[:, 0, 0:P]), ("decay", decay), ("rope_mla", rope_mla),
                  ("upper", upper), ("fox_b", fox_b)]
        const_src = {n: dram[n] for n in ("ident", "mask", "upper")}
        const_src["x"] = dram["x"].rearrange("(t p) n -> p t n", p=P)
        const_src["decay"] = dram["decay"].rearrange("p (h n) -> p h n", h=RET_H)
        for n in ("rope_ret", "rope_mla"):
            const_src[n] = dram[n].rearrange("p (t n) -> p t n", t=T)
        const_src["head_q"] = bcast_rows(dram["q_norm_w"], MOBA_DH)
        const_src["head_k"] = bcast_rows(dram["k_norm_w"], MOBA_DH)
        const_src["fox_b"] = bcast_rows(dram["fox_b_f"], FOX_H)
        N_CONST = 16 * len(CONSTS)

        def site_ready(site, t, q):
            return {"ret": ("ev", f"rg{q}", t), "moba": ("o", "moba", MOBA_H - 1), "mix": ("ev", f"moba_out{q}", t),
                    "fox": ("o", "fox", 8 * q + 7), "raw": ("ffn_out", 0, t)}.get(site, ("norm", site, t, q))

        @block.tensor
        def _(pe):
            ENG["pe"] = pe
            freed = {b: None for b in range(8)}

            def take(b, label):
                if freed[b]:
                    need("pe", *freed[b])
                freed[b] = label

            def transposes(b, free, label, pairs):
                take(b, free)
                for c, src in pairs:
                    mm = pe.matmul(bank[b][:, c:c + P], src, ident, is_transpose=True, start=True, stop=True)
                mm.then_inc(pe_done, mark("pe_done", *label))

            def mm3(out, ah, al, bh, bl, first, last):
                pe.matmul(out, ah, bh, start=first, stop=False)
                pe.matmul(out, ah, bl, start=False, stop=False)
                return pe.matmul(out, al, bh, start=False, stop=last)

            class Chunk:

                def __init__(self, stage, banks, src=None, slot0=0, half=None, ready=None):
                    self.us = unit_at[stage] if half is None else [unit_at[stage][half[0]]]
                    self.name = (stage,) if half is None else (stage, half[0] * 2 + half[1])
                    self.ah, self.al = src or (xTh, xTl)
                    self.banks, self.slot0, self.half, self.ready = banks, slot0, half, ready
                    self.kts = [units[u][1] for u in self.us]

                def run(self, *which):
                    last = len(self.us) - 1
                    for t in range(T):
                        if which[0] == 0:
                            take(self.banks[t], ("ev", *self.name, t))
                        for w in which:
                            u, kt = self.us[w], self.kts[w]
                            n = units[u][2]
                            if t == 0:
                                pe.wait_ge(w_lo_done[u % RING], u // RING + 1)
                            wh, wl = (m[u % RING][:, 0:kt * n].rearrange("p (k n) -> p k n", k=kt)
                                      for m in (w_hi, w_lo))
                            cols = slice(0, n) if self.half is None else slice(self.half[1] * CH, (self.half[1] + 1) * CH)
                            for j in range(kt):
                                k = sum(self.kts[:w]) + j
                                if self.ready is not None:
                                    need("pe", "xT", self.ready, t, k // 4)
                                a, tok = self.slot0 + k, slice(t * P, (t + 1) * P)
                                mm = mm3(bank[self.banks[t]][:, 0:cols.stop - cols.start], self.ah[:, a, tok],
                                         self.al[:, a, tok], wh[:, j, cols], wl[:, j, cols],
                                         w == 0 and j == 0, w == last and j == kt - 1)
                            if t == 0 and w == last:
                                mm.then_inc(pe_done, mark("pe_done", "full", *self.name, 0))
                            if t == 1 and (self.half is None or self.half[1] == 1):
                                mm.then_inc(w_used, 1)
                                if w == last:
                                    note(("full", *self.name, 1), "w_used", u + 1)
                            elif t == 1:
                                mm.then_inc(pe_done, mark("pe_done", "full", *self.name, 1))

            def chunk(stage, banks, src=None, slot0=0, half=None, ready=None):
                c = Chunk(stage, banks, src, slot0, half, ready)
                c.run(*range(len(c.us)))

            def unit_steps(stage, banks, **kw):
                c = Chunk(stage, banks, **kw)
                return [(lambda w=w: c.run(w)) for w in range(len(c.us))]

            def to_xT(site, src, qs_=(0, 1), b0=0):
                for t in range(T):
                    for q in qs_:
                        need("pe", *site_ready(site, t, q))
                        transposes((b0 + t * len(qs_) + q - qs_[0]) % 4, ("xT", site, t, q), ("T", site, t, q),
                                   [(j * P, src[:, t, (4 * q + j) * P:(4 * q + j + 1) * P]) for j in range(4)])

            def need_xT(site, qs_=(0, 1)):
                for t in range(T):
                    for q in qs_:
                        need("pe", "xT", site, t, q)

            def ffn(f, site):
                u0 = unit_at[f"ffn{f}"][0]
                g0 = f * FI
                assert 3 * FI == len(unit_at[f"ffn{f}"])

                def gate_up(slot, split, half):
                    pe.wait_ge(w_lo_done[slot], split)
                    wh, wl = (w[slot][:, :].rearrange("p (k n) -> p k n", k=4) for w in (w_hi, w_lo))
                    for t in range(T):
                        for j in range(4):
                            k, tok = half * 4 + j, slice(t * P, (t + 1) * P)
                            mm = mm3(bank[t], xTh[:, k, tok], xTl[:, k, tok], wh[:, j], wl[:, j], k == 0, k == 7)
                            if k == 7 and t == 0:
                                mm.then_inc(gu0_full, 1)
                    mm.then_inc(w_used, 1)

                def first_gate_up():
                    for t in range(T):
                        for half in range(2):
                            s = (u0 + half) % RING
                            need("pe", "xT", site, t, half)
                            if t == 0:
                                pe.wait_ge(w_lo_done[s], (u0 + half) // RING + 1)
                            wh, wl = (w[s][:, :].rearrange("p (k n) -> p k n", k=4) for w in (w_hi, w_lo))
                            for j in range(4):
                                k, tok = half * 4 + j, slice(t * P, (t + 1) * P)
                                mm = mm3(bank[t], xTh[:, k, tok], xTl[:, k, tok], wh[:, j], wl[:, j], k == 0, k == 7)
                            if t == 1:
                                mm.then_inc(w_used, 1)
                            elif half == 1:
                                mm.then_inc(gu0_full, 1)

                def transpose_hid(i):
                    pe.wait_ge(hid_done, (i + (g0 + 1)) * T)
                    for k in range(2):
                        for t in range(T):
                            mm = pe.matmul(bank[2 + k][:, t * P:(t + 1) * P], hid[:, t, k * P:(k + 1) * P],
                                           ident, is_transpose=True, start=True, stop=True)
                        mm.then_inc(hT_full, 1)

                def down(slot, split, i, first, last):
                    pe.wait_ge(w_lo_done[slot], split)
                    pe.wait_ge(hT_lo, (i + (g0 + 1)) * 2)
                    wh, wl = (w[slot][:, :].rearrange("p (k n) -> p k n", k=2) for w in (w_hi, w_lo))
                    for t in range(T):
                        tok = slice(t * P, (t + 1) * P)
                        for n in range(2):
                            cols = slice(n * CH, (n + 1) * CH)
                            for k in range(2):
                                mm = mm3(acc[:, t, cols], hTh[:, k, tok], hTl[:, k, tok], wh[:, k, cols],
                                         wl[:, k, cols], first and k == 0, last and k == 1)
                            if last and (t, n) != (1, 1):
                                mm.then_inc(pe_done, mark("pe_done", "ffn_full", f, t, n))
                    mm.then_inc(w_used, 1)

                for b in range(8):
                    take(b, ("ffn_out", f, 1))
                first_gate_up()
                transpose_hid(0)
                gate_up((u0 + 2) % RING, (u0 + 2) // RING + 1, 0)
                gate_up(u0 % RING, u0 // RING + 2, 1)
                down((u0 + 1) % RING, (u0 + 1) // RING + 2, 0, True, False)
                transpose_hid(1)
                with pe.Fori(2, FI) as i:
                    gate_up((u0 + 2) % RING, i + ((u0 - 1) // RING + 1), 0)
                    gate_up(u0 % RING, i + (u0 // RING + 1), 1)
                    down((u0 + 1) % RING, i + ((u0 + 1) // RING + 1), i - 1, False, False)
                    transpose_hid(i)
                u = u0 + 3 * FI - 1
                down(u % RING, u // RING + 1, FI - 1, False, True)
                note(("ffn_full", f, 1, 1), "w_used", u + 1)

            def nothing():
                pass

            def attention(name, heads, qk, v, dv, fill):
                def scores(h):
                    take(4 + h % 2, ("exp", name, h))
                    b = bank[4 + h % 2]
                    for t in range(T):
                        c0 = t * P
                        out = b[:, c0:c0 + (t + 1) * P]
                        pe.matmul(out, ident_r, mask_r[:, P - c0:], start=True, stop=False)
                        *more, (q, k, _) = qk(h, t)
                        for a, b_, o in more:
                            pe.matmul(out if o is None else b[:, c0 + o * P:c0 + (o + 1) * P], a, b_,
                                      start=False, stop=False)
                        mm = pe.matmul(out, q, k, start=False, stop=True)
                    mm.then_inc(pe_done, mark("pe_done", "S", name, h))

                def turn(h):
                    need("pe", "exp", name, h)
                    transposes(6, ("pT", name, h), ("PT", name, h),
                               [(c * P, pr[:, h % 2, c * P:(c + 1) * P]) for c in range(3)])

                def weigh(h):
                    take(7, ("o", name, h))
                    need("pe", "pT", name, h)
                    b, p = bank[7], pT[:, h % 2]
                    pe.matmul(b[:, 0:dv], p[:, 0:P], v(h, 0), start=True, stop=True)
                    pe.matmul(b[:, dv:2 * dv], p[:, P:2 * P], v(h, 0), start=True, stop=False)
                    pe.matmul(b[:, dv:2 * dv], p[:, 2 * P:3 * P], v(h, 1), start=False, stop=True)\
                        .then_inc(pe_done, mark("pe_done", "PV", name, h))

                for s in range(heads + 2):
                    if s < heads:
                        scores(s)
                    if 1 <= s <= heads:
                        turn(s - 1)
                    if s >= 2:
                        weigh(s - 2)
                    for work in fill.get(s, ()):
                        work()

            def tok(t):
                return slice(t * P, (t + 1) * P)

            def pair(h):
                return slice(64 * (h % 2), 64 * (h % 2) + 64)

            def turn_qk(name, src):
                for i in range(2):
                    for t in range(T):
                        need("pe", name, i, t)
                        transposes(4 + 2 * i + t, ("qkT", name, i, t), ("qkTf", name, i, t),
                                   [(j * P, src[:, 2 * i + t, j * P:(j + 1) * P]) for j in range(4)])

            pe.wait_ge(const_loaded, N_CONST)
            to_xT(0, normed)
            chunk("rq0", (0, 1), ready=0)
            chunk("rk0", (2, 3))
            chunk("rv0", (0, 1))
            chunk("rv1", (2, 3))
            turn_qk("rot", rqk)
            for h, stage in enumerate(("mq0", "mk0", "mv0", "rg0", "rg1")):
                if h == 0:
                    chunk(stage, (0, 1))
                    for i in range(2):
                        for t in range(T):
                            need("pe", "qkT", "rot", i, t)
                if h < RET_H:
                    take(4 + h % 2, ("decayed", h))
                    b = bank[4 + h % 2]
                    pe.matmul(b[:, 0:S], rkT[:, h, 0:P], rqT[:, h, :], start=True, stop=True)
                    pe.matmul(b[:, S:S + P], rkT[:, h, P:S], rqT[:, h, P:S], start=True, stop=True)\
                        .then_inc(pe_done, mark("pe_done", "RS", h))
                if h >= 1:
                    g = h - 1
                    take(6 + g % 2, ("ro", g))
                    need("pe", "decayed", g)
                    need("pe", "ev", "rv1", 1)
                    b, s = bank[6 + g % 2], pT[:, g % 2]
                    v = [rv[:, t, g * RET_DV:(g + 1) * RET_DV] for t in range(T)]
                    pe.matmul(b[:, 0:RET_DV], s[:, 0:P], v[0], start=True, stop=True)
                    pe.matmul(b[:, RET_DV:], s[:, P:2 * P], v[0], start=True, stop=False)
                    pe.matmul(b[:, RET_DV:], s[:, 2 * P:3 * P], v[1], start=False, stop=True)\
                        .then_inc(pe_done, mark("pe_done", "RO", g))
                if h:
                    chunk(stage, ((0, 1), (2, 3))[h % 2])
            turn_qk("mnorm", mqk)
            ga0, ga1, gb0, gb1 = (unit_steps(f"{n}{c}", ((2, 3), (0, 1))[c]) for n in ("ga", "gb") for c in range(2))
            ga0[0]()
            for i in range(2):
                for t in range(T):
                    need("pe", "qkT", "mnorm", i, t)
            need("pe", "ev", "mv0", 1)
            attention("moba", MOBA_H, lambda h, t: [(mqT[pair(h), h // 2, tok(t)], mkT[pair(h), h // 2, 0:(t + 1) * P], None)],
                      lambda h, t: mv[:, t, h * MOBA_DH:(h + 1) * MOBA_DH], MOBA_DH,
                      {0: [ga0[1]], 1: [ga1[0]], 2: [ga1[1]], 4: [gb0[0]], 5: [gb0[1]], 7: [gb1[0]], 8: [gb1[1]]})
            to_xT("ret", ro)
            need_xT("ret")
            chunk("ret_out0", (0, 1), slot0=8)
            to_xT("moba", mo, (0,), b0=2)
            chunk("ret_out1", (2, 3), slot0=8)
            need_xT("moba", (0,))
            chunk("moba_out0", (0, 1))
            chunk("moba_out1", (2, 3))
            to_xT("mix", sga)
            chunk("w_o0", (0, 1), slot0=8, ready="mix")
            chunk("w_o1", (2, 3), slot0=8)
            to_xT(1, normed)
            ffn(0, 1)
            for l in range(2):
                if l == 0:
                    to_xT("raw", x)
                if l == 1:
                    chunk("kv_down0", (4, 5), ready=5)
                ffn(1 + 2 * l, ("raw", 5)[l])

                def kv(gs):
                    for g in (*gs, gs[-1] + 1):
                        if g in gs:
                            chunk("kv_up", ((0, 1), (2, 3))[g % 2], src=(cTh, cTl), half=(g // 2, g % 2))
                        if g - 1 in gs:
                            for t in range(T):
                                need("pe", "ks", g - 1, t)
                            transposes(4 + g % 2, ("kT", g - 1), ("kTf", g - 1),
                                       [(j * S + t * P, qs[:, t, j * P:(j + 1) * P]) for t in range(T) for j in range(2)])

                if l == 1:
                    for t in range(T):
                        need("pe", "ckv", t)
                        take(6 + t, ("ckvT", t))
                        for c in range(3):
                            src = cq[:, t, c * P:(c + 1) * P] if c < 2 else kr[:, t, :]
                            mm = pe.matmul(bank[6 + t][:, c * P:(c + 1) * P], src, ident, is_transpose=True,
                                           start=True, stop=True)
                        mm.then_inc(pe_done, mark("pe_done", "ckvTf", t))
                    for t in range(T):
                        need("pe", "ckvT", t)
                    kv(range(4))
                to_xT(2 + 4 * l, x)
                if l == 0:
                    need_xT(2)
                    chunk("fox_f", (4, 5))
                    chunk("fox_in0", (0, 1))
                    chunk("fox_in2", (2, 3))
                    need("pe", "logf")
                    pe.wait_ge(ones_set, 1)
                    ls = [fg[:, 5, t * FOX_H:(t + 1) * FOX_H] for t in range(T)]
                    take(7, ("cum",))
                    pe.matmul(bank[7][0:FOX_H, 0:P], ls[0], upper, start=True, stop=True)
                    pe.matmul(bank[7][0:FOX_H, P:S], ls[0], ones, start=True, stop=False)
                    pe.matmul(bank[7][0:FOX_H, P:S], ls[1], upper, start=False, stop=True)\
                        .then_inc(pe_done, mark("pe_done", "cumf"))

                    def turn_fox(c, b):
                        for t in range(T):
                            need("pe", "ev", f"fox_in{c}", t)
                            transposes(b + t, ("fT", c, t), ("fTf", c, t),
                                       [(j * P, fqk[:, t, j * P:(j + 1) * P]) for j in range(4)])

                    turn_fox(0, 4)
                    fox_4 = unit_steps("fox_in4", (0, 1))
                    fox_4[0]()
                    turn_fox(2, 6)
                    fox_4[1]()
                    for c in (0, 2):
                        for t in range(T):
                            need("pe", "fT", c, t)
                    need("pe", "cum")
                    need("pe", "ev", "fox_in4", 1)
                    need("pe", "fsel")

                    def fox_qk(h, t):
                        keys = slice(0, (t + 1) * P)
                        out = []
                        for c in (cTh, cTl):
                            out.append((fsel[:, h, :], c[0:FOX_H, 0, keys], None))
                        for c in (cTh, cTl):
                            for o in range(t + 1):
                                out.append((c[0:FOX_H, 1, tok(t)], fsel[:, h, :], o))
                        out.append((fqT[pair(h), h // 2, tok(t)], fkT[pair(h), h // 2, keys], None))
                        return out

                    def ready_b(c):
                        for t in range(T):
                            need("pe", "fT", c, t)

                    f1, f3, f5 = (unit_steps(f"fox_in{c}", b) for c, b in ((1, (2, 3)), (3, (0, 1)), (5, (2, 3))))
                    o0, o1 = (unit_steps(f"fox_o{c}", b) for c, b in ((0, (0, 1)), (1, (2, 3))))
                    attention("fox", FOX_H, fox_qk, lambda h, t: fv[:, t, h * FOX_DH:(h + 1) * FOX_DH], FOX_DH,
                              {0: [f1[0]], 1: [f1[1]], 2: [f3[0]], 3: [lambda: turn_fox(1, 2), f3[1]], 4: [f5[0]],
                               5: [lambda: turn_fox(3, 0), f5[1]],
                               7: [lambda: ready_b(1), lambda: ready_b(3), lambda: need("pe", "ev", "fox_in5", 1)],
                               11: [lambda: to_xT("fox", fo, (0,), b0=2)],
                               13: [lambda: need_xT("fox", (0,)), o0[0]], 15: [o1[0]]})
                    for t in range(T):
                        need("pe", *site_ready("fox", t, 1))
                        transposes(4 + t, ("xT", "fox", t, 1), ("T", "fox", t, 1),
                                   [(j * P, fo[:, t, (4 + j) * P:(5 + j) * P]) for j in range(4)])
                    need_xT("fox", (1,))
                    o0[1]()
                    o1[1]()
                else:
                    chunk("dq0", (2, 3), ready=6)
                    kv(range(4, 8))
                    for t in range(T):
                        need("pe", "cqn", t)
                        take(6 + t, ("cqT", t))
                        for c in range(3):
                            mm = pe.matmul(bank[6 + t][:, c * P:(c + 1) * P], cq[:, t, c * P:(c + 1) * P], ident,
                                           is_transpose=True, start=True, stop=True)
                        mm.then_inc(pe_done, mark("pe_done", "cqTf", t))
                    for t in range(T):
                        need("pe", "cqT", t)
                    need("pe", "kT", 7)

                    def uq(g):
                        u = unit_at["uq"][g]
                        pe.wait_ge(w_lo_done[u % RING], u // RING + 1)
                        wh, wl = (w[u % RING][:, 0:3 * QL].rearrange("p (k n) -> p k n", k=3) for w in (w_hi, w_lo))
                        for t in range(T):
                            take(t, ("qs", g, t))
                            for j in range(3):
                                mm = mm3(bank[t][:, 0:QL], cTh[:, j, tok(t)], cTl[:, j, tok(t)], wh[:, j],
                                         wl[:, j], j == 0, j == 2)
                            if t == 0:
                                mm.then_inc(pe_done, mark("pe_done", "qf", g, 0))
                        mm.then_inc(w_used, 1)
                        note(("qf", g, 1), "w_used", u + 1)

                    def turn_q(g):
                        for t in range(T):
                            need("pe", "qs", g, t)
                            transposes(t, ("qT", g, t), ("qTf", g, t),
                                       [(j * P, qs[:, t, j * P:(j + 1) * P]) for j in range(3)])

                    def turn_o(g):
                        need("pe", "o", "mla", 2 * g + 1)
                        transposes(6, ("oT", g), ("oTf", g),
                                   [(j * S + t * P, mlo[:, g % 2, t, j * VD:(j + 1) * VD])
                                    for t in range(T) for j in range(2)])

                    def mla_qk(h, t):
                        g, keys = h // 2, slice(0, (t + 1) * P)
                        need("pe", "qT", g, 0)
                        need("pe", "qT", g, 1)
                        return [(qT[:, g % 2, h % 2, tok(t)], kT[:, h, keys], None),
                                (qT[pair(h), g % 2, 2, tok(t)], krT[pair(h), keys], None)]

                    uq(0)
                    turn_q(0)
                    fill = {s: [] for s in range(MLA_H + 2)}
                    for g in range(1, 8):
                        fill[2 * g - 2].append(lambda g=g: uq(g))
                        fill[2 * g - 1].append(lambda g=g: turn_q(g))
                    for g in range(7):
                        fill[2 * g + 4].append(lambda g=g: turn_o(g))
                    oa = [unit_steps(f"mla_oa{c}", (2, 3)) for c in range(2)]
                    fill[11] += [lambda: [need("pe", "oT", g) for g in range(4)], oa[0][0]]
                    fill[13].append(oa[0][1])
                    fill[14].append(oa[1][0])
                    fill[15].append(oa[1][1])
                    attention("mla", MLA_H, mla_qk, lambda h, t: vv[:, t, h * VD:(h + 1) * VD], VD, fill)
                    turn_o(7)
                    for g in range(4, 8):
                        need("pe", "oT", g)
                    chunk("mla_ob0", (0, 1), slot0=8)
                    chunk("mla_ob1", (2, 3), slot0=8)
                to_xT(3 + 4 * l, x)
                pe.wait_ge(p_loaded, 16 * (l + 1))
                transposes(4, ("pT", l), ("pTf", l),
                           [(j * S + t * P, pin[:, t, j * P:(j + 1) * P]) for t in range(T) for j in range(2)])
                ffn(2 + 2 * l, 3 + 4 * l)
                need("pe", "pT", l)
                for c in range(2):
                    chunk(f"ple_p{l}", ((4, 5), (6, 7))[c], src=(cTh, cTl), half=(0, c))
                to_xT(4 + 4 * l, x)
                chunk(f"ple_g{l}0", (0, 1), ready=4 + 4 * l)
                chunk(f"ple_g{l}1", (2, 3))
                if l == 0:
                    to_xT(5, x)

        @block.scalar
        def _(act):
            ENG["act"] = act
            for name, dst in CONSTS:
                act.dma_start(dst, const_src[name]).then_inc(const_loaded, 16)
            split = [0]

            def split_to(n):
                while split[0] < min(n, N_UNITS):
                    u = split[0]
                    cols = units[u][1] * units[u][2] or UNIT
                    act.wait_ge(w_loaded[u % RING], 32 * (u // RING + 1))
                    if u >= RING:
                        act.wait_ge(w_used, u - RING + 1)
                    nc.scalar.activation(w_hi[u % RING][:, 0:cols], w_raw[u % RING][:, 0:cols], ACT.Copy)\
                        .then_inc(w_hi_done, 1)
                    split[0] += 1

            def ahead(stage, part=None):
                us = unit_at[stage]
                split_to((us[-1] if part is None else us[part]) + RING)

            def go(label, out, in_, func=ACT.Copy, **kw):
                nc.scalar.activation(out, in_, func, **kw).then_inc(act_done, mark("act_done", *label))

            def xT_evac(site, qs_=(0, 1), slot0=0, b0=0, scale=1.0):
                for t in range(T):
                    for q in qs_:
                        need("act", "T", site, t, q)
                        b = (b0 + t * len(qs_) + q - qs_[0]) % 4 if b0 < 4 else b0 + t
                        go(("xTh", site, t, q), xTh[:, slot0 + 4 * q:slot0 + 4 * q + 4, t * P:(t + 1) * P],
                           bank[b].rearrange("p (k n) -> p k n", k=4), scale=scale)

            def load_norm(site):
                if site:
                    need("act", "norm", site - 1, 1, 1)
                g, b = norm_src[site]
                act.dma_start(gb[:, 0, :], bcast_rows(g, D)).then_inc(gb_loaded, 16)
                act.dma_start(gb[:, 1, :], bcast_rows(b if b is not None else g, D)).then_inc(gb_loaded, 16)

            def load_p(l):
                act.dma_start(pin, dram["p"][l].rearrange("(t p) n -> p t n", p=P)).then_inc(p_loaded, 16)

            def ffn(f):
                u0 = unit_at[f"ffn{f}"][0]
                g0 = f * FI

                def split_unit(slot, loaded, used):
                    act.wait_ge(w_loaded[slot], loaded)
                    act.wait_ge(w_used, used)
                    nc.scalar.activation(w_hi[slot][:, :], w_raw[slot][:, :], ACT.Copy).then_inc(w_hi_done, 1)

                def half_tanh(i, last_used):
                    act.wait_ge(gu0_full, i + (g0 + 1))
                    nc.scalar.activation(tanh[:, 0, 0:HB], bank[0][:, 0:HB], ACT.Tanh, scale=0.5)\
                        .then_inc(tanh_done, 1)
                    act.wait_ge(w_used, last_used)
                    nc.scalar.activation(tanh[:, 1, 0:HB], bank[1][:, 0:HB], ACT.Tanh, scale=0.5)\
                        .then_inc(tanh_done, 1)

                def hT_round(i):
                    for k in range(2):
                        act.wait_ge(hT_full, i * 2 + (2 * g0 + k + 1))
                        nc.scalar.activation(hTh[:, k, :], bank[2 + k][:, 0:S], ACT.Copy).then_inc(hT_hi, 1)

                split_to(u0 + 3)
                half_tanh(0, u0 + 2)
                split_to(u0 + 4)
                hT_round(0)
                with act.Fori(1, FI) as i:
                    s, n = (u0 + 4) % RING, (u0 + 4) // RING
                    split_unit(s, i * 32 + 32 * n, i * 3 + (u0 - 1))
                    half_tanh(i, i * 3 + (u0 + 1))
                    s, n = (u0 + 5) % RING, (u0 + 5) // RING
                    split_unit(s, i * 32 + 32 * n, i * 3 + u0)
                    s, n = (u0 + 6) % RING, (u0 + 6) // RING
                    split_unit(s, i * 32 + 32 * n, i * 3 + (u0 + 1))
                    hT_round(i)
                split[0] = u0 + 3 * FI + 1
                split_to(u0 + 3 * FI + 2)

            def attention(name, heads, scale, fill):
                def exps(h):
                    need("act", "soft", name, h)
                    s = 2 * (h % 4)
                    b = bank[4 + h % 2]
                    for t in range(T):
                        c = slice(0, P) if t == 0 else slice(P, 3 * P)
                        go(("exp", name, h) if t else (), pr[:, h % 2, c], b[:, c], ACT.Exp,
                           bias=negmax[:, s + t:s + t + 1], scale=scale, accum_out=psum_e[:, s + t:s + t + 1])

                def turned(h):
                    need("act", "PT", name, h)
                    go(("pT", name, h), pT[:, h % 2], bank[6][:, 0:3 * P])

                for s in range(heads + 3):
                    for work in fill.get(s - 1, ()):
                        work()
                    if s < heads:
                        exps(s)
                    if 1 <= s <= heads:
                        turned(s - 1)

            def copy_chunk(stage, banks, dst):
                for t in range(T):
                    need("act", "full", stage, t)
                    go(("ev", stage, t), dst(t), bank[banks[t]])

            load_norm(0)
            load_p(0)
            split_to(3)
            act.wait_ge(const_loaded, N_CONST)
            go((), ident_r, ident)
            go((), mask_r[:, 0:P], pr[:, 0, 0:P], scale=0.0)
            go(("mask_r",), mask_r[:, P:], pr[:, 0, 0:P])
            xT_evac(0)
            load_norm(1)
            ahead("rq0")
            ahead("rk0")
            for n, stage in enumerate(("rv0", "rv1")):
                ahead(stage)
                copy_chunk(stage, (2 * n, 2 * n + 1), lambda t: rv[:, t, n * CH:(n + 1) * CH])
            for i in range(2):
                for t in range(T):
                    need("act", "qkTf", "rot", i, t)
                    go(("qkT", "rot", i, t), (rqT, rkT)[i][:, :, t * P:(t + 1) * P],
                       bank[4 + 2 * i + t].rearrange("p (k n) -> p k n", k=4))
            for n, stage in enumerate(("mq0", "mk0")):
                ahead(stage)
                for t in range(T):
                    need("act", "full", stage, t)
                    go(("ev", stage, t), mqk[:, 2 * n + t], bank[2 * n + t])
                    act.wait_ge(act_done, counts["act_done"])
                    if n * T + t:
                        need("act", "mss", n * T + t - 1)
                    go(("msq", n, t), tanh[:, 0], mqk[:, 2 * n + t], ACT.Square)

            def keep_ro(h):
                need("act", "rstats", h)
                go(("ro", h), ro[:, :, h * RET_DV:(h + 1) * RET_DV],
                   bank[6 + h % 2].rearrange("p (t n) -> p t n", t=T))

            keep_ro(0)
            ahead("mv0")
            copy_chunk("mv0", (0, 1), lambda t: mv[:, t])
            keep_ro(1)

            def gate(stage, banks, out, *free):
                ahead(stage)
                for t in range(T):
                    need("act", "full", stage, t)
                    if free:
                        need("act", *free, t)
                    go(("tanh", stage, t), out(t), bank[banks[t]], ACT.Tanh, scale=0.5)

            gate("rg0", (2, 3), lambda t: tanh[:, t])
            keep_ro(2)
            keep_ro(3)
            gate("rg1", (0, 1), lambda t: tanh[:, t], "ev", "rg0")
            for i in range(2):
                for t in range(T):
                    need("act", "qkTf", "mnorm", i, t)
                    go(("qkT", "mnorm", i, t), (mqT, mkT)[i][:, :, t * P:(t + 1) * P],
                       bank[4 + 2 * i + t].rearrange("p (k n) -> p k n", k=4))

            def keep_gate(n, c):
                stage, dst = f"{n}{c}", {"ga": sga, "gb": sgb}[n]
                ahead(stage)
                for t in range(T):
                    need("act", "full", stage, t)
                    go(("ev", stage, t), dst[:, t, c * CH:(c + 1) * CH], bank[(2 - 2 * c) + t], ACT.Tanh, scale=0.5)

            split_to(unit_at["ga0"][0] + RING)
            attention("moba", MOBA_H, MOBA_DH ** -0.5,
                      {0: [lambda: keep_gate("ga", 0)], 1: [lambda: split_to(unit_at["ga1"][0] + RING)],
                       2: [lambda: keep_gate("ga", 1)], 4: [lambda: split_to(unit_at["gb0"][0] + RING)],
                       5: [lambda: keep_gate("gb", 0)], 7: [lambda: split_to(unit_at["gb1"][0] + RING)],
                       8: [lambda: keep_gate("gb", 1)]})
            xT_evac("ret", slot0=8)
            xT_evac("moba", (0,), b0=2)
            for stage in ("ret_out0", "ret_out1", "moba_out0", "moba_out1"):
                ahead(stage)
            xT_evac("mix", slot0=8, scale=0.5)
            ahead("w_o0")
            ahead("w_o1")
            xT_evac(1)
            load_norm(2)
            ffn(0)
            for l in range(2):
                if l == 0:
                    xT_evac("raw")
                    act.dma_start(fsel_raw[0:FOX_H], dram["sel"].rearrange("p (h n) -> p h n", h=FOX_H))\
                        .then_inc(aux_loaded, 16)
                if l == 1:
                    ahead("kv_down0")
                    for t in range(T):
                        need("act", "full", "kv_down0", t)
                        go(("kvsq", t), tanh[:, t, 0:KVL], bank[4 + t][:, 0:KVL], ACT.Square,
                           accum_out=stats[:, t:t + 1])
                ffn(1 + 2 * l)

                def kv(gs):
                    for g in (*gs, gs[-1] + 1):
                        if g in gs:
                            if g % 2 == 1:
                                ahead("kv_up", g // 2)
                            for t in range(T):
                                need("act", "full", "kv_up", g, t)
                                if g:
                                    need("act", "kTf", g - 1)
                                b = bank[2 * (g % 2) + t].rearrange("p (h n) -> p h n", h=2)
                                go(("ks", g, t), qs[:, t, 0:2 * NOPE].rearrange("p (h n) -> p h n", h=2),
                                   b[:, :, 0:NOPE])
                                go(("ev", "kv_up", g, t),
                                   vv[:, t, 2 * g * VD:(2 * g + 2) * VD].rearrange("p (h n) -> p h n", h=2),
                                   b[:, :, NOPE:])
                        if g - 1 in gs:
                            need("act", "kTf", g - 1)
                            go(("kT", g - 1), kT[:, 2 * g - 2:2 * g, :],
                               bank[4 + g % 2].rearrange("p (h n) -> p h n", h=2))

                if l == 1:
                    for t in range(T):
                        need("act", "ckvTf", t)
                        go(("ckvTh", t), cTh[:, 0:2, t * P:(t + 1) * P],
                           bank[6 + t][:, 0:2 * P].rearrange("p (k n) -> p k n", k=2))
                        go(("krT", t), krT[:, t * P:(t + 1) * P], bank[6 + t][:, 2 * P:3 * P])
                    kv(range(4))
                xT_evac(2 + 4 * l)
                load_norm(3 + 4 * l)
                if l == 0:
                    act.wait_ge(aux_loaded, 16)
                    go(("fsel",), fsel, fsel_raw[0:FOX_H])
                    ahead("fox_f")
                    need("act", "fz")
                    go(("fabs",), fg[:, 1], fg[:, 0], ACT.Abs)
                    act.wait_ge(act_done, counts["act_done"])
                    go(("fexp",), fg[:, 2], fg[:, 1], ACT.Exp, scale=-1.0)
                    need("act", "fexp1")
                    go(("fln",), fg[:, 3], fg[:, 3], ACT.Ln)

                    def keep_fqk(c, b):
                        for t in range(T):
                            need("act", "full", f"fox_in{c}", t)
                            if c:
                                need("act", "fTf", {2: 0, 1: 2, 3: 1}[c], t)
                            go(("ev", f"fox_in{c}", t), fqk[:, t], bank[b + t])

                    def keep_fT(c, b):
                        for t in range(T):
                            need("act", "fTf", c, t)
                            dst = (fqT, fkT)[c // 2][:, 4 * (c % 2):4 * (c % 2) + 4, t * P:(t + 1) * P]
                            go(("fT", c, t), dst, bank[b + t].rearrange("p (k n) -> p k n", k=4))

                    def keep_fv(c, b):
                        copy_chunk(f"fox_in{c}", (b, b + 1), lambda t: fv[:, t, (c - 4) * CH:(c - 3) * CH])

                    ahead("fox_in0")
                    keep_fqk(0, 0)
                    ahead("fox_in2")
                    need("act", "cumf")
                    go(("cumh",), cTh[0:FOX_H, 0, :], bank[7][0:FOX_H, 0:S])
                    go(("ncumh",), cTh[0:FOX_H, 1, :], bank[7][0:FOX_H, 0:S], scale=-1.0)
                    keep_fT(0, 4)
                    keep_fqk(2, 2)
                    ahead("fox_in4")
                    keep_fT(2, 6)
                    keep_fv(4, 0)
                    base = unit_at["fox_in1"][0]
                    attention("fox", FOX_H, FOX_DH ** -0.5,
                              {0: [lambda: split_to(base + 4)], 1: [lambda: split_to(base + 5), lambda: keep_fqk(1, 2)],
                               2: [lambda: split_to(base + 6)],
                               3: [lambda: split_to(base + 7), lambda: keep_fT(1, 2), lambda: keep_fqk(3, 0)],
                               4: [lambda: split_to(base + 8)],
                               5: [lambda: split_to(base + 9), lambda: keep_fT(3, 0), lambda: keep_fv(5, 2)],
                               11: [lambda: xT_evac("fox", (0,), b0=2)], 13: [lambda: split_to(base + 10)],
                               15: [lambda: split_to(base + 11)]})
                    xT_evac("fox", (1,), b0=4)
                    ahead("fox_o1")
                else:
                    act.dma_start(norm_c[:, 0:QL], bcast_rows(dram["q_norm"], QL)).then_inc(aux_loaded, 16)
                    ahead("dq0")
                    for t in range(T):
                        need("act", "full", "dq0", t)
                        go(("cqsq", t), tanh[:, t, 0:QL], bank[2 + t][:, 0:QL], ACT.Square,
                           accum_out=stats[:, t:t + 1])
                    kv(range(4, 8))
                    for t in range(T):
                        need("act", "cqTf", t)
                        go(("cqTh", t), cTh[:, :, t * P:(t + 1) * P],
                           bank[6 + t][:, 0:3 * P].rearrange("p (k n) -> p k n", k=3))

                    def keep_q(g):
                        for t in range(T):
                            need("act", "qf", g, t)
                            need("act", "qTf", g - 1, t) if g else need("act", "kTf", 7)
                            go(("qn", g, t), qs[:, t, 0:2 * NOPE].rearrange("p (h n) -> p h n", h=2),
                               bank[t][:, 0:QL].rearrange("p (h n) -> p h n", h=2)[:, :, 0:NOPE])

                    def keep_qT(g):
                        for t in range(T):
                            need("act", "qTf", g, t)
                            if g >= 2:
                                need("act", "S", "mla", 2 * g - 3)
                            go(("qT", g, t), qT[:, g % 2, :, t * P:(t + 1) * P],
                               bank[t][:, 0:3 * P].rearrange("p (k n) -> p k n", k=3))

                    def keep_oT(g):
                        need("act", "oTf", g)
                        go(("oTh", g), xTh[:, 2 * g:2 * g + 2, :], bank[6].rearrange("p (k n) -> p k n", k=2))

                    ahead("uq", 0)
                    keep_q(0)
                    keep_qT(0)
                    fill = {s: [] for s in range(MLA_H + 2)}
                    for g in range(1, 8):
                        fill[2 * g - 2] += [lambda g=g: ahead("uq", g), lambda g=g: keep_q(g)]
                        fill[2 * g - 1].append(lambda g=g: keep_qT(g))
                    for g in range(7):
                        fill[2 * g + 4].append(lambda g=g: keep_oT(g))
                    for s, (c, k) in zip((11, 13, 14, 15), ((0, 0), (0, 1), (1, 0), (1, 1))):
                        fill[s].append(lambda c=c, k=k: split_to(unit_at[f"mla_oa{c}"][k] + RING))
                    attention("mla", MLA_H, (NOPE + ROPE_D) ** -0.5, fill)
                    keep_oT(7)
                    ahead("mla_ob0")
                    ahead("mla_ob1")
                xT_evac(3 + 4 * l)
                load_norm(4 + 4 * l)
                need("act", "pTf", l)
                go(("pTh", l), cTh[:, 0:2, :], bank[4].rearrange("p (k n) -> p k n", k=2))
                ffn(2 + 2 * l)
                act.dma_start(pb, bcast_rows(dram["ple_b"][l], D)).then_inc(aux_loaded, 16)
                if l == 0:
                    load_p(1)
                for c in range(2):
                    if c == 1:
                        ahead(f"ple_p{l}")
                    for t in range(T):
                        need("act", "full", f"ple_p{l}", c, t)
                        go(("ev", f"ple_p{l}", c, t), pp[:, t, c * CH:(c + 1) * CH], bank[4 + 2 * c + t], scale=0.5)
                xT_evac(4 + 4 * l)
                load_norm(5 + 4 * l)
                for c in range(2):
                    ahead(f"ple_g{l}{c}")
                    for t in range(T):
                        need("act", "pz", l, c, t)
                        go(("ptanh", l, c, t), tanh[:, t], pz[:, t], ACT.Tanh, scale=0.5)
                if l == 0:
                    xT_evac(5)
                    load_norm(6)
                    act.dma_start(norm_c[:, 0:KVL], bcast_rows(dram["kv_norm"], KVL)).then_inc(aux_loaded, 16)

        @block.vector
        def _(dve):
            ENG["dve"] = dve
            split = [0]

            def split_to(n):
                while split[0] < min(n, N_UNITS):
                    u = split[0]
                    if units[u][0] not in POOL_STAGES:
                        dve.wait_ge(w_hi_done, u + 1)
                        lo(u % RING, units[u][1] * units[u][2] or UNIT)
                    split[0] += 1

            def lo(slot, cols=UNIT):
                nc.vector.tensor_tensor(w_lo[slot][:, 0:cols], w_raw[slot][:, 0:cols],
                                        w_hi[slot][:, 0:cols].bitcast(F32), ALU.subtract)\
                    .then_inc(w_lo_done[slot], 1)

            def ahead(stage, part=None):
                us = unit_at[stage]
                split_to((us[-1] if part is None else us[part]) + RING)

            def did(ins, *label):
                ins.then_inc(dve_done, mark("dve_done", *label))

            def settle():
                dve.wait_ge(dve_done, counts["dve_done"])

            def rsqrt(n, label=()):
                v, y, a, b = (r[:, 0:n] for r in (rs_v, rs_y, rs_a, rs_b))
                settle()
                did(nc.vector.tensor_scalar(a.bitcast(I32), v.bitcast(I32), 1, None, ALU.logical_shift_right))
                settle()
                did(nc.vector.tensor_scalar(y.bitcast(I32), a.bitcast(I32), -1.0, float(0x5F3759DF), ALU.mult, ALU.add))
                for step in range(3):
                    settle()
                    did(nc.vector.tensor_tensor(a, y, y, ALU.mult))
                    settle()
                    did(nc.vector.scalar_tensor_tensor(out=b, in0=a, scalar=-0.5, in1=v, op0=ALU.mult, op1=ALU.mult))
                    settle()
                    did(nc.vector.scalar_tensor_tensor(out=y, in0=b, scalar=1.5, in1=y, op0=ALU.add, op1=ALU.mult),
                        *(label if step == 2 else ()))
                settle()

            def xT_evac(site, qs_=(0, 1), slot0=0, b0=0, scale=None, tiles=range(T)):
                for t in tiles:
                    for q in qs_:
                        need("dve", "xTh", site, t, q)
                        b = (b0 + t * len(qs_) + q - qs_[0]) % 4 if b0 < 4 else b0 + t
                        sl = (slice(None), slice(slot0 + 4 * q, slot0 + 4 * q + 4), slice(t * P, (t + 1) * P))
                        src = bank[b].rearrange("p (k n) -> p k n", k=4)
                        if scale is None:
                            did(nc.vector.tensor_tensor(xTl[sl], src, xTh[sl].bitcast(F32), ALU.subtract),
                                "xT", site, t, q)
                        else:
                            did(nc.vector.scalar_tensor_tensor(out=xTl[sl], in0=src, scalar=scale,
                                                               in1=xTh[sl].bitcast(F32), op0=ALU.mult,
                                                               op1=ALU.subtract), "xT", site, t, q)

            def moments(t, n):
                settle()
                at = 12 * t + 6 * n
                did(nc.vector.bn_stats(stats[:, at:at + 6], x[:, t, n * CH:(n + 1) * CH]))

            def norm_and_turn(site, rms=False):
                settle()
                for t in range(T):
                    did(nc.vector.bn_aggr(mv_[:, t], stats[:, 12 * t:12 * t + 12]))
                settle()
                if rms:
                    did(nc.vector.tensor_tensor(rs_a[:, 0:T], mv_[:, 0:T, 0], mv_[:, 0:T, 0], ALU.mult))
                    settle()
                    did(nc.vector.scalar_tensor_tensor(out=rs_v[:, 0:T], in0=mv_[:, 0:T, 1], scalar=RMS_EPS,
                                                       in1=rs_a[:, 0:T], op0=ALU.add, op1=ALU.add))
                else:
                    did(nc.vector.tensor_scalar(rs_v[:, 0:T], mv_[:, 0:T, 1], LN_EPS, None, ALU.add))
                rsqrt(T)
                dve.wait_ge(gb_loaded, 32 * (site + 1))

                def apply(t, q):
                    cols = slice(q * CH, (q + 1) * CH)
                    xs, gain = x[:, t, cols], gb[:, 0, cols]
                    if rms:
                        did(nc.vector.scalar_tensor_tensor(out=normed[:, t, cols], in0=xs, scalar=rs_y[:, t:t + 1],
                                                           in1=gain, op0=ALU.mult, op1=ALU.mult), "norm", site, t, q)
                        return
                    did(nc.vector.scalar_tensor_tensor(out=xs, in0=xs, scalar=mv_[:, t, 0:1], in1=gain,
                                                       op0=ALU.subtract, op1=ALU.mult))
                    settle()
                    did(nc.vector.scalar_tensor_tensor(out=xs, in0=xs, scalar=rs_y[:, t:t + 1], in1=gb[:, 1, cols],
                                                       op0=ALU.mult, op1=ALU.add), "norm", site, t, q)

                turned = site not in (9,)
                apply(0, 0)
                apply(0, 1)
                if turned:
                    evac_one(site, 0, 0)
                apply(1, 0)
                if turned:
                    evac_one(site, 0, 1)
                apply(1, 1)
                if turned:
                    evac_one(site, 1, 0)
                    evac_one(site, 1, 1)

            def evac_one(site, t, q):
                need("dve", "xTh", site, t, q)
                sl = (slice(None), slice(4 * q, 4 * q + 4), slice(t * P, (t + 1) * P))
                did(nc.vector.tensor_tensor(xTl[sl], bank[2 * t + q].rearrange("p (k n) -> p k n", k=4),
                                            xTh[sl].bitcast(F32), ALU.subtract), "xT", site, t, q)

            def ffn(f, alpha):
                u0 = unit_at[f"ffn{f}"][0]
                g0 = f * FI
                half = 0.5 if f == 0 else 0.25

                def hidden(i):
                    for t in range(T):
                        dve.wait_ge(tanh_done, i * 2 + (2 * g0 + t + 1))
                        nc.vector.scalar_tensor_tensor(out=hid[:, t], in0=tanh[:, t, 0:HB], scalar=1.0,
                                                       in1=bank[t][:, 0:HB], op0=ALU.add, op1=ALU.mult)\
                            .then_inc(hid_part, 1)
                    for t in range(T):
                        dve.wait_ge(hid_part, i * 2 + (2 * g0 + t + 1))
                        nc.vector.scalar_tensor_tensor(out=hid[:, t], in0=hid[:, t], scalar=half,
                                                       in1=bank[t][:, HB:2 * HB], op0=ALU.mult, op1=ALU.mult)\
                            .then_inc(hid_done, 1)

                def hT_rest(i):
                    for k in range(2):
                        dve.wait_ge(hT_hi, i * 2 + (2 * g0 + k + 1))
                        nc.vector.tensor_tensor(hTl[:, k, :], bank[2 + k][:, 0:S], hTh[:, k, :].bitcast(F32),
                                                ALU.subtract).then_inc(hT_lo, 1)

                split_to(u0 + 3)
                hidden(0)
                split_to(u0 + 4)
                hT_rest(0)
                with dve.Fori(1, FI) as i:
                    dve.wait_ge(w_hi_done, i * 3 + (u0 + 2))
                    lo((u0 + 4) % RING)
                    hidden(i)
                    dve.wait_ge(w_hi_done, i * 3 + (u0 + 3))
                    lo((u0 + 5) % RING)
                    dve.wait_ge(w_hi_done, i * 3 + (u0 + 4))
                    lo((u0 + 6) % RING)
                    hT_rest(i)
                split[0] = u0 + 3 * FI + 1
                for t in range(T):
                    for n in range(2):
                        need("dve", "ffn_full", f, t, n)
                        c = slice(n * CH, (n + 1) * CH)
                        did(nc.vector.scalar_tensor_tensor(out=x[:, t, c], in0=x[:, t, c], scalar=alpha,
                                                           in1=acc[:, t, c], op0=ALU.mult, op1=ALU.add),
                            *(("ffn_out", f, t) if n else ()))
                        if f:
                            moments(t, n)

            def attention(name, heads, out, dv, fill):
                def soft(h):
                    need("dve", "S", name, h)
                    if h >= 4:
                        need("dve", "exp", name, h - 4)
                    s, a = 2 * (h % 4), 4 * (h % 2)
                    b = bank[4 + h % 2]
                    did(nc.vector.tensor_reduce(rs_a[:, a:a + 1], b[:, 0:P], AX_X, ALU.max))
                    did(nc.vector.tensor_reduce(rs_a[:, a + 1:a + 2], b[:, P:3 * P], AX_X, ALU.max))
                    settle()
                    did(nc.vector.tensor_scalar(negmax[:, s:s + 2], rs_a[:, a:a + 2], -SCALE[name], None, ALU.mult),
                        "soft", name, h)

                def gather(h):
                    need("dve", "PV", name, h)
                    s, r = 2 * (h % 4), 2 * (h % 2)
                    did(nc.vector.reciprocal(rsum[:, r:r + 2], psum_e[:, s:s + 2]))
                    settle()
                    for t in range(T):
                        did(nc.vector.tensor_scalar(out(h, t), bank[7][:, t * dv:(t + 1) * dv],
                                                    rsum[:, r + t:r + t + 1], None, ALU.mult),
                            *(("o", name, h) if t else ()))

                for s in range(heads + 3):
                    for work in fill.get(s - 1, ()):
                        work()
                    if s < heads:
                        soft(s)
                    if 2 <= s < heads + 2:
                        gather(s - 2)

            SCALE = {"moba": MOBA_DH ** -0.5, "fox": FOX_DH ** -0.5, "mla": (NOPE + ROPE_D) ** -0.5}

            split_to(3)
            dve.wait_ge(const_loaded, N_CONST)
            for t in range(T):
                for n in range(2):
                    did(nc.vector.bn_stats(stats[:, 12 * t + 6 * n:12 * t + 6 * n + 6], x[:, t, n * CH:(n + 1) * CH]))
            norm_and_turn(0, rms=True)
            for n, stage in enumerate(("rq0", "rk0")):
                ahead(stage)
                for t in range(T):
                    need("dve", "full", stage, t)
                    if n or t:
                        settle()
                    b = bank[2 * n + t].rearrange("p (h a n) -> p h a n", h=RET_H, a=2)
                    r = rope_ret[:, t].rearrange("p (a n) -> p a n", a=4)
                    o = rqk[:, 2 * n + t].rearrange("p (h a n) -> p h a n", h=RET_H, a=2)
                    z = rtmp.rearrange("p (h a n) -> p h a n", h=RET_H, a=2)
                    for a in range(2):
                        did(nc.vector.tensor_tensor(z[:, :, a], b[:, :, 1 - a],
                                                    r[:, 2 + a].unsqueeze(1).broadcast_to([P, RET_H, 64]), ALU.mult))
                        did(nc.vector.tensor_tensor(o[:, :, a], b[:, :, a],
                                                    r[:, a].unsqueeze(1).broadcast_to([P, RET_H, 64]), ALU.mult),
                            *(("ev", stage, t) if a else ()))
                    settle()
                    did(nc.vector.tensor_tensor(rqk[:, 2 * n + t], rqk[:, 2 * n + t], rtmp, ALU.add), "rot", n, t)
            ahead("rv0")
            ahead("rv1")

            def decay_scores(h):
                need("dve", "RS", h)
                if h >= 2:
                    need("dve", "RO", h - 2)
                did(nc.vector.tensor_tensor(pT[:, h % 2], bank[4 + h % 2][:, 0:3 * P], decay[:, h], ALU.mult),
                    "decayed", h)

            def ret_moments(g):
                need("dve", "RO", g)
                for t in range(T):
                    did(nc.vector.bn_stats(stats[:, 6 * t:6 * t + 6], bank[6 + g % 2][:, t * RET_DV:(t + 1) * RET_DV]),
                        *(("rstats", g) if t else ()))
                settle()
                for t in range(T):
                    did(nc.vector.bn_aggr(mv_[:, 2 * g + t], stats[:, 6 * t:6 * t + 6]))
                settle()

            def sum_squares(n, stage):
                ahead(stage)
                for t in range(T):
                    need("dve", "msq", n, t)
                    did(nc.vector.tensor_reduce(rs_b[:, 8 * (2 * n + t):8 * (2 * n + t) + 8],
                                                tanh[:, 0].rearrange("p (h n) -> p h n", n=MOBA_DH), AX_X, ALU.add),
                        "mss", 2 * n + t)

            sum_squares(0, "mq0")
            decay_scores(0)
            decay_scores(1)
            sum_squares(1, "mk0")
            ret_moments(0)
            decay_scores(2)
            ahead("mv0")
            did(nc.vector.tensor_scalar(rs_v, rs_b, 1.0 / MOBA_DH, RMS_EPS, ALU.mult, ALU.add))
            rsqrt(32)
            for i in range(2):
                for t in range(T):
                    m = mqk[:, 2 * i + t].rearrange("p (h n) -> p h n", n=MOBA_DH)
                    y = rs_y[:, 8 * (2 * i + t):8 * (2 * i + t) + 8]
                    did(nc.vector.tensor_tensor(m, m, y.unsqueeze(2).broadcast_to([P, MOBA_H, MOBA_DH]), ALU.mult))
                    settle()
                    did(nc.vector.tensor_tensor(m, m, head_w[:, i].unsqueeze(1).broadcast_to([P, MOBA_H, MOBA_DH]),
                                                ALU.mult), "mnorm", i, t)
            ret_moments(1)
            decay_scores(3)
            ahead("rg0")
            ret_moments(2)
            ret_moments(3)
            did(nc.vector.tensor_scalar(rs_v[:, 0:8], mv_[:, 0:8, 1], GN_EPS, None, ALU.add))
            rsqrt(8)
            need("dve", "ro", RET_H - 1)
            for h in range(RET_H):
                for t in range(T):
                    r = ro[:, t, h * RET_DV:(h + 1) * RET_DV]
                    did(nc.vector.tensor_scalar(r, r, mv_[:, 2 * h + t, 0:1], rs_y[:, 2 * h + t:2 * h + t + 1],
                                                ALU.subtract, ALU.mult))
            settle()
            for n in range(2):
                ahead(f"rg{n}")
                for t in range(T):
                    need("dve", "tanh", f"rg{n}", t)
                    c = slice(n * CH, (n + 1) * CH)
                    did(nc.vector.scalar_tensor_tensor(out=tanh[:, t], in0=tanh[:, t], scalar=1.0,
                                                       in1=bank[2 - 2 * n + t], op0=ALU.add, op1=ALU.mult))
                    settle()
                    did(nc.vector.scalar_tensor_tensor(out=ro[:, t, c], in0=tanh[:, t], scalar=0.5, in1=ro[:, t, c],
                                                       op0=ALU.mult, op1=ALU.mult), "ev", f"rg{n}", t)
            split_to(unit_at["ga0"][0] + RING)
            attention("moba", MOBA_H, lambda h, t: mo[:, t, h * MOBA_DH:(h + 1) * MOBA_DH], MOBA_DH,
                      {s: [lambda u=u: split_to(u + RING)] for s, u in
                       zip((0, 1, 2, 4, 5, 7, 8), [*unit_at["ga0"], *unit_at["ga1"], *unit_at["gb0"], *unit_at["gb1"]][1:])})
            xT_evac("ret", slot0=8)
            xT_evac("moba", (0,), b0=2)
            for n in range(2):
                ahead(f"ret_out{n}")
                for t in range(T):
                    need("dve", "full", f"ret_out{n}", t)
                    m = sga[:, t, n * CH:(n + 1) * CH]
                    did(nc.vector.scalar_tensor_tensor(out=m, in0=m, scalar=1.0, in1=bank[2 * n + t],
                                                       op0=ALU.add, op1=ALU.mult), "ev", f"ret_out{n}", t)
            for n in range(2):
                ahead(f"moba_out{n}")
                for t in range(T):
                    need("dve", "full", f"moba_out{n}", t)
                    c = slice(n * CH, (n + 1) * CH)
                    did(nc.vector.scalar_tensor_tensor(out=sgb[:, t, c], in0=sgb[:, t, c], scalar=1.0,
                                                       in1=bank[2 * n + t], op0=ALU.add, op1=ALU.mult))
                    settle()
                    did(nc.vector.tensor_tensor(sga[:, t, c], sga[:, t, c], sgb[:, t, c], ALU.add),
                        "ev", f"moba_out{n}", t)
            xT_evac("mix", slot0=8, scale=0.5)

            def update(stage, alpha, stats_too=True):
                for n in range(2):
                    for t in range(T):
                        add_chunk(stage, n, t, (2 * n, 2 * n + 1), alpha)
                        if stats_too:
                            moments(t, n)
                    ahead(f"{stage}{n}")

            def add_chunk(stage, n, t, banks, alpha):
                need("dve", "full", f"{stage}{n}", t)
                xs = x[:, t, n * CH:(n + 1) * CH]
                did(nc.vector.scalar_tensor_tensor(out=xs, in0=xs, scalar=alpha, in1=bank[banks[t]],
                                                   op0=ALU.mult, op1=ALU.add), "ev", f"{stage}{n}", t)

            ahead("w_o0")
            update("w_o", 1.0)
            norm_and_turn(1, rms=True)
            ffn(0, 1.0)
            for l in range(2):
                if l == 0:
                    xT_evac("raw")
                if l == 1:
                    ahead("kv_down0")
                    for t in range(T):
                        need("dve", "kvsq", t)
                    did(nc.vector.tensor_scalar(rs_v[:, 0:T], stats[:, 0:T], 1.0 / KVL, RMS_EPS, ALU.mult, ALU.add))
                    rsqrt(T)
                    dve.wait_ge(aux_loaded, 48)
                    for t in range(T):
                        did(nc.vector.scalar_tensor_tensor(out=cq[:, t, 0:KVL], in0=bank[4 + t][:, 0:KVL],
                                                           scalar=rs_y[:, t:t + 1], in1=norm_c[:, 0:KVL],
                                                           op0=ALU.mult, op1=ALU.mult))
                        b = bank[4 + t][:, KVL:KVL + ROPE_D].rearrange("p (a n) -> p a n", a=2)
                        r = rope_mla[:, t].rearrange("p (a n) -> p a n", a=4)
                        z = kr[:, t].rearrange("p (c a n) -> p c a n", c=2, a=2)
                        for a in range(2):
                            did(nc.vector.tensor_tensor(z[:, 0, a], b[:, a], r[:, a], ALU.mult))
                            did(nc.vector.tensor_tensor(z[:, 1, a], b[:, 1 - a], r[:, 2 + a], ALU.mult),
                                *(("ev", "kv_down0", t) if a else ()))
                        settle()
                        did(nc.vector.tensor_tensor(kr[:, t, 0:ROPE_D], kr[:, t, 0:ROPE_D], kr[:, t, ROPE_D:], ALU.add))
                        settle()
                        did(nc.vector.tensor_copy(kr[:, t, ROPE_D:], kr[:, t, 0:ROPE_D]), "ckv", t)
                ffn(1 + 2 * l, ALPHA)
                if l == 1:
                    for t in range(T):
                        need("dve", "krT", t)
                        did(nc.vector.tensor_tensor(cTl[:, 0:2, t * P:(t + 1) * P],
                                                    bank[6 + t][:, 0:2 * P].rearrange("p (k n) -> p k n", k=2),
                                                    cTh[:, 0:2, t * P:(t + 1) * P].bitcast(F32), ALU.subtract),
                            "ckvT", t)
                    split_to(unit_at["kv_up"][0] + 2)
                norm_and_turn(2 + 4 * l)
                if l == 0:
                    ahead("fox_f")
                    for t in range(T):
                        need("dve", "full", "fox_f", t)
                        did(nc.vector.tensor_tensor(fg[:, 0, t * FOX_H:(t + 1) * FOX_H], bank[4 + t][:, 0:FOX_H],
                                                    fox_b, ALU.add), "ev", "fox_f", t)
                    note(("fz",), "dve_done", counts["dve_done"])
                    need("dve", "fexp")
                    did(nc.vector.tensor_scalar(fg[:, 3], fg[:, 2], 1.0, None, ALU.add), "fexp1")
                    need("dve", "fln")
                    did(nc.vector.scalar_tensor_tensor(out=fg[:, 5], in0=fg[:, 0], scalar=0.0, in1=fg[:, 3],
                                                       op0=ALU.min, op1=ALU.subtract), "logf")
                    ahead("fox_in0")
                    ahead("fox_in2")
                    need("dve", "ncumh")
                    did(nc.vector.tensor_tensor(cTl[0:FOX_H, 0, :], bank[7][0:FOX_H, 0:S],
                                                cTh[0:FOX_H, 0, :].bitcast(F32), ALU.subtract))
                    did(nc.vector.scalar_tensor_tensor(out=cTl[0:FOX_H, 1, :], in0=bank[7][0:FOX_H, 0:S], scalar=-1.0,
                                                       in1=cTh[0:FOX_H, 1, :].bitcast(F32), op0=ALU.mult,
                                                       op1=ALU.subtract), "cum")
                    ahead("fox_in4")
                    base = unit_at["fox_in1"][0]
                    attention("fox", FOX_H, lambda h, t: fo[:, t, h * FOX_DH:(h + 1) * FOX_DH], FOX_DH,
                              {4: [lambda: split_to(base + 8)], 6: [lambda: split_to(base + 9)],
                               12: [lambda: xT_evac("fox", (0,), b0=2)], 13: [lambda: split_to(base + 10)],
                               15: [lambda: split_to(base + 11)]})
                    xT_evac("fox", (1,), b0=4)
                    ahead("fox_o1")
                    update("fox_o", ALPHA)
                else:
                    ahead("kv_up", 1)
                    ahead("dq0")
                    for t in range(T):
                        need("dve", "cqsq", t)
                    did(nc.vector.tensor_scalar(rs_v[:, 0:T], stats[:, 0:T], 1.0 / QL, RMS_EPS, ALU.mult, ALU.add))
                    rsqrt(T)
                    dve.wait_ge(aux_loaded, 64)
                    for t in range(T):
                        did(nc.vector.scalar_tensor_tensor(out=cq[:, t], in0=bank[2 + t][:, 0:QL],
                                                           scalar=rs_y[:, t:t + 1], in1=norm_c,
                                                           op0=ALU.mult, op1=ALU.mult), "cqn", t)
                        note(("ev", "dq0", t), "dve_done", counts["dve_done"])
                    ahead("kv_up", 3)
                    for t in range(T):
                        need("dve", "cqTh", t)
                        did(nc.vector.tensor_tensor(cTl[:, :, t * P:(t + 1) * P],
                                                    bank[6 + t][:, 0:3 * P].rearrange("p (k n) -> p k n", k=3),
                                                    cTh[:, :, t * P:(t + 1) * P].bitcast(F32), ALU.subtract),
                            "cqT", t)

                    def rope_q(g):
                        for t in range(T):
                            need("dve", "qn", g, t)
                            b = bank[t][:, 0:QL].rearrange("p (h n) -> p h n", h=2)[:, :, NOPE:]
                            r = rope_mla[:, t].rearrange("p (a n) -> p a n", a=4)
                            o = qs[:, t, 2 * NOPE:].rearrange("p (h n) -> p h n", h=2)
                            z = kr[:, t].rearrange("p (h n) -> p h n", h=2)
                            for a in range(2):
                                lo_, hi_ = slice(32 * a, 32 * a + 32), slice(32 - 32 * a, 64 - 32 * a)
                                rb = [r[:, q].unsqueeze(1).broadcast_to([P, 2, 32]) for q in (a, 2 + a)]
                                did(nc.vector.tensor_tensor(o[:, :, lo_], b[:, :, lo_], rb[0], ALU.mult))
                                did(nc.vector.tensor_tensor(z[:, :, lo_], b[:, :, hi_], rb[1], ALU.mult))
                            settle()
                            did(nc.vector.tensor_tensor(qs[:, t, 2 * NOPE:], qs[:, t, 2 * NOPE:], kr[:, t], ALU.add),
                                "qs", g, t)

                    def rest_oT(g):
                        need("dve", "oTh", g)
                        did(nc.vector.tensor_tensor(xTl[:, 2 * g:2 * g + 2, :],
                                                    bank[6].rearrange("p (k n) -> p k n", k=2),
                                                    xTh[:, 2 * g:2 * g + 2, :].bitcast(F32), ALU.subtract), "oT", g)

                    rope_q(0)
                    fill = {s: [] for s in range(MLA_H + 2)}
                    for g in range(1, 8):
                        fill[2 * g - 2].append(lambda g=g: rope_q(g))
                    for g in range(7):
                        fill[2 * g + 4].append(lambda g=g: rest_oT(g))
                    fill[13] += [lambda t=t: add_chunk("mla_oa", 0, t, (2, 3), ALPHA) for t in range(T)]
                    fill[15] += [lambda t=t: add_chunk("mla_oa", 1, t, (2, 3), ALPHA) for t in range(T)]
                    fill[15].append(lambda: ahead("mla_oa1"))
                    attention("mla", MLA_H, lambda h, t: mlo[:, (h // 2) % 2, t, (h % 2) * VD:(h % 2 + 1) * VD], VD, fill)
                    rest_oT(7)
                    ahead("mla_ob0")
                    update("mla_ob", 1.0)
                norm_and_turn(3 + 4 * l)
                need("dve", "pTh", l)
                did(nc.vector.tensor_tensor(cTl[:, 0:2, :], bank[4].rearrange("p (k n) -> p k n", k=2),
                                            cTh[:, 0:2, :].bitcast(F32), ALU.subtract), "pT", l)
                ffn(2 + 2 * l, ALPHA)
                norm_and_turn(4 + 4 * l)
                ahead(f"ple_p{l}")
                dve.wait_ge(aux_loaded, (32, 80)[l])
                for c in range(2):
                    ahead(f"ple_g{l}{c}")
                    cols = slice(c * CH, (c + 1) * CH)
                    for t in range(T):
                        need("dve", "full", f"ple_g{l}{c}", t)
                        if c:
                            need("dve", "ptanh", l, 0, t)
                        did(nc.vector.tensor_tensor(pz[:, t], bank[2 * c + t], pb[:, cols], ALU.add), "pz", l, c, t)
                        note(("ev", f"ple_g{l}{c}", t), "dve_done", counts["dve_done"])
                    for t in range(T):
                        need("dve", "ptanh", l, c, t)
                        need("dve", "ev", f"ple_p{l}", c, t)
                        did(nc.vector.scalar_tensor_tensor(out=tanh[:, t], in0=tanh[:, t], scalar=1.0,
                                                           in1=pp[:, t, cols], op0=ALU.add, op1=ALU.mult))
                        settle()
                        did(nc.vector.scalar_tensor_tensor(out=x[:, t, cols], in0=x[:, t, cols], scalar=ALPHA,
                                                           in1=tanh[:, t], op0=ALU.mult, op1=ALU.add))
                        moments(t, c)
                norm_and_turn(5 + 4 * l)
    return found


def kernel(**inputs):
    import concourse.bacc as bacc
    from concourse.bass_utils import run_bass_kernel_spmd

    a = {n: np.asarray(v) for n, v in inputs.items()}
    arrays = {"x": a["x"].reshape(S, D)}
    for n in ("norm1_w", "w_in", "q_norm_w", "k_norm_w", "w_ret_out", "w_moba_out", "w_o", "norm2_w", "w_ffn_gate",
              "w_ffn_up", "w_ffn_down"):
        arrays[n] = a[n][0]
    arrays["p"] = a["p_2"].reshape(2, S, PLE)
    for n in ("ffn1_w_in", "ffn1_w_out", "ffn2_w_in", "ffn2_w_out", "ln_g", "ln_b", "ple_w_gate", "ple_w_proj"):
        arrays[n] = a[n + "_2"]
    arrays["ple_b"] = a["ple_b_gate_2"]
    for n in ("fox_w_in", "fox_b_f", "fox_w_o", "mla_w_dq", "mla_w_o"):
        arrays[n] = a[n + "_2"][0]
    arrays["q_norm"] = a["mla_q_norm_2"][0]
    arrays["mla_w_uq"] = a["mla_w_uq_2"].reshape(QL, MLA_H * (NOPE + ROPE_D))
    arrays["kv_w_down"], arrays["kv_norm"] = a["kv_w_down_2"], a["kv_norm_2"]
    arrays["kv_w_up"] = a["kv_w_up_2"].reshape(KVL, MLA_H * (NOPE + VD))
    arrays.update(shape_constants())
    arrays = {f"in_{n}": np.ascontiguousarray(v) for n, v in arrays.items()}

    def program(marks):
        nc = bacc.Bacc("TRN2", target_bir_lowering=False, num_devices=1)
        dram = {n[3:]: nc.dram_tensor(n, v.shape, mybir.dt.from_np(v.dtype), kind="ExternalInput").ap()
                for n, v in arrays.items()}
        dram["out"] = nc.dram_tensor("out_x", (S, D), F32, kind="ExternalOutput").ap()
        return nc, build(nc, dram, marks)

    _, marks = program({})
    nc, again = program(marks)
    assert again == marks
    r = run_bass_kernel_spmd(nc, [arrays], core_ids=[0])
    return r.results[0]["out_x"].reshape(1, S, D)
```

```python
from contextlib import ExitStack
import math

import numpy as np
import concourse.bass as bass
from concourse import mybir

P = 128
T = 2
S = T * P
D = 1024
KD = D // P
CH = 512
RING = 3
UNIT = 2048
F_HID = 2816
HB = 256
FI = F_HID // HB
RET_H, RET_DK, RET_DV = 4, 128, 256
MOBA_H, MOBA_DH = 8, 64
FOX_H, FOX_DH = 16, 64
FOX_LO = 64
FOX_K = FOX_LO + FOX_H
MLA_H, NOPE, ROPE_D, VD = 16, 128, 64, 128
QL, KVL = 384, 256
PLE = 256
RMS_EPS, LN_EPS, GN_EPS = 1e-6, 1e-5, 1e-5
ALPHA = float((2 * 2) ** 0.25)
NEG = -1e30
POOL_STAGES = ("kv_down0", "kv_up", "fox_q1", "fox_k1", "fox_q2", "fox_k2", "fox_v5", "fox_q3", "fox_k3", "uq",
               "mla_oa0", "mla_oa1")

F32 = mybir.dt.float32
F32R = mybir.dt.float32r
I32 = mybir.dt.int32
ALU = mybir.AluOpType
ACT = mybir.ActivationFunctionType
AX_X = mybir.AxisListType.X


def shape_constants():
    c = {}
    c["ident"] = np.eye(P, dtype=np.float32)
    i = np.arange(P)
    c["mask"] = np.where(i[None, :] <= i[:, None], 0.0, NEG)
    lg = np.log1p(-np.exp2(-5.0 - np.arange(RET_H)))
    dec = np.zeros((P, RET_H, 3, P))
    for h in range(RET_H):
        diff = i[None, :] - i[:, None]
        own = np.where(diff >= 0, np.exp(np.maximum(diff, 0) * lg[h]), 0.0)
        dec[:, h, 0] = own
        dec[:, h, 1] = np.exp((diff + P) * lg[h])
        dec[:, h, 2] = own
    c["decay"] = (dec * RET_DK ** -0.5).reshape(P, RET_H * 3 * P)
    pos = np.arange(S).reshape(T, P).T

    def rope(half, base):
        inv = (base ** (-np.arange(half, dtype=np.float32) / np.float32(half))).astype(np.float32)
        ang = (pos[:, :, None].astype(np.float32) * inv).astype(np.float32)
        return np.cos(ang.astype(np.float64)), np.sin(ang.astype(np.float64))

    for name, half in (("rope_ret", RET_DK // 2), ("rope_mla", ROPE_D // 2)):
        cos, sin = rope(half, np.float32(10000.0))
        c[name] = np.concatenate([cos, cos, -sin, sin], 2).reshape(P, T * 4 * half)
    sel = np.zeros((FOX_K, FOX_H, P))
    for r in (0, FOX_LO):
        sel[r + np.arange(FOX_H), np.arange(FOX_H), :] = -math.sqrt(FOX_DH)
    c["sel"] = sel.reshape(FOX_K, FOX_H * P)
    return {n: np.ascontiguousarray(a, dtype=np.float32) for n, a in c.items()}


def weight_units(w):
    units, at = [], {}

    def add(stage, kt, n, halves):
        at.setdefault(stage, []).append(len(units))
        units.append((stage, kt, n, halves))

    def dense(stage, m, k0, kts, c0, n):
        rows = m[k0 * P:(k0 + kts) * P, c0:c0 + n].rearrange("(k p) n -> p k n", p=P)
        a = (kts + 1) // 2
        if kts == 1:
            b = n // 2
            add(stage, kts, n, [((0, 1), (0, b), rows[:, :, 0:b]), ((0, 1), (b, n), rows[:, :, b:n])])
        else:
            add(stage, kts, n, [((0, a), (0, n), rows[:, 0:a, :]), ((a, kts), (0, n), rows[:, a:kts, :])])

    def chunks(stage, m, k, c0, count, n=CH, per=4, first=0):
        for c in range(count):
            for k0 in range(0, k, per):
                dense(f"{stage}{c + first}", m, k0, min(per, k - k0), c0 + c * n, n)

    def ffn(f):
        for _ in range(3 * FI):
            add(f"ffn{f}", 0, 0, None)

    w_in = w["w_in"]
    for name, c0, count in (("rq", 0, 1), ("rk", 512, 1), ("rv", 1024, 2), ("mq", 3072, 1), ("mk", 3584, 1),
                            ("mv", 4096, 1), ("rg", 2048, 2)):
        chunks(name, w_in, KD, c0, count)
    chunks("ga", w_in, KD, 4608, 2)
    chunks("gb", w_in, KD, 5632, 2)
    chunks("ret_out", w["w_ret_out"], KD, 0, 2)
    chunks("moba_out", w["w_moba_out"], 4, 0, 2)
    chunks("w_o", w["w_o"], KD, 0, 2)
    ffn(0)
    ffn(1)

    def fox_qk(j):
        for c0, name in ((0, "q"), (D, "k")):
            dense(f"fox_{name}{j}", w["fox_w_in"], 0, KD, c0 + j * S, S)

    chunks("fox_v", w["fox_w_in"], KD, 4 * CH, 1, first=4)
    dense("fox_f", w["fox_w_in"], 0, KD, 3 * D, FOX_H)
    fox_qk(0)
    fox_qk(1)
    fox_qk(2)
    chunks("fox_v", w["fox_w_in"], KD, 5 * CH, 1, first=5)
    fox_qk(3)
    for k0 in (0, 4):
        for c in range(2):
            dense(f"fox_o{c}", w["fox_w_o"], k0, 4, c * CH, CH)
    ffn(2)
    dense("ple_p0", w["ple_w_proj"][0], 0, 2, 0, D)
    chunks("ple_g0", w["ple_w_gate"][0], KD, 0, 2)
    chunks("kv_down", w["kv_w_down"], KD, 0, 1, n=KVL + ROPE_D)
    ffn(3)

    def kv_up(c):
        dense("kv_up", w["kv_w_up"], 0, 2, c * D, D)

    def uq(g):
        dense("uq", w["mla_w_uq"], 0, 3, g * QL, QL)

    for c in range(2):
        kv_up(c)
    chunks("dq", w["mla_w_dq"], KD, 0, 1, n=QL)
    kv_up(2)
    uq(0)
    kv_up(3)
    for g in range(1, 8):
        uq(g)
    for k0 in (0, 4):
        dense("mla_oa0", w["mla_w_o"], k0, 4, 0, CH)
    for k0 in (0, 4):
        dense("mla_oa1", w["mla_w_o"], k0, 4, CH, CH)
    for c in range(2):
        for k0 in (8, 12):
            dense(f"mla_ob{c}", w["mla_w_o"], k0, 4, c * CH, CH)
    ffn(4)
    dense("ple_p1", w["ple_w_proj"][1], 0, 2, 0, D)
    chunks("ple_g1", w["ple_w_gate"][1], KD, 0, 2)
    return units, at


def build(nc, dram, marks):
    found = {}
    units, unit_at = weight_units(dram)
    N_UNITS = len(units)
    pool_units = {u for u, unit in enumerate(units) if unit[0] in POOL_STAGES}
    pool_units |= {unit_at[f"ffn{f}"][0] + 1 for f in range(5)}
    pool_units |= {unit_at[stage][i] for stage, i in (("rq0", 1), ("rg0", 1), ("moba_out1", 0), ("fox_v4", 1),
                                                      ("ple_g00", 1), ("ple_g10", 1))}
    ffn_w = [(dram["w_ffn_gate"], dram["w_ffn_up"], dram["w_ffn_down"])]
    for l in range(2):
        for n in (1, 2):
            m = dram[f"ffn{n}_w_in"][l]
            ffn_w.append((m[:, 0:F_HID], m[:, F_HID:2 * F_HID], dram[f"ffn{n}_w_out"][l]))

    with ExitStack() as ctx:
        def sb(name, cols, dt=F32):
            return ctx.enter_context(nc.sbuf_tensor(name, [P, cols], dt))

        sems = {}

        def sem(name):
            sems[name] = ctx.enter_context(nc.semaphore(name))
            return sems[name]

        w_raw = [sb(f"w_raw{s}", UNIT) for s in range(RING)]
        w_hi = [sb(f"w_hi{s}", UNIT, F32R) for s in range(RING)]
        w_lo = [sb(f"w_lo{s}", UNIT, F32R) for s in range(RING)]
        x = sb("x", T * D)[:, :].rearrange("p (t n) -> p t n", t=T)
        xTh = sb("xTh", 16 * S, F32R)[:, :].rearrange("p (k n) -> p k n", k=16)
        fsel = xTh[0:FOX_K, 8:16, :].rearrange("p k (a n) -> p (k a) n", n=P)
        xTl = sb("xTl", 16 * S, F32R)[:, :].rearrange("p (k n) -> p k n", k=16)
        cqTh, cqTl = xTh[:, 13:16], xTl[:, 13:16]
        cTh = sb("cTh", 3 * S, F32R)[:, :].rearrange("p (k n) -> p k n", k=3)
        cTl = sb("cTl", 3 * S, F32R)[:, :].rearrange("p (k n) -> p k n", k=3)
        hTh = sb("hTh", 2 * S, F32R)[:, :].rearrange("p (k n) -> p k n", k=2)
        hTl = sb("hTl", 2 * S, F32R)[:, :].rearrange("p (k n) -> p k n", k=2)
        hLh, hLl = xTh[:, 8:10], xTl[:, 8:10]
        hid = sb("hid", 2 * S)[:, :].rearrange("p (k n) -> p k n", k=2)
        norm_c = hid.rearrange("p k n -> p (k n)")[:, 0:QL]
        tanh = sb("tanh", T * CH)[:, :].rearrange("p (t n) -> p t n", t=T)
        gb = sb("gb", 2 * D)[:, :].rearrange("p (a n) -> p a n", a=2)
        pin = sb("pin", T * PLE)[:, :].rearrange("p (t n) -> p t n", t=T)
        ident = sb("ident", P)[:, :]
        ident_r = sb("ident_r", P, F32R)[:, :]
        mask_r = sb("mask_r", 2 * P, F32R)[:, :]
        decay = sb("decay", RET_H * 3 * P)[:, :].rearrange("p (h n) -> p h n", h=RET_H)
        rope_ret = sb("rope_ret", T * 256)[:, :].rearrange("p (t n) -> p t n", t=T)
        rope_mla = sb("rope_mla", T * 128)[:, :].rearrange("p (t n) -> p t n", t=T)
        head_w = sb("head_w", 2 * MOBA_DH)[:, :].rearrange("p (a n) -> p a n", a=2)
        fox_b = sb("fox_b", 1)[0:FOX_H, :]
        stats = sb("stats", 64)[:, :]
        row_sum = sb("row_sum", 2 * T)[:, :]
        neg_mean, sq_sum, std, rstd = (sb(n, T)[:, :] for n in ("neg_mean", "sq_sum", "std", "rstd"))
        unused = sb("unused", 1)[:, :]
        eps = sb("eps", 2)[:, :]
        squares = sb("squares", D)[:, :]
        mv_ = sb("mean_var", 2 * 16)[:, :].rearrange("p (a n) -> p a n", n=2)
        rs_v, rs_y, rs_a, rs_b = (sb(f"rsqrt_{n}", 32)[:, :] for n in "vyab")
        negmax = sb("negmax", 8)[:, :]
        psum_e = sb("exp_sum", 8)[:, :]
        rsum = sb("exp_rsum", 4)[:, :]

        ARENA = 13568
        arena = sb("arena", ARENA)[:, :]

        class Carve:
            def __init__(self):
                self.at = 0

            def __call__(self, cols):
                self.at += cols
                assert self.at <= ARENA, self.at
                return arena[:, self.at - cols:self.at]

            def tiles(self, a, n):
                return self(a * n).rearrange("p (a n) -> p a n", a=a)

        common = Carve()
        pr = common.tiles(2, 384)
        pT = common.tiles(2, 384)
        shared_end = common.at

        def carve():
            c = Carve()
            c.at = shared_end
            return c

        c1 = carve()
        rqk = c1.tiles(4, 512)
        rqT = c1.tiles(4, S)
        rkT = c1.tiles(4, S)
        rv = c1.tiles(T, D)
        mqk = c1.tiles(4, 512)
        mqT = c1.tiles(4, S)
        mkT = c1.tiles(4, S)
        mv = c1.tiles(T, 512)
        mo = mqk.rearrange("p (b t) n -> p b t n", b=2)[:, 0]
        rtmp = arena[:, 0:512]
        c1b = carve()
        ro = c1b.tiles(T, D)
        sga = c1b.tiles(T, D)
        sgb = c1b.tiles(T, D)
        normed = c1b.tiles(T, D)
        cf = carve()
        fqT = cf.tiles(8, S)
        fkT = cf.tiles(8, S)
        fv = cf.tiles(T, D)
        fg = cf.tiles(4, S)[0:FOX_H]
        fo = cf.tiles(T, D)
        fsel_raw = fo.rearrange("p t (h n) -> p (t h) n", n=P)
        cm = carve()
        kT = cm.tiles(MLA_H, S)
        vv = cm.tiles(T, MLA_H * VD)
        krT = cm(S)
        cq_ = cm(2 * 512)
        cq = cq_[:, 0:T * QL].rearrange("p (t n) -> p t n", t=T)
        mlo = cq_.rearrange("p (b t n) -> p b t n", b=2, t=T)
        kr = cm.tiles(T, 2 * ROPE_D)
        qs = cm.tiles(T, 384)
        qT = cm(2 * 3 * S).rearrange("p (b k n) -> p b k n", b=2, k=3)
        cp = carve()
        pp = cp.tiles(T, D)
        pz = cp.tiles(T, CH)
        pb = cp(D)

        bank = [ctx.enter_context(nc.psum_tensor(f"bank{b}", [P, CH], F32))[:, :] for b in range(4)]
        acc_t = ctx.enter_context(nc.psum_tensor("acc", [P, T, D], F32))
        acc = acc_t[:, :, :]
        bank += [acc[:, b // 2, (b % 2) * CH:(b % 2 + 1) * CH] for b in range(4)]

        w_loaded = [sem(f"w_loaded{s}") for s in range(RING)]
        w_hi_done, w_used = sem("w_hi_done"), sem("w_used")
        w_lo_done = [sem(f"w_lo_done{s}") for s in range(RING)]
        pe_done, act_done, dve_done = sem("pe_done"), sem("act_done"), sem("dve_done")
        x_loaded = [sem(f"x_loaded{t}") for t in range(T)]
        ident_loaded, const_loaded = sem("ident_loaded"), sem("const_loaded")
        gb_loaded, out_stored = sem("gb_loaded"), sem("out_stored")
        p_loaded, aux_loaded, eps_set = sem("p_loaded"), sem("aux_loaded"), sem("eps_set")
        tanh_done = sem("tanh_done")
        hid_part, hid_done = sem("hid_part"), sem("hid_done")
        hT_hi, hT_lo = sem("hT_hi"), sem("hT_lo")

        counts = {"pe_done": 0, "act_done": 0, "dve_done": 0}
        seen = {}

        def mark(name, *label):
            counts[name] += 1
            if label:
                assert label not in found, label
                found[label] = (name, counts[name])
            return 1

        def note(label, name, value):
            assert label not in found, label
            found[label] = (name, value)

        def need(eng, *label):
            if not marks:
                return
            name, value = marks[label]
            if seen.get((eng, name), 0) < value:
                seen[(eng, name)] = value
                ENG[eng].wait_ge(sems[name], value)

        ENG = {}
        block = ctx.enter_context(nc.Block())

        def bcast_rows(src, n):
            return src.rearrange("(a n) -> a n", a=1).broadcast_to([P, n])

        CONSTS = [("head_q", head_w[:, 0]), ("head_k", head_w[:, 1]),
                  ("rope_ret", rope_ret), ("mask", pr[:, 0, 0:P]), ("decay", decay), ("rope_mla", rope_mla),
                  ("fox_b", fox_b)]
        const_src = {n: dram[n] for n in ("mask",)}
        const_src["decay"] = dram["decay"].rearrange("p (h n) -> p h n", h=RET_H)
        for n in ("rope_ret", "rope_mla"):
            const_src[n] = dram[n].rearrange("p (t n) -> p t n", t=T)
        const_src["head_q"] = bcast_rows(dram["q_norm_w"], MOBA_DH)
        const_src["head_k"] = bcast_rows(dram["k_norm_w"], MOBA_DH)
        const_src["fox_b"] = dram["fox_b_f"].rearrange("(h a) -> h a", a=1)
        N_CONST = 16 * len(CONSTS)

        @block.sync
        def _(sp):
            def store_x(t):
                sp.dma_start(dram["out"][t * P:(t + 1) * P, :], x[:, t, :]).then_inc(out_stored, 16)

            ENG["sp"] = sp

            def load(u):
                _, kt, n, halves = units[u]
                slot = w_raw[u % RING][:, 0:kt * n].rearrange("p (k n) -> p k n", k=kt)
                if u >= RING:
                    sp.wait_ge(w_lo_done[u % RING], u // RING)
                for (k0, k1), (n0, n1), src in halves:
                    sp.dma_start(slot[:, k0:k1, n0:n1], src).then_inc(w_loaded[u % RING], 16)

            def load_ffn(f):
                u0 = unit_at[f"ffn{f}"][0]
                gate, up, down = ffn_w[f]

                def columns(m, u_slot, need_lo, i):
                    if need_lo is not None:
                        sp.wait_ge(w_lo_done[u_slot], need_lo)
                    slot = w_raw[u_slot][:, :].rearrange("p (k n) -> p k n", k=KD)
                    src = m.rearrange("(k p) n -> p k n", p=P)
                    for k in (0, KD // 2):
                        sp.dma_start(slot[:, k:k + KD // 2], src[:, k:k + KD // 2, bass.ds(i * HB, HB)])\
                            .then_inc(w_loaded[u_slot], 16)

                def down_rows(u_slot, need_lo, i):
                    sp.wait_ge(w_lo_done[u_slot], need_lo)
                    slot = w_raw[u_slot][:, :].rearrange("p (k n) -> p k n", k=2)
                    for k in range(2):
                        sp.dma_start(slot[:, k], down[bass.ds(i * HB + k * P, P), :]).then_inc(w_loaded[u_slot], 16)

                columns(gate, u0 % RING, u0 // RING, 0)
                columns(up, (u0 + 1) % RING, (u0 + 1) // RING, 0)
                with sp.Fori(1, FI) as i:
                    columns(gate, (u0 + 2) % RING, i + (u0 - 1) // RING, i)
                    columns(up, u0 % RING, i + u0 // RING, i)
                    down_rows((u0 + 1) % RING, i + (u0 + 1) // RING, i - 1)
                u = u0 + 3 * FI - 1
                down_rows(u % RING, u // RING, FI - 1)

            for t in range(T):
                sp.dma_start(x[:, t], dram["x"][t * P:(t + 1) * P, :]).then_inc(x_loaded[t], 16)
            u = 0
            while u < N_UNITS:
                if units[u][3] is None:
                    load_ffn(int(units[u][0][3:]))
                    u += 3 * FI
                else:
                    load(u)
                    u += 1
                if u == 2:
                    for name, dst in CONSTS:
                        sp.dma_start(dst, const_src[name]).then_inc(const_loaded, 16)
            for t in range(T):
                need("sp", "norm", 9, t, 1)
                store_x(t)
            sp.wait_ge(out_stored, 16 * T)

        norm_src = [(dram["norm1_w"], None), (dram["norm2_w"], None)] + \
                   [(dram["ln_g"][l, j], dram["ln_b"][l, j]) for l in range(2) for j in range(4)]

        @block.gpsimd
        def _(pool):
            ENG["pool"] = pool
            pool.memset(eps[:, 0:1], LN_EPS).then_inc(eps_set, 1)
            pool.memset(eps[:, 1:2], RMS_EPS).then_inc(eps_set, 1)
            for u, unit in enumerate(units):
                if u in pool_units:
                    cols, slot = unit[1] * unit[2] or UNIT, u % RING
                    pool.wait_ge(w_hi_done, u + 1)
                    pool.tensor_tensor(w_lo[slot][:, 0:cols], w_raw[slot][:, 0:cols],
                                       w_hi[slot][:, 0:cols].bitcast(F32), ALU.subtract).then_inc(w_lo_done[slot], 1)

        def gb_count(site):
            return 16 * (site + 1) if site < 2 else 32 * site

        def site_ready(site, t, q):
            return {"ret": ("gated", q, t), "moba": ("o", "moba", MOBA_H - 1), "mix": ("ev", f"moba_out{q}", t),
                    "fox": ("o", "fox", 8 * q + 7), "raw": ("ffn_out", 0, t)}.get(site, ("norm", site, t, q))

        O_BANK = [2, 3, 2, 3, 2, 1, 0, 1]

        def q_bank(g):
            return 0 if g else 4

        FOX_FILL = {0: ("fox_q1", 0), 2: ("fox_k1", 1), 3: ("fox_q2", 2), 4: ("fox_k2", 3), 8: ("fox_q3", 2),
                    9: ("fox_k3", 3)}

        @block.tensor
        def _(pe):
            ENG["pe"] = pe
            freed = {b: None for b in range(8)}

            def take(b, label):
                if freed[b]:
                    need("pe", *freed[b])
                freed[b] = label

            def transposes(b, free, label, pairs):
                take(b, free)
                for c, src in pairs:
                    mm = pe.matmul(bank[b][:, c:c + P], src, ident, is_transpose=True, start=True, stop=True)
                mm.then_inc(pe_done, mark("pe_done", *label))

            def mm3(out, ah, al, bh, bl, first, last):
                pe.matmul(out, ah, bh, start=first, stop=False)
                pe.matmul(out, ah, bl, start=False, stop=False)
                return pe.matmul(out, al, bh, start=False, stop=last)

            class Chunk:

                def __init__(self, stage, banks, src=None, slot0=0, half=None, ready=None):
                    self.us = unit_at[stage] if half is None else [unit_at[stage][half[0]]]
                    self.name = (stage,) if half is None else (stage, half[0] * 2 + half[1])
                    self.ah, self.al = src or (xTh, xTl)
                    self.banks, self.slot0, self.half, self.ready = banks, slot0, half, ready
                    self.kts = [units[u][1] for u in self.us]

                def run(self, *which, tiles=range(T)):
                    last = len(self.us) - 1
                    for t in tiles:
                        if which[0] == 0:
                            take(self.banks[t], ("ev", *self.name, t))
                        for w in which:
                            u, kt = self.us[w], self.kts[w]
                            n = units[u][2]
                            if t == 0:
                                pe.wait_ge(w_lo_done[u % RING], u // RING + 1)
                            wh, wl = (m[u % RING][:, 0:kt * n].rearrange("p (k n) -> p k n", k=kt)
                                      for m in (w_hi, w_lo))
                            c0 = 0 if self.half is None else self.half[1] * CH
                            cols = slice(c0, c0 + min(n, CH))
                            for j in range(kt):
                                k = sum(self.kts[:w]) + j
                                if self.ready is not None:
                                    need("pe", "xT", self.ready, t, k // 4)
                                a, tok = self.slot0 + k, slice(t * P, (t + 1) * P)
                                mm = mm3(bank[self.banks[t]][:, 0:cols.stop - cols.start], self.ah[:, a, tok],
                                         self.al[:, a, tok], wh[:, j, cols], wl[:, j, cols],
                                         w == 0 and j == 0, w == last and j == kt - 1)
                            if t == 0 and w == last:
                                mm.then_inc(pe_done, mark("pe_done", "full", *self.name, 0))
                            if t == 1 and (self.half is None or self.half[1] == 1):
                                mm.then_inc(w_used, 1)
                                if w == last:
                                    note(("full", *self.name, 1), "w_used", u + 1)
                            elif t == 1:
                                mm.then_inc(pe_done, mark("pe_done", "full", *self.name, 1))

            def chunk(stage, banks, src=None, slot0=0, half=None, ready=None):
                c = Chunk(stage, banks, src, slot0, half, ready)
                c.run(*range(len(c.us)))

            def tile_steps(stage, banks, **kw):
                c = Chunk(stage, banks, **kw)
                return [lambda: c.run(0, tiles=(0,)), lambda: c.run(1, tiles=(0,)), lambda: c.run(0, 1, tiles=(1,))]

            def unit_steps(stage, banks, **kw):
                c = Chunk(stage, banks, **kw)
                return [(lambda w=w: c.run(w)) for w in range(len(c.us))]

            def to_xT(site, src, qs_=(0, 1), b0=0, between=None):
                for t in range(T):
                    if t and between:
                        between()
                    for q in qs_:
                        need("pe", *site_ready(site, t, q))
                        transposes(b0 + t * len(qs_) + q - qs_[0], ("xT", site, t, q), ("T", site, t, q),
                                   [(j * P, src[:, t, (4 * q + j) * P:(4 * q + j + 1) * P]) for j in range(4)])

            def need_xT(site, qs_=(0, 1)):
                for t in range(T):
                    for q in qs_:
                        need("pe", "xT", site, t, q)

            def ffn(f, site, src=None, mid=None):
                u0 = unit_at[f"ffn{f}"][0]
                g0 = f * FI
                assert 3 * FI == len(unit_at[f"ffn{f}"])

                def wide(slot, split, b):
                    pe.wait_ge(w_lo_done[slot], split)
                    wh, wl = (w[slot][:, :].rearrange("p (k m n) -> p k m n", k=KD, m=2) for w in (w_hi, w_lo))
                    for m in range(2):
                        for k in range(KD):
                            mm = mm3(bank[b][:, m * S:(m + 1) * S], wh[:, k, m], wl[:, k, m], xTh[:, k], xTl[:, k],
                                     k == 0, k == KD - 1)
                    mm.then_inc(w_used, 1)

                def first(b, t):
                    u = u0 + b
                    if t == 0:
                        pe.wait_ge(w_lo_done[u % RING], u // RING + 1)
                    wh, wl = (w[u % RING][:, :].rearrange("p (k n) -> p k n", k=KD) for w in (w_hi, w_lo))
                    for k in range(KD):
                        need("pe", "xT", site, t, k // 4)
                        tok = slice(t * P, (t + 1) * P)
                        mm = mm3(bank[b][:, t * HB:(t + 1) * HB], xTh[:, k, tok], xTl[:, k, tok], wh[:, k], wl[:, k],
                                 k == 0, k == KD - 1)
                    if t == 1:
                        mm.then_inc(w_used, 1)

                def turn_first():
                    pe.wait_ge(hid_done, g0 + 1)
                    transposes(3, ("hT0", f), ("hT0f", f),
                               [(m * S + t * P, hid[:, t, m * P:(m + 1) * P]) for m in range(2) for t in range(T)])

                def down(slot, split, hh, hl, first, last, tiles=range(T)):
                    if tiles[0] == 0:
                        pe.wait_ge(w_lo_done[slot], split)
                    wh, wl = (w[slot][:, :].rearrange("p (k n) -> p k n", k=2) for w in (w_hi, w_lo))
                    for t in tiles:
                        tok = slice(t * P, (t + 1) * P)
                        for n in range(2):
                            cols = slice(n * CH, (n + 1) * CH)
                            for k in range(2):
                                mm = mm3(acc[:, t, cols], hh[:, k, tok], hl[:, k, tok], wh[:, k, cols],
                                         wl[:, k, cols], first and k == 0, last and k == 1)
                            if last and (t, n) != (1, 1):
                                mm.then_inc(pe_done, mark("pe_done", "ffn_full", f, t, n))
                    if tiles[-1] == T - 1:
                        mm.then_inc(w_used, 1)

                def start():
                    for b in range(2):
                        take(b, ("ffn_out", f, 0))
                    first(0, 0)

                if src is None:
                    start()
                else:
                    to_xT(site, src, b0=4, between=start)
                for b, t in ((1, 0), (0, 1), (1, 1)):
                    first(b, t)
                if mid:
                    mid()

                def step(i, first=False):
                    pe.wait_ge(hid_part, i + g0)
                    wide((u0 + 2) % RING, i + ((u0 - 1) // RING + 1), 0)
                    if first:
                        turn_first()
                    pe.wait_ge(hid_done, i + g0)
                    wide(u0 % RING, i + (u0 // RING + 1), 1)
                    pe.wait_ge(hT_lo, i + g0)
                    if not isinstance(i, int) or i < FI - 1:
                        down((u0 + 1) % RING, i + ((u0 + 1) // RING + 1), hTh, hTl, first, False)

                for b in range(4, 8):
                    take(b, ("ffn_out", f, b // 2 - 2))
                step(1, True)
                with pe.Fori(2, FI - 1) as i:
                    step(i)
                step(FI - 1)
                u = u0 + 3 * FI - 2
                for t in range(T):
                    down(u % RING, u // RING + 1, hTh, hTl, False, False, (t,))
                    if t == 0:
                        pe.wait_ge(hT_lo, g0 + FI)
                    down((u + 1) % RING, (u + 1) // RING + 1, hLh, hLl, False, True, (t,))
                note(("ffn_full", f, 1, 1), "w_used", u + 2)

            def attention(name, heads, qk, v, dv, fill):
                def scores(h):
                    take(4 + h % 2, ("exp", name, h))
                    b = bank[4 + h % 2]
                    for t in range(T):
                        c0 = t * P
                        out = b[:, c0:c0 + (t + 1) * P]
                        pe.matmul(out, ident_r, mask_r[:, P - c0:], start=True, stop=False)
                        *more, (q, k, _) = qk(h, t)
                        for a, b_, n in more:
                            pe.matmul(out if n is None else out.rearrange("p (a n) -> p a n", a=n), a, b_,
                                      start=False, stop=False)
                        mm = pe.matmul(out, q, k, start=False, stop=True)
                    mm.then_inc(pe_done, mark("pe_done", "S", name, h))

                def turn(h):
                    need("pe", "exp", name, h)
                    transposes(6, ("pT", name, h), ("PT", name, h),
                               [(c * P, pr[:, h % 2, c * P:(c + 1) * P]) for c in range(3)])

                def weigh(h):
                    take(7, ("o", name, h))
                    need("pe", "pT", name, h)
                    b, p = bank[7], pT[:, h % 2]
                    pe.matmul(b[:, 0:dv], p[:, 0:P], v(h, 0), start=True, stop=True)
                    pe.matmul(b[:, dv:2 * dv], p[:, P:2 * P], v(h, 0), start=True, stop=False)
                    pe.matmul(b[:, dv:2 * dv], p[:, 2 * P:3 * P], v(h, 1), start=False, stop=True)\
                        .then_inc(pe_done, mark("pe_done", "PV", name, h))

                for s in range(heads + 2):
                    if s < heads:
                        scores(s)
                    if 1 <= s <= heads:
                        turn(s - 1)
                    if s >= 2:
                        weigh(s - 2)
                    for work in fill.get(s, ()):
                        work()

            def tok(t):
                return slice(t * P, (t + 1) * P)

            def pair(h):
                return slice(64 * (h % 2), 64 * (h % 2) + 64)

            def turn_qk(name, src):
                for i in range(2):
                    for t in range(T):
                        need("pe", name, i, t)
                        transposes(4 + 2 * i + t, ("qkT", name, i, t), ("qkTf", name, i, t),
                                   [(j * P, src[:, 2 * i + t, j * P:(j + 1) * P]) for j in range(4)])

            pe.wait_ge(ident_loaded, 16)
            rq = tile_steps("rq0", (0, 1), ready=0)
            to_xT(0, normed, b0=4, between=rq[0])
            rq[1]()
            rq[2]()
            chunk("rk0", (2, 3))
            chunk("rv0", (0, 1))
            chunk("rv1", (2, 3))
            turn_qk("rot", rqk)
            for h, stage in enumerate(("mq0", "mk0", "mv0", "rg0", "rg1")):
                if h == 0:
                    chunk(stage, (0, 1))
                    for i in range(2):
                        for t in range(T):
                            need("pe", "qkT", "rot", i, t)
                if h < RET_H:
                    take(4 + h % 2, ("decayed", h))
                    b = bank[4 + h % 2]
                    pe.matmul(b[:, 0:S], rkT[:, h, 0:P], rqT[:, h, :], start=True, stop=True)
                    pe.matmul(b[:, S:S + P], rkT[:, h, P:S], rqT[:, h, P:S], start=True, stop=True)\
                        .then_inc(pe_done, mark("pe_done", "RS", h))
                if h >= 1:
                    g = h - 1
                    take(6 + g % 2, ("ro", g))
                    need("pe", "decayed", g)
                    need("pe", "ev", "rv1", 1)
                    b, s = bank[6 + g % 2], pT[:, g % 2]
                    v = [rv[:, t, g * RET_DV:(g + 1) * RET_DV] for t in range(T)]
                    pe.matmul(b[:, 0:RET_DV], s[:, 0:P], v[0], start=True, stop=True)
                    pe.matmul(b[:, RET_DV:], s[:, P:2 * P], v[0], start=True, stop=False)
                    pe.matmul(b[:, RET_DV:], s[:, 2 * P:3 * P], v[1], start=False, stop=True)\
                        .then_inc(pe_done, mark("pe_done", "RO", g))
                if h:
                    chunk(stage, ((0, 1), (2, 3))[h % 2])
            turn_qk("mnorm", mqk)
            ga0, ga1, gb0, gb1 = (unit_steps(f"{n}{c}", ((2, 3), (0, 1))[c]) for n in ("ga", "gb") for c in range(2))
            ga0[0]()
            for i in range(2):
                for t in range(T):
                    need("pe", "qkT", "mnorm", i, t)
            need("pe", "ev", "mv0", 1)
            attention("moba", MOBA_H, lambda h, t: [(mqT[pair(h), h // 2, tok(t)], mkT[pair(h), h // 2, 0:(t + 1) * P], None)],
                      lambda h, t: mv[:, t, h * MOBA_DH:(h + 1) * MOBA_DH], MOBA_DH,
                      {0: [ga0[1]], 1: [ga1[0]], 2: [ga1[1]], 3: [gb0[0]], 4: [gb0[1], lambda: to_xT("ret", ro, (0,))],
                       6: [lambda: to_xT("ret", ro, (1,), b0=2)], 8: [gb1[0]], 9: [gb1[1]]})
            need_xT("ret")
            chunk("ret_out0", (2, 3), slot0=8)
            to_xT("moba", mo, (0,), b0=4)
            chunk("ret_out1", (0, 1), slot0=8)
            need_xT("moba", (0,))
            chunk("moba_out0", (0, 1))
            moba_out1 = Chunk("moba_out1", (2, 3))
            w_o0 = Chunk("w_o0", (0, 1), slot0=8, ready="mix")
            moba_out1.run(0, tiles=(0,))
            to_xT("mix", sga, (0,), b0=4)
            moba_out1.run(0, tiles=(1,))
            w_o0.run(0, tiles=(0,))
            to_xT("mix", sga, (1,), b0=6)
            w_o0.run(0, tiles=(1,))
            w_o0.run(1)
            chunk("w_o1", (2, 3), slot0=8)
            ffn(0, 1, normed)
            for l in range(2):

                def turn_ckv():
                    for t in range(T):
                        need("pe", "ckv", t)
                        take(2 + t, ("ckvT", t))
                        for c in range(3):
                            src = cq[:, t, c * P:(c + 1) * P] if c < 2 else kr[:, t, :]
                            mm = pe.matmul(bank[2 + t][:, c * P:(c + 1) * P], src, ident, is_transpose=True,
                                           start=True, stop=True)
                        mm.then_inc(pe_done, mark("pe_done", "ckvTf", t))

                ffn(1 + 2 * l, ("raw", 5)[l], (x, None)[l], turn_ckv if l else None)

                def kv(c):
                    u = unit_at["kv_up"][c]
                    pe.wait_ge(w_lo_done[u % RING], u // RING + 1)
                    wh, wl = (w[u % RING][:, :].rearrange("p (k h a n) -> p k h a n", k=2, h=4, a=2)
                              for w in (w_hi, w_lo))
                    for t in range(T):
                        need("pe", "ckvT", t)
                    for i in range(2):
                        take(i, ("kT", c, i))
                        for h in range(2):
                            for k in range(2):
                                mm = mm3(bank[i][:, h * S:(h + 1) * S], wh[:, k, 2 * i + h, 0], wl[:, k, 2 * i + h, 0],
                                         cTh[:, k], cTl[:, k], k == 0, k == 1)
                        mm.then_inc(pe_done, mark("pe_done", "kTf", c, i))
                    for t in range(T):
                        take(2 + t, ("vv", c, t))
                        for k in range(2):
                            mm = mm3(bank[2 + t].rearrange("p (h n) -> p h n", h=4), cTh[:, k, tok(t)],
                                     cTl[:, k, tok(t)], wh[:, k, :, 1], wl[:, k, :, 1], k == 0, k == 1)
                        if t == 0:
                            mm.then_inc(pe_done, mark("pe_done", "vf", c, 0))
                    mm.then_inc(w_used, 1)
                    note(("vf", c, 1), "w_used", u + 1)

                if l == 0:
                    v4 = tile_steps("fox_v4", (2, 3), ready=2)
                    to_xT(2, x, b0=4, between=v4[0])
                else:
                    to_xT(6, x, b0=4, between=lambda: kv(0))
                if l == 0:
                    v4[1]()
                    v4[2]()
                    u = unit_at["fox_f"][0]
                    take(4, ("fz",))
                    pe.wait_ge(w_lo_done[u % RING], u // RING + 1)
                    wh, wl = (w[u % RING][:, 0:KD * FOX_H].rearrange("p (k n) -> p k n", k=KD) for w in (w_hi, w_lo))
                    for k in range(KD):
                        for t in range(T):
                            need("pe", "xT", 2, t, k // 4)
                        mm = mm3(bank[4][0:FOX_H, 0:S], wh[:, k], wl[:, k], xTh[:, k], xTl[:, k], k == 0, k == KD - 1)
                    mm.then_inc(w_used, 1)
                    note(("fox_f",), "w_used", u + 1)

                    def turned(stage, b):
                        u = unit_at[stage][0]
                        take(b, ("fT", stage))
                        pe.wait_ge(w_lo_done[u % RING], u // RING + 1)
                        wh, wl = (w[u % RING][:, :].rearrange("p (k m n) -> p k m n", k=KD, m=2) for w in (w_hi, w_lo))
                        for m in range(2):
                            for k in range(KD):
                                mm = mm3(bank[b][:, m * S:(m + 1) * S], wh[:, k, m], wl[:, k, m], xTh[:, k],
                                         xTl[:, k], k == 0, k == KD - 1)
                        mm.then_inc(w_used, 1)
                        note(("full", stage), "w_used", u + 1)

                    turned("fox_q0", 0)
                    turned("fox_k0", 1)
                    need("pe", "cum")
                    need("pe", "fsel")

                    def fox_qk(h, t):
                        need("pe", "fT", f"fox_q{h // 4}")
                        need("pe", "fT", f"fox_k{h // 4}")
                        keys, n = slice(0, (t + 1) * P), t + 1
                        rows = fsel[:, h, :].unsqueeze(1).broadcast_to([FOX_K, n, P])
                        return [(fsel[:, h, :], cTh[0:FOX_K, 0, keys], None),
                                (cTh[0:FOX_K, 1, tok(t)], rows, n),
                                (fqT[pair(h), h // 2, tok(t)], fkT[pair(h), h // 2, keys], None)]

                    def fox_v(h, t):
                        need("pe", "ev", f"fox_v{4 + h // 8}", 1)
                        return fv[:, t, h * FOX_DH:(h + 1) * FOX_DH]

                    v5 = unit_steps("fox_v5", (0, 1))
                    o0, o1 = (unit_steps(f"fox_o{c}", b) for c, b in ((0, (0, 1)), (1, (2, 3))))
                    fill = {s: [lambda a=a: turned(*a)] for s, a in FOX_FILL.items()}
                    fill |= {5: [v5[0]], 6: [v5[1]], 11: [lambda: to_xT("fox", fo, (0,), b0=2)],
                             15: [lambda: need_xT("fox", (0,)), o0[0]], 16: [o1[0]]}
                    attention("fox", FOX_H, fox_qk, fox_v, FOX_DH, fill)
                    for t in range(T):
                        need("pe", *site_ready("fox", t, 1))
                        transposes(4 + t, ("xT", "fox", t, 1), ("T", "fox", t, 1),
                                   [(j * P, fo[:, t, (4 + j) * P:(5 + j) * P]) for j in range(4)])
                    need_xT("fox", (1,))
                    o0[1]()
                    o1[1]()
                else:
                    kv(1)
                    chunk("dq0", (4, 5), ready=6)
                    kv(2)
                    for t in range(T):
                        need("pe", "cqn", t)
                        take(6 + t, ("cqT", t))
                        for c in range(3):
                            mm = pe.matmul(bank[6 + t][:, c * P:(c + 1) * P], cq[:, t, c * P:(c + 1) * P], ident,
                                           is_transpose=True, start=True, stop=True)
                        mm.then_inc(pe_done, mark("pe_done", "cqTf", t))
                    for t in range(T):
                        need("pe", "cqT", t)

                    def uq(g):
                        u = unit_at["uq"][g]
                        pe.wait_ge(w_lo_done[u % RING], u // RING + 1)
                        wh, wl = (w[u % RING][:, 0:3 * QL].rearrange("p (k n) -> p k n", k=3) for w in (w_hi, w_lo))
                        for t in range(T):
                            take(q_bank(g) + t, ("qs", g, t))
                            for j in range(3):
                                mm = mm3(bank[q_bank(g) + t][:, 0:QL], cqTh[:, j, tok(t)], cqTl[:, j, tok(t)], wh[:, j],
                                         wl[:, j], j == 0, j == 2)
                            if t == 0:
                                mm.then_inc(pe_done, mark("pe_done", "qf", g, 0))
                        mm.then_inc(w_used, 1)
                        note(("qf", g, 1), "w_used", u + 1)

                    def turn_q(g):
                        for t in range(T):
                            need("pe", "qs", g, t)
                            transposes(q_bank(g) + t, ("qT", g, t), ("qTf", g, t),
                                       [(j * P, qs[:, t, j * P:(j + 1) * P]) for j in range(3)])

                    def turn_o(g):
                        need("pe", "o", "mla", 2 * g + 1)
                        transposes(O_BANK[g], ("oT", g), ("oTf", g),
                                   [(j * S + t * P, mlo[:, g % 2, t, j * VD:(j + 1) * VD])
                                    for t in range(T) for j in range(2)])

                    def mla_qk(h, t):
                        g, keys = h // 2, slice(0, (t + 1) * P)
                        need("pe", "qT", g, 0)
                        need("pe", "qT", g, 1)
                        return [(qT[:, g % 2, h % 2, tok(t)], kT[:, h, keys], None),
                                (qT[pair(h), g % 2, 2, tok(t)], krT[pair(h), keys], None)]

                    uq(0)
                    kv(3)
                    turn_q(0)
                    uq(1)
                    for c in range(4):
                        for i in range(2):
                            need("pe", "kT", c, i)
                            need("pe", "vv", c, i)
                    fill = {s: [] for s in range(MLA_H + 2)}
                    for g in range(7):
                        fill[2 * g + 4].append(lambda g=g: turn_o(g))
                    for g in range(1, 8):
                        fill[2 * g - 2].append(lambda g=g: turn_q(g))
                    for g in range(2, 8):
                        fill[2 * g - 3].append(lambda g=g: uq(g))
                    oa = [unit_steps(f"mla_oa{c}", (2, 3)) for c in range(2)]
                    fill[13] += [lambda: [need("pe", "oT", g) for g in range(4)], oa[0][0]]
                    fill[15].append(oa[0][1])
                    fill[16].append(oa[1][0])
                    fill[17].append(oa[1][1])
                    attention("mla", MLA_H, mla_qk, lambda h, t: vv[:, t, h * VD:(h + 1) * VD], VD, fill)
                    ob = tile_steps("mla_ob0", (4, 5), slot0=8)
                    need("pe", "oT", 4)
                    need("pe", "oT", 5)
                    ob[0]()
                    turn_o(7)
                    need("pe", "oT", 6)
                    need("pe", "oT", 7)
                    ob[1]()
                    ob[2]()
                    chunk("mla_ob1", (2, 3), slot0=8)
                pe.wait_ge(p_loaded, 16 * (l + 1))
                transposes(2, ("pT", l), ("pTf", l),
                           [(j * S + t * P, pin[:, t, j * P:(j + 1) * P]) for t in range(T) for j in range(2)])
                ffn(2 + 2 * l, 3 + 4 * l, x)
                need("pe", "pT", l)

                def ple_p(c):
                    chunk(f"ple_p{l}", ((4, 5), (6, 7))[c], src=(cTh, cTl), half=(0, c))

                ple_g = tile_steps(f"ple_g{l}0", (0, 1), ready=4 + 4 * l)

                def between():
                    ple_p(1)
                    ple_g[0]()

                ple_p(0)
                to_xT(4 + 4 * l, x, between=between)
                ple_g[1]()
                ple_g[2]()
                chunk(f"ple_g{l}1", (2, 3))
                if l == 0:
                    kv_down = tile_steps("kv_down0", (4, 5), ready=5)
                    to_xT(5, x, between=kv_down[0])
                    kv_down[1]()
                    kv_down[2]()

        @block.scalar
        def _(act):
            ENG["act"] = act
            split = [0]

            def split_to(n):
                while split[0] < min(n, N_UNITS):
                    u = split[0]
                    cols = units[u][1] * units[u][2] or UNIT
                    act.wait_ge(w_loaded[u % RING], 32 * (u // RING + 1))
                    if u >= RING:
                        act.wait_ge(w_used, u - RING + 1)
                    nc.scalar.activation(w_hi[u % RING][:, 0:cols], w_raw[u % RING][:, 0:cols], ACT.Copy)\
                        .then_inc(w_hi_done, 1)
                    split[0] += 1

            def ahead(stage, part=None):
                us = unit_at[stage]
                split_to((us[-1] if part is None else us[part]) + RING)

            def go(label, out, in_, func=ACT.Copy, **kw):
                nc.scalar.activation(out, in_, func, **kw).then_inc(act_done, mark("act_done", *label))

            def xT_evac(site, qs_=(0, 1), slot0=0, b0=0, scale=1.0, tiles=range(T)):
                for t in tiles:
                    for q in qs_:
                        need("act", "T", site, t, q)
                        b = b0 + t * len(qs_) + q - qs_[0]
                        go(("xTh", site, t, q), xTh[:, slot0 + 4 * q:slot0 + 4 * q + 4, t * P:(t + 1) * P],
                           bank[b].rearrange("p (k n) -> p k n", k=4), scale=scale)

            def load_norm(site):
                if site:
                    need("act", "norm", site - 1, 1, 1)
                g, b = norm_src[site]
                act.dma_start(gb[:, 0, :], bcast_rows(g, D)).then_inc(gb_loaded, 16)
                if b is not None:
                    act.dma_start(gb[:, 1, :], bcast_rows(b, D)).then_inc(gb_loaded, 16)

            def root_table():
                go((), unused, eps[:, 0:1], ACT.Sqrt)

            def squares_sum(site, t, rms):
                if site == 0:
                    act.wait_ge(x_loaded[t], 16)
                else:
                    need("act", *(("sum", site, t) if rms else ("mean", site, t)))
                act.wait_ge(act_done, counts["act_done"])
                go((), squares, x[:, t], ACT.Square, bias=0.0 if rms else neg_mean[:, t:t + 1],
                   accum_out=sq_sum[:, t:t + 1])

            def root(site, t, rms):
                act.wait_ge(act_done, counts["act_done"])
                e = 1 if rms else 0
                go(("std", site, t), std[:, t:t + 1], sq_sum[:, t:t + 1], ACT.Sqrt, bias=eps[:, e:e + 1], scale=1.0 / D)

            def norm_and_turn(site, rms=False, first=None, early=None, between=None, b0=0):
                squares_sum(site, 0, rms)
                root(site, 0, rms)
                if first is not None:
                    first()
                if early is not None:
                    split_to(early)
                if site < 9:
                    xT_evac(site, b0=b0, tiles=(0,))
                squares_sum(site, 1, rms)
                root(site, 1, rms)
                if site < 9:
                    if between is not None:
                        between()
                    xT_evac(site, b0=b0, tiles=(1,))

            def load_p(l):
                act.dma_start(pin, dram["p"][l].rearrange("(t p) n -> p t n", p=P)).then_inc(p_loaded, 16)

            def ffn(f, mid=None):
                u0 = unit_at[f"ffn{f}"][0]
                g0 = f * FI

                def split_unit(slot, loaded, used):
                    act.wait_ge(w_loaded[slot], loaded)
                    act.wait_ge(w_used, used)
                    nc.scalar.activation(w_hi[slot][:, :], w_raw[slot][:, :], ACT.Copy).then_inc(w_hi_done, 1)

                def half_tanh(i, used):
                    act.wait_ge(w_used, used)
                    nc.scalar.activation(tanh[:, 0], bank[0], ACT.Tanh, scale=0.5).then_inc(tanh_done, 1)

                def hT_round(i, used, dst):
                    act.wait_ge(hid_done, i + (g0 + 1))
                    if used is not None:
                        act.wait_ge(w_used, used)
                    nc.scalar.activation(dst, hid, ACT.Copy).then_inc(hT_hi, 1)

                def step(i, last=False):
                    s, n = (u0 + 4) % RING, (u0 + 4) // RING
                    split_unit(s, i * 32 + 32 * n, i * 3 + (u0 - 1))
                    half_tanh(i, i * 3 + u0)
                    s, n = (u0 + 5) % RING, (u0 + 5) // RING
                    split_unit(s, i * 32 + 32 * n, i * 3 + u0)
                    if last:
                        hT_round(i, None, hLh)
                        return
                    s, n = (u0 + 6) % RING, (u0 + 6) // RING
                    split_unit(s, i * 32 + 32 * n, i * 3 + (u0 + 1))
                    hT_round(i, i * 3 + (u0 + 2), hTh)

                split_to(u0 + 3)
                half_tanh(0, u0 + 1)
                split_to(u0 + 4)
                if mid:
                    mid()
                need("act", "hT0f", f)
                nc.scalar.activation(hTh, bank[3].rearrange("p (k n) -> p k n", k=2), ACT.Copy).then_inc(hT_hi, 1)
                with act.Fori(1, FI - 1) as i:
                    step(i)
                step(FI - 1, True)
                if f:
                    root_table()
                split[0] = u0 + 3 * FI
                split_to(u0 + 3 * FI + 1)

            def attention(name, heads, scale, fill):
                def exps(h):
                    need("act", "soft", name, h)
                    s = 2 * (h % 4)
                    b = bank[4 + h % 2]
                    for t in range(T):
                        c = slice(0, P) if t == 0 else slice(P, 3 * P)
                        go(("exp", name, h) if t else (), pr[:, h % 2, c], b[:, c], ACT.Exp,
                           bias=negmax[:, s + t:s + t + 1], scale=scale, accum_out=psum_e[:, s + t:s + t + 1])

                def turned(h):
                    need("act", "PT", name, h)
                    go(("pT", name, h), pT[:, h % 2], bank[6][:, 0:3 * P])

                for s in range(heads + 3):
                    for work in fill.get(s - 1, ()):
                        work()
                    if s < heads:
                        exps(s)
                    if 1 <= s <= heads:
                        turned(s - 1)

            def copy_chunk(stage, banks, dst):
                for t in range(T):
                    need("act", "full", stage, t)
                    go(("ev", stage, t), dst(t), bank[banks[t]])

            load_norm(0)
            act.dma_start(ident, dram["ident"]).then_inc(ident_loaded, 16)
            act.wait_ge(eps_set, 2)
            root_table()
            norm_and_turn(0, rms=True, early=1, between=lambda: split_to(2), b0=4)
            split_to(3)
            act.wait_ge(const_loaded, N_CONST)
            load_p(0)
            go((), ident_r, ident)
            go((), mask_r[:, 0:P], pr[:, 0, 0:P], scale=0.0)
            go(("mask_r",), mask_r[:, P:], pr[:, 0, 0:P])
            load_norm(1)
            ahead("rq0")
            ahead("rk0")
            for n, stage in enumerate(("rv0", "rv1")):
                ahead(stage)
                copy_chunk(stage, (2 * n, 2 * n + 1), lambda t: rv[:, t, n * CH:(n + 1) * CH])
            for i in range(2):
                for t in range(T):
                    need("act", "qkTf", "rot", i, t)
                    go(("qkT", "rot", i, t), (rqT, rkT)[i][:, :, t * P:(t + 1) * P],
                       bank[4 + 2 * i + t].rearrange("p (k n) -> p k n", k=4))
            for n, stage in enumerate(("mq0", "mk0")):
                ahead(stage)
                for t in range(T):
                    need("act", "full", stage, t)
                    go(("ev", stage, t), mqk[:, 2 * n + t], bank[2 * n + t])
                    act.wait_ge(act_done, counts["act_done"])
                    if n * T + t:
                        need("act", "mss", n * T + t - 1)
                    go(("msq", n, t), tanh[:, 0], mqk[:, 2 * n + t], ACT.Square)

            def keep_ro(h):
                need("act", "rstats", h)
                go(("ro", h), ro[:, :, h * RET_DV:(h + 1) * RET_DV],
                   bank[6 + h % 2].rearrange("p (t n) -> p t n", t=T))

            keep_ro(0)
            ahead("mv0")
            copy_chunk("mv0", (0, 1), lambda t: mv[:, t])
            keep_ro(1)

            def gate(stage, banks, out):
                ahead(stage)
                for t in range(T):
                    need("act", "full", stage, t)
                    go(("tanh", stage, t), out(t), bank[banks[t]], ACT.Tanh, scale=0.5)

            ahead("rg0", 0)
            keep_ro(2)
            gate("rg0", (2, 3), lambda t: tanh[:, t])
            keep_ro(3)
            gate("rg1", (0, 1), lambda t: squares[:, t * CH:(t + 1) * CH])
            for i in range(2):
                for t in range(T):
                    need("act", "qkTf", "mnorm", i, t)
                    go(("qkT", "mnorm", i, t), (mqT, mkT)[i][:, :, t * P:(t + 1) * P],
                       bank[4 + 2 * i + t].rearrange("p (k n) -> p k n", k=4))

            def keep_gate(n, c):
                stage, dst = f"{n}{c}", {"ga": sga, "gb": sgb}[n]
                ahead(stage)
                for t in range(T):
                    need("act", "full", stage, t)
                    go(("ev", stage, t), dst[:, t, c * CH:(c + 1) * CH], bank[(2 - 2 * c) + t], ACT.Tanh, scale=0.5)

            split_to(unit_at["ga0"][0] + RING)
            attention("moba", MOBA_H, MOBA_DH ** -0.5,
                      {0: [lambda: keep_gate("ga", 0)], 1: [lambda: split_to(unit_at["ga1"][0] + RING)],
                       2: [lambda: keep_gate("ga", 1)], 3: [lambda: split_to(unit_at["gb0"][0] + RING)],
                       4: [lambda: keep_gate("gb", 0), lambda: xT_evac("ret", (0,), slot0=8)],
                       6: [lambda: xT_evac("ret", (1,), slot0=8, b0=2)],
                       8: [lambda: split_to(unit_at["gb1"][0] + RING)], 9: [lambda: keep_gate("gb", 1)]})
            ahead("ret_out0")
            xT_evac("moba", (0,), b0=4)
            for stage in ("ret_out1", "moba_out0", "moba_out1"):
                ahead(stage)
            xT_evac("mix", (0,), slot0=8, b0=4, scale=0.5)
            xT_evac("mix", (1,), slot0=8, b0=6, scale=0.5)
            split_to(unit_at["ffn0"][0] + 1)
            root_table()
            norm_and_turn(1, rms=True, early=unit_at["ffn0"][0] + 2, b0=4)
            load_norm(2)
            ffn(0)
            for l in range(2):
                if l == 0:
                    split_to(unit_at["ffn1"][0] + 2)
                    xT_evac("raw", b0=4)
                    act.dma_start(fsel_raw[0:FOX_K], dram["sel"].rearrange("p (h n) -> p h n", h=FOX_H))\
                        .then_inc(aux_loaded, 16)
                if l == 1:
                    ahead("kv_down0")
                    for t in range(T):
                        need("act", "full", "kv_down0", t)
                        go(("kvsq", t), squares[:, t * CH:t * CH + KVL], bank[4 + t][:, 0:KVL], ACT.Square,
                           accum_out=stats[:, t:t + 1])

                def keep_ckv():
                    for t in range(T):
                        need("act", "ckvTf", t)
                        go(("ckvTh", t), cTh[:, 0:2, t * P:(t + 1) * P],
                           bank[2 + t][:, 0:2 * P].rearrange("p (k n) -> p k n", k=2))
                        go(("krT", t), krT[:, t * P:(t + 1) * P], bank[2 + t][:, 2 * P:3 * P])

                ffn(1 + 2 * l, keep_ckv if l else None)

                def keep_kv(c):
                    ahead("kv_up", c)
                    for i in range(2):
                        need("act", "kTf", c, i)
                        go(("kT", c, i), kT[:, 4 * c + 2 * i:4 * c + 2 * i + 2, :],
                           bank[i].rearrange("p (h n) -> p h n", h=2))
                    for t in range(T):
                        need("act", "vf", c, t)
                        go(("vv", c, t), vv[:, t, 4 * c * VD:4 * (c + 1) * VD], bank[2 + t])

                if l == 0:
                    norm_and_turn(2, early=split[0] + 1, b0=4)
                else:
                    norm_and_turn(6, early=split[0] + 1, between=lambda: keep_kv(0), b0=4)
                load_norm(3 + 4 * l)
                if l == 0:
                    act.wait_ge(aux_loaded, 16)
                    go(("fsel",), fsel, fsel_raw[0:FOX_K])
                    def keep_fv(c, b):
                        ahead(f"fox_v{c}")
                        copy_chunk(f"fox_v{c}", (b, b + 1), lambda t: fv[:, t, (c - 4) * CH:(c - 3) * CH])

                    keep_fv(4, 2)
                    ahead("fox_f")
                    need("act", "fz")
                    go(("fabs",), fg[:, 1], fg[:, 0], ACT.Abs)
                    act.wait_ge(act_done, counts["act_done"])
                    go(("fexp",), fg[:, 2], fg[:, 1], ACT.Exp, scale=-1.0)
                    need("act", "fexp1")
                    go(("fln",), fg[:, 3], fg[:, 3], ACT.Ln)

                    def keep_turned(stage, b):
                        ahead(stage)
                        need("act", "full", stage)
                        j = 2 * int(stage[-1])
                        go(("fT", stage), (fqT, fkT)[stage[4] == "k"][:, j:j + 2, :],
                           bank[b].rearrange("p (k n) -> p k n", k=2))

                    keep_turned("fox_q0", 0)
                    go((), cTh[0:FOX_K, 0:2, :], x[0:FOX_K, 0, 0:2 * S].rearrange("p (a n) -> p a n", a=2), scale=0.0)
                    need("act", "cumf")
                    act.wait_ge(act_done, counts["act_done"])
                    go(("cumh",), cTh[0:FOX_H, 0, :], fg[:, 1])
                    go(("ncumh",), cTh[0:FOX_H, 1, :], fg[:, 1], scale=-1.0)
                    keep_turned("fox_k0", 1)
                    u5, uo = unit_at["fox_v5"][0], unit_at["fox_o0"][0]
                    fill = {s: [lambda a=a: keep_turned(*a)] for s, a in FOX_FILL.items()}
                    fill |= {5: [lambda: split_to(u5 + RING)], 6: [lambda: keep_fv(5, 0)],
                             11: [lambda: xT_evac("fox", (0,), b0=2)], 15: [lambda: split_to(uo + 3)],
                             16: [lambda: split_to(uo + 4)]}
                    attention("fox", FOX_H, FOX_DH ** -0.5, fill)
                    xT_evac("fox", (1,), b0=4)
                    split_to(unit_at["ffn2"][0] + 1)
                else:
                    act.dma_start(norm_c[:, 0:QL], bcast_rows(dram["q_norm"], QL)).then_inc(aux_loaded, 16)
                    keep_kv(1)
                    ahead("dq0")
                    for t in range(T):
                        need("act", "full", "dq0", t)
                        go(("cqsq", t), squares[:, t * CH:t * CH + QL], bank[4 + t][:, 0:QL], ACT.Square,
                           accum_out=stats[:, t:t + 1])
                    keep_kv(2)
                    for t in range(T):
                        need("act", "cqTf", t)
                        go(("cqTh", t), cqTh[:, :, t * P:(t + 1) * P],
                           bank[6 + t][:, 0:3 * P].rearrange("p (k n) -> p k n", k=3))

                    def keep_q(g):
                        for t in range(T):
                            need("act", "qf", g, t)
                            if g:
                                need("act", "qTf", g - 1, t)
                            go(("qn", g, t), qs[:, t, 0:2 * NOPE].rearrange("p (h n) -> p h n", h=2),
                               bank[q_bank(g) + t][:, 0:QL].rearrange("p (h n) -> p h n", h=2)[:, :, 0:NOPE])

                    def keep_qT(g):
                        for t in range(T):
                            need("act", "qTf", g, t)
                            if g >= 2:
                                need("act", "S", "mla", 2 * g - 3)
                            go(("qT", g, t), qT[:, g % 2, :, t * P:(t + 1) * P],
                               bank[q_bank(g) + t][:, 0:3 * P].rearrange("p (k n) -> p k n", k=3))

                    def keep_oT(g):
                        need("act", "oTf", g)
                        go(("oTh", g), xTh[:, 2 * g:2 * g + 2, :], bank[O_BANK[g]].rearrange("p (k n) -> p k n", k=2))

                    ahead("uq", 0)
                    keep_q(0)
                    keep_kv(3)
                    keep_qT(0)
                    ahead("uq", 1)
                    keep_q(1)
                    fill = {s: [] for s in range(MLA_H + 2)}
                    for g in range(7):
                        fill[2 * g + 4].append(lambda g=g: keep_oT(g))
                    for g in range(1, 8):
                        fill[2 * g - 2].append(lambda g=g: keep_qT(g))
                    for g in range(2, 8):
                        fill[2 * g - 3] += [lambda g=g: ahead("uq", g), lambda g=g: keep_q(g)]
                    for s, (c, k) in zip((13, 15, 16, 17), ((0, 0), (0, 1), (1, 0), (1, 1))):
                        fill[s].append(lambda c=c, k=k: split_to(unit_at[f"mla_oa{c}"][k] + RING))
                    attention("mla", MLA_H, (NOPE + ROPE_D) ** -0.5, fill)
                    keep_oT(7)
                    ahead("mla_ob0")
                split_to(unit_at[f"ffn{2 + 2 * l}"][0] + 1)
                root_table()
                norm_and_turn(3 + 4 * l, early=unit_at[f"ffn{2 + 2 * l}"][0] + 2, b0=4)
                load_norm(4 + 4 * l)
                need("act", "pTf", l)
                go(("pTh", l), cTh[:, 0:2, :], bank[2].rearrange("p (k n) -> p k n", k=2))
                ffn(2 + 2 * l)
                act.dma_start(pb, bcast_rows(dram["ple_b"][l], D)).then_inc(aux_loaded, 16)
                if l == 0:
                    load_p(1)

                def keep_ple_p(c):
                    if c == 1:
                        ahead(f"ple_p{l}")
                    for t in range(T):
                        need("act", "full", f"ple_p{l}", c, t)
                        go(("ev", f"ple_p{l}", c, t), pp[:, t, c * CH:(c + 1) * CH], bank[4 + 2 * c + t], scale=0.5)

                norm_and_turn(4 + 4 * l, early=unit_at[f"ple_p{l}"][0] + 3,
                              between=lambda: [keep_ple_p(c) for c in range(2)])
                load_norm(5 + 4 * l)

                def ptanh(c, t):
                    need("act", "pz", l, c, t)
                    go(("ptanh", l, c, t), tanh[:, t], pz[:, t], ACT.Tanh, scale=0.5)

                def last_tanh():
                    ptanh(1, 1)
                    act.wait_ge(act_done, counts["act_done"])
                    root_table()

                ahead(f"ple_g{l}0")
                for t in range(T):
                    ptanh(0, t)
                last = unit_at[f"ple_g{l}1"][1]
                split_to(last + 2)
                ptanh(1, 0)
                root_table()
                norm_and_turn(5 + 4 * l, first=last_tanh, early=last + 3)
                if l == 0:
                    load_norm(6)
                    act.dma_start(norm_c[:, 0:KVL], bcast_rows(dram["kv_norm"], KVL)).then_inc(aux_loaded, 16)

        @block.vector
        def _(dve):
            ENG["dve"] = dve
            split = [0]

            def split_to(n):
                while split[0] < min(n, N_UNITS):
                    u = split[0]
                    if u not in pool_units:
                        dve.wait_ge(w_hi_done, u + 1)
                        lo(u % RING, units[u][1] * units[u][2] or UNIT)
                    split[0] += 1

            def lo(slot, cols=UNIT):
                nc.vector.tensor_tensor(w_lo[slot][:, 0:cols], w_raw[slot][:, 0:cols],
                                        w_hi[slot][:, 0:cols].bitcast(F32), ALU.subtract)\
                    .then_inc(w_lo_done[slot], 1)

            def ahead(stage, part=None):
                us = unit_at[stage]
                split_to((us[-1] if part is None else us[part]) + RING)

            def did(ins, *label):
                ins.then_inc(dve_done, mark("dve_done", *label))

            def settle():
                dve.wait_ge(dve_done, counts["dve_done"])

            def rsqrt(n, label=()):
                v, y, a, b = (r[:, 0:n] for r in (rs_v, rs_y, rs_a, rs_b))
                settle()
                did(nc.vector.tensor_scalar(a.bitcast(I32), v.bitcast(I32), 1, None, ALU.logical_shift_right))
                settle()
                did(nc.vector.tensor_scalar(y.bitcast(I32), a.bitcast(I32), -1.0, float(0x5F3759DF), ALU.mult, ALU.add))
                for step in range(3):
                    settle()
                    did(nc.vector.tensor_tensor(a, y, y, ALU.mult))
                    settle()
                    did(nc.vector.scalar_tensor_tensor(out=b, in0=a, scalar=-0.5, in1=v, op0=ALU.mult, op1=ALU.mult))
                    settle()
                    did(nc.vector.scalar_tensor_tensor(out=y, in0=b, scalar=1.5, in1=y, op0=ALU.add, op1=ALU.mult),
                        *(label if step == 2 else ()))
                settle()

            def xT_evac(site, qs_=(0, 1), slot0=0, b0=0, scale=None, tiles=range(T)):
                for t in tiles:
                    for q in qs_:
                        need("dve", "xTh", site, t, q)
                        b = b0 + t * len(qs_) + q - qs_[0]
                        sl = (slice(None), slice(slot0 + 4 * q, slot0 + 4 * q + 4), slice(t * P, (t + 1) * P))
                        src = bank[b].rearrange("p (k n) -> p k n", k=4)
                        if scale is None:
                            did(nc.vector.tensor_tensor(xTl[sl], src, xTh[sl].bitcast(F32), ALU.subtract),
                                "xT", site, t, q)
                        else:
                            did(nc.vector.scalar_tensor_tensor(out=xTl[sl], in0=src, scalar=scale,
                                                               in1=xTh[sl].bitcast(F32), op0=ALU.mult,
                                                               op1=ALU.subtract), "xT", site, t, q)

            def add(t, n, alpha, product, *label):
                cols = slice(n * CH, (n + 1) * CH)
                did(nc.vector.scalar_tensor_tensor(out=x[:, t, cols], in0=x[:, t, cols], scalar=alpha, in1=product,
                                                   op0=ALU.mult, op1=ALU.add,
                                                   accum_out=row_sum[:, 2 * t + n:2 * t + n + 1]), *label)

            def norm_and_turn(site, finish, rms=False, b0=0, middle=None):
                tmp = pp if site in (5, 9) else None

                def mean(t):
                    if rms:
                        note(("sum", site, t), "dve_done", counts["dve_done"])
                        if t:
                            rest(0, 0)
                            rest(0, 1)
                        return
                    settle()
                    did(nc.vector.tensor_scalar(neg_mean[:, t:t + 1], row_sum[:, 2 * t:2 * t + 1],
                                                row_sum[:, 2 * t + 1:2 * t + 2], -1.0 / D, ALU.add, ALU.mult),
                        "mean", site, t)
                    settle()
                    if t == 0:
                        dve.wait_ge(gb_loaded, gb_count(site))
                    else:
                        rest(0, 0)
                        rest(0, 1)
                    for q in range(2):
                        did(nc.vector.scalar_tensor_tensor(out=part(t, q), in0=x[:, t, q * CH:(q + 1) * CH],
                                                           scalar=neg_mean[:, t:t + 1], in1=gb[:, 0, q * CH:(q + 1) * CH],
                                                           op0=ALU.add, op1=ALU.mult))

                def part(t, q):
                    return tanh[:, q] if tmp is None else tmp[:, t, q * CH:(q + 1) * CH]

                def inverse(t):
                    need("dve", "std", site, t)
                    did(nc.vector.reciprocal(rstd[:, t:t + 1], std[:, t:t + 1]))
                    if rms and t == 0:
                        dve.wait_ge(gb_loaded, gb_count(site))
                    settle()

                def apply(t, q):
                    cols = slice(q * CH, (q + 1) * CH)
                    if rms:
                        did(nc.vector.scalar_tensor_tensor(out=normed[:, t, cols], in0=x[:, t, cols],
                                                           scalar=rstd[:, t:t + 1], in1=gb[:, 0, cols],
                                                           op0=ALU.mult, op1=ALU.mult), "norm", site, t, q)
                    else:
                        did(nc.vector.scalar_tensor_tensor(out=x[:, t, cols], in0=part(t, q), scalar=rstd[:, t:t + 1],
                                                           in1=gb[:, 1, cols], op0=ALU.mult, op1=ALU.add),
                            "norm", site, t, q)

                def rest(t, q):
                    if site < 9:
                        xT_evac(site, (q,), b0=b0 + t + q, tiles=(t,))

                finish(0)
                mean(0)
                if middle is not None:
                    middle()
                inverse(0)
                apply(0, 0)
                apply(0, 1)
                finish(1)
                mean(1)
                inverse(1)
                apply(1, 0)
                apply(1, 1)
                rest(1, 0)
                rest(1, 1)

            def ffn(f, alpha, mid=None):
                u0 = unit_at[f"ffn{f}"][0]
                g0 = f * FI
                half = 0.5 if f == 0 else 0.25

                def hidden(i):
                    dve.wait_ge(tanh_done, i + (g0 + 1))
                    nc.vector.scalar_tensor_tensor(out=hid, in0=halves(tanh[:, 0]), scalar=1.0, in1=halves(bank[0]),
                                                   op0=ALU.add, op1=ALU.mult).then_inc(hid_part, 1)

                def hidden_up(i, used):
                    dve.wait_ge(w_used, used)
                    dve.wait_ge(hid_part, i + (g0 + 1))
                    nc.vector.scalar_tensor_tensor(out=hid, in0=hid, scalar=half, in1=halves(bank[1]),
                                                   op0=ALU.mult, op1=ALU.mult).then_inc(hid_done, 1)

                def halves(a):
                    return a.rearrange("p (k n) -> p k n", k=2)

                def hT_rest(i, hh, hl):
                    dve.wait_ge(hT_hi, i + (g0 + 1))
                    nc.vector.tensor_tensor(hl, hid, hh.bitcast(F32), ALU.subtract).then_inc(hT_lo, 1)

                def step(i, last=False):
                    dve.wait_ge(hT_lo, i + g0)
                    dve.wait_ge(w_hi_done, i * 3 + (u0 + 2))
                    lo((u0 + 4) % RING)
                    hidden(i)
                    dve.wait_ge(w_hi_done, i * 3 + (u0 + 3))
                    lo((u0 + 5) % RING)
                    hidden_up(i, i * 3 + (u0 + 1))
                    if last:
                        hT_rest(i, hLh, hLl)
                        return
                    dve.wait_ge(w_hi_done, i * 3 + (u0 + 4))
                    lo((u0 + 6) % RING)
                    hT_rest(i, hTh, hTl)

                split_to(u0 + 3)
                if f:
                    dve.wait_ge(hT_lo, g0)
                hidden(0)
                hidden_up(0, u0 + 2)
                if mid:
                    mid()
                split_to(u0 + 4)
                dve.wait_ge(hT_hi, g0 + 1)
                nc.vector.tensor_tensor(hTl, halves(bank[3]), hTh.bitcast(F32), ALU.subtract).then_inc(hT_lo, 1)
                note(("hT0", f), "hT_lo", g0 + 1)
                with dve.Fori(1, FI - 1) as i:
                    step(i)
                step(FI - 1, True)
                split[0] = u0 + 3 * FI
                split_to(u0 + 3 * FI + 1)

                def finish(t):
                    for n in range(2):
                        need("dve", "ffn_full", f, t, n)
                        add(t, n, alpha, acc[:, t, n * CH:(n + 1) * CH], *(("ffn_out", f, t) if n else ()))
                return finish

            def attention(name, heads, out, dv, fill):
                def soft(h):
                    need("dve", "S", name, h)
                    if h >= 4:
                        need("dve", "exp", name, h - 4)
                    s, a = 2 * (h % 4), 4 * (h % 2)
                    b = bank[4 + h % 2]
                    did(nc.vector.tensor_reduce(rs_a[:, a:a + 1], b[:, 0:P], AX_X, ALU.max))
                    did(nc.vector.tensor_reduce(rs_a[:, a + 1:a + 2], b[:, P:3 * P], AX_X, ALU.max))
                    settle()
                    did(nc.vector.tensor_scalar(negmax[:, s:s + 2], rs_a[:, a:a + 2], -SCALE[name], None, ALU.mult),
                        "soft", name, h)

                def gather(h):
                    need("dve", "PV", name, h)
                    s, r = 2 * (h % 4), 2 * (h % 2)
                    did(nc.vector.reciprocal(rsum[:, r:r + 2], psum_e[:, s:s + 2]))
                    settle()
                    for t in range(T):
                        did(nc.vector.tensor_scalar(out(h, t), bank[7][:, t * dv:(t + 1) * dv],
                                                    rsum[:, r + t:r + t + 1], None, ALU.mult),
                            *(("o", name, h) if t else ()))

                for s in range(heads + 3):
                    if s < heads:
                        soft(s)
                    for work in fill.get(s - 1, ()):
                        work()
                    if 2 <= s < heads + 2:
                        gather(s - 2)

            SCALE = {"moba": MOBA_DH ** -0.5, "fox": FOX_DH ** -0.5, "mla": (NOPE + ROPE_D) ** -0.5}


            def x_tile(t):
                dve.wait_ge(x_loaded[t], 16)
                if t:
                    split_to(1)

            norm_and_turn(0, x_tile, rms=True, b0=4)
            split_to(3)
            dve.wait_ge(const_loaded, N_CONST)
            for n, stage in enumerate(("rq0", "rk0")):
                ahead(stage)
                for t in range(T):
                    need("dve", "full", stage, t)
                    if n or t:
                        settle()
                    b = bank[2 * n + t].rearrange("p (h a n) -> p h a n", h=RET_H, a=2)
                    r = rope_ret[:, t].rearrange("p (a n) -> p a n", a=4)
                    o = rqk[:, 2 * n + t].rearrange("p (h a n) -> p h a n", h=RET_H, a=2)
                    z = rtmp.rearrange("p (h a n) -> p h a n", h=RET_H, a=2)
                    for a in range(2):
                        did(nc.vector.tensor_tensor(z[:, :, a], b[:, :, 1 - a],
                                                    r[:, 2 + a].unsqueeze(1).broadcast_to([P, RET_H, 64]), ALU.mult))
                        did(nc.vector.tensor_tensor(o[:, :, a], b[:, :, a],
                                                    r[:, a].unsqueeze(1).broadcast_to([P, RET_H, 64]), ALU.mult),
                            *(("ev", stage, t) if a else ()))
                    settle()
                    did(nc.vector.tensor_tensor(rqk[:, 2 * n + t], rqk[:, 2 * n + t], rtmp, ALU.add), "rot", n, t)
            ahead("rv0")
            ahead("rv1")

            def decay_scores(h):
                need("dve", "RS", h)
                if h >= 2:
                    need("dve", "RO", h - 2)
                did(nc.vector.tensor_tensor(pT[:, h % 2], bank[4 + h % 2][:, 0:3 * P], decay[:, h], ALU.mult),
                    "decayed", h)

            def ret_moments(g):
                need("dve", "RO", g)
                for t in range(T):
                    did(nc.vector.bn_stats(stats[:, 6 * t:6 * t + 6], bank[6 + g % 2][:, t * RET_DV:(t + 1) * RET_DV]),
                        *(("rstats", g) if t else ()))
                settle()
                for t in range(T):
                    did(nc.vector.bn_aggr(mv_[:, 2 * g + t], stats[:, 6 * t:6 * t + 6]))
                settle()

            def sum_squares(n, stage):
                ahead(stage)
                for t in range(T):
                    need("dve", "msq", n, t)
                    did(nc.vector.tensor_reduce(rs_b[:, 8 * (2 * n + t):8 * (2 * n + t) + 8],
                                                tanh[:, 0].rearrange("p (h n) -> p h n", n=MOBA_DH), AX_X, ALU.add),
                        "mss", 2 * n + t)

            ahead("mq0")
            decay_scores(0)
            decay_scores(1)
            sum_squares(0, "mq0")
            sum_squares(1, "mk0")
            ret_moments(0)
            decay_scores(2)
            ahead("mv0")
            did(nc.vector.tensor_scalar(rs_v, rs_b, 1.0 / MOBA_DH, RMS_EPS, ALU.mult, ALU.add))
            rsqrt(32)
            for i in range(2):
                for t in range(T):
                    m = mqk[:, 2 * i + t].rearrange("p (h n) -> p h n", n=MOBA_DH)
                    y = rs_y[:, 8 * (2 * i + t):8 * (2 * i + t) + 8]
                    did(nc.vector.tensor_tensor(m, m, y.unsqueeze(2).broadcast_to([P, MOBA_H, MOBA_DH]), ALU.mult))
                    settle()
                    did(nc.vector.tensor_tensor(m, m, head_w[:, i].unsqueeze(1).broadcast_to([P, MOBA_H, MOBA_DH]),
                                                ALU.mult), "mnorm", i, t)
            ret_moments(1)
            decay_scores(3)
            ahead("rg0", 0)
            ret_moments(2)
            ahead("rg0")

            def times_gate(n, t):
                need("dve", "tanh", f"rg{n}", t)
                did(nc.vector.scalar_tensor_tensor(out=gated(n, t), in0=gated(n, t), scalar=1.0,
                                                   in1=bank[2 - 2 * n + t], op0=ALU.add, op1=ALU.mult),
                    "ev", f"rg{n}", t)

            def gated(n, t):
                return (tanh[:, t], squares[:, t * CH:(t + 1) * CH])[n]

            for t in range(T):
                times_gate(0, t)
            ret_moments(3)
            did(nc.vector.tensor_scalar(rs_v[:, 0:8], mv_[:, 0:8, 1], GN_EPS, None, ALU.add))
            rsqrt(8)
            need("dve", "ro", RET_H - 1)
            for h in range(RET_H):
                for t in range(T):
                    r = ro[:, t, h * RET_DV:(h + 1) * RET_DV]
                    did(nc.vector.tensor_scalar(r, r, mv_[:, 2 * h + t, 0:1], rs_y[:, 2 * h + t:2 * h + t + 1],
                                                ALU.subtract, ALU.mult))
            settle()
            for n in range(2):
                if n:
                    ahead("rg1")
                    for t in range(T):
                        times_gate(1, t)
                    settle()
                for t in range(T):
                    c = slice(n * CH, (n + 1) * CH)
                    did(nc.vector.scalar_tensor_tensor(out=ro[:, t, c], in0=gated(n, t), scalar=0.5, in1=ro[:, t, c],
                                                       op0=ALU.mult, op1=ALU.mult), "gated", n, t)
            split_to(unit_at["ga0"][0] + RING)
            fill = {s: [lambda u=u: split_to(u + RING)] for s, u in
                    zip((0, 1, 2, 3, 4, 8, 9), [*unit_at["ga0"], *unit_at["ga1"], *unit_at["gb0"], *unit_at["gb1"]][1:])}
            fill[5] = [lambda: xT_evac("ret", (0,), slot0=8)]
            fill[6] = [lambda: xT_evac("ret", (1,), slot0=8, b0=2)]
            attention("moba", MOBA_H, lambda h, t: mo[:, t, h * MOBA_DH:(h + 1) * MOBA_DH], MOBA_DH,
                      fill)
            ahead("ret_out0")
            xT_evac("moba", (0,), b0=4)
            for n in range(2):
                ahead(f"ret_out{n}")
                for t in range(T):
                    need("dve", "full", f"ret_out{n}", t)
                    m = sga[:, t, n * CH:(n + 1) * CH]
                    did(nc.vector.scalar_tensor_tensor(out=m, in0=m, scalar=1.0, in1=bank[2 - 2 * n + t],
                                                       op0=ALU.add, op1=ALU.mult), "ev", f"ret_out{n}", t)
            for n in range(2):
                ahead(f"moba_out{n}")
                for t in range(T):
                    need("dve", "full", f"moba_out{n}", t)
                    c = slice(n * CH, (n + 1) * CH)
                    did(nc.vector.scalar_tensor_tensor(out=sgb[:, t, c], in0=sgb[:, t, c], scalar=1.0,
                                                       in1=bank[2 * n + t], op0=ALU.add, op1=ALU.mult))
                    settle()
                    did(nc.vector.tensor_tensor(sga[:, t, c], sga[:, t, c], sgb[:, t, c], ALU.add),
                        "ev", f"moba_out{n}", t)
                xT_evac("mix", (n,), slot0=8, b0=4 + 2 * n, scale=0.5)

            def update(stage, alpha, banks=(0, 1)):
                for t in range(T):
                    add_chunk(stage, 0, t, banks, alpha)
                split_to(unit_at[f"{stage}1"][-1] + 2)
                return lambda t: add_chunk(stage, 1, t, (2, 3), alpha)

            def add_chunk(stage, n, t, banks, alpha):
                need("dve", "full", f"{stage}{n}", t)
                add(t, n, alpha, bank[banks[t]], "ev", f"{stage}{n}", t)

            ahead("w_o0")
            norm_and_turn(1, update("w_o", 1.0), rms=True, b0=4)
            finish = ffn(0, 1.0)
            for t in range(T):
                finish(t)
            for l in range(2):
                if l == 0:
                    xT_evac("raw", b0=4)
                if l == 1:
                    ahead("kv_down0")
                    for t in range(T):
                        need("dve", "kvsq", t)
                    did(nc.vector.tensor_scalar(rs_v[:, 0:T], stats[:, 0:T], 1.0 / KVL, RMS_EPS, ALU.mult, ALU.add))
                    rsqrt(T)
                    dve.wait_ge(aux_loaded, 48)
                    for t in range(T):
                        did(nc.vector.scalar_tensor_tensor(out=cq[:, t, 0:KVL], in0=bank[4 + t][:, 0:KVL],
                                                           scalar=rs_y[:, t:t + 1], in1=norm_c[:, 0:KVL],
                                                           op0=ALU.mult, op1=ALU.mult))
                        b = bank[4 + t][:, KVL:KVL + ROPE_D].rearrange("p (a n) -> p a n", a=2)
                        r = rope_mla[:, t].rearrange("p (a n) -> p a n", a=4)
                        z = kr[:, t].rearrange("p (c a n) -> p c a n", c=2, a=2)
                        for a in range(2):
                            did(nc.vector.tensor_tensor(z[:, 0, a], b[:, a], r[:, a], ALU.mult))
                            did(nc.vector.tensor_tensor(z[:, 1, a], b[:, 1 - a], r[:, 2 + a], ALU.mult),
                                *(("ev", "kv_down0", t) if a else ()))
                        settle()
                        did(nc.vector.tensor_tensor(kr[:, t, 0:ROPE_D], kr[:, t, 0:ROPE_D], kr[:, t, ROPE_D:], ALU.add))
                        settle()
                        did(nc.vector.tensor_copy(kr[:, t, ROPE_D:], kr[:, t, 0:ROPE_D]), "ckv", t)

                def ckv_rest():
                    for t in range(T):
                        need("dve", "krT", t)
                        did(nc.vector.tensor_tensor(cTl[:, 0:2, t * P:(t + 1) * P],
                                                    bank[2 + t][:, 0:2 * P].rearrange("p (k n) -> p k n", k=2),
                                                    cTh[:, 0:2, t * P:(t + 1) * P].bitcast(F32), ALU.subtract),
                            "ckvT", t)

                norm_and_turn(2 + 4 * l, ffn(1 + 2 * l, ALPHA, ckv_rest if l else None), b0=4)
                if l == 0:
                    ahead("fox_v4")
                    ahead("fox_f")
                    need("dve", "fox_f")
                    did(nc.vector.tensor_scalar(fg[:, 0], bank[4][0:FOX_H, 0:S], fox_b, None, ALU.add), "fz")
                    need("dve", "fexp")
                    did(nc.vector.tensor_scalar(fg[:, 3], fg[:, 2], 1.0, None, ALU.add), "fexp1")
                    did(nc.vector.tensor_scalar(fg[:, 0], fg[:, 0], 0.0, None, ALU.min))
                    settle()
                    need("dve", "fln")
                    did(nc.vector.tensor_tensor_scan(fg[:, 1], fg[:, 0], fg[:, 3], 0.0, ALU.add, ALU.subtract), "cumf")
                    ahead("fox_q0")
                    ahead("fox_k0")
                    need("dve", "ncumh")
                    lo_rows = slice(FOX_LO, FOX_K)
                    did(nc.vector.tensor_tensor(cTh[lo_rows, 0, :], fg[:, 1], cTh[0:FOX_H, 0, :].bitcast(F32),
                                                ALU.subtract))
                    did(nc.vector.scalar_tensor_tensor(out=cTh[lo_rows, 1, :], in0=fg[:, 1], scalar=-1.0,
                                                       in1=cTh[0:FOX_H, 1, :].bitcast(F32), op0=ALU.mult,
                                                       op1=ALU.subtract), "cum")
                    uo = unit_at["fox_o0"][0]
                    attention("fox", FOX_H, lambda h, t: fo[:, t, h * FOX_DH:(h + 1) * FOX_DH], FOX_DH,
                              {10: [lambda: split_to(uo + 1)], 11: [lambda: split_to(uo + 2)],
                               12: [lambda: xT_evac("fox", (0,), b0=2)], 15: [lambda: split_to(uo + 3)],
                               16: [lambda: split_to(uo + 4)]})
                    xT_evac("fox", (1,), b0=4)
                    split_to(unit_at["ffn2"][0] + 1)
                    finish = update("fox_o", ALPHA)
                else:
                    ahead("dq0")
                    for t in range(T):
                        need("dve", "cqsq", t)
                    did(nc.vector.tensor_scalar(rs_v[:, 0:T], stats[:, 0:T], 1.0 / QL, RMS_EPS, ALU.mult, ALU.add))
                    rsqrt(T)
                    dve.wait_ge(aux_loaded, 64)
                    for t in range(T):
                        did(nc.vector.scalar_tensor_tensor(out=cq[:, t], in0=bank[4 + t][:, 0:QL],
                                                           scalar=rs_y[:, t:t + 1], in1=norm_c,
                                                           op0=ALU.mult, op1=ALU.mult), "cqn", t)
                        note(("ev", "dq0", t), "dve_done", counts["dve_done"])
                    ahead("kv_up", 3)
                    for t in range(T):
                        need("dve", "cqTh", t)
                        did(nc.vector.tensor_tensor(cqTl[:, :, t * P:(t + 1) * P],
                                                    bank[6 + t][:, 0:3 * P].rearrange("p (k n) -> p k n", k=3),
                                                    cqTh[:, :, t * P:(t + 1) * P].bitcast(F32), ALU.subtract),
                            "cqT", t)

                    def rope_q(g):
                        for t in range(T):
                            need("dve", "qn", g, t)
                            b = bank[q_bank(g) + t][:, 0:QL].rearrange("p (h n) -> p h n", h=2)[:, :, NOPE:]
                            r = rope_mla[:, t].rearrange("p (a n) -> p a n", a=4)
                            o = qs[:, t, 2 * NOPE:].rearrange("p (h n) -> p h n", h=2)
                            z = kr[:, t].rearrange("p (h n) -> p h n", h=2)
                            for a in range(2):
                                lo_, hi_ = slice(32 * a, 32 * a + 32), slice(32 - 32 * a, 64 - 32 * a)
                                rb = [r[:, q].unsqueeze(1).broadcast_to([P, 2, 32]) for q in (a, 2 + a)]
                                did(nc.vector.tensor_tensor(o[:, :, lo_], b[:, :, lo_], rb[0], ALU.mult))
                                did(nc.vector.tensor_tensor(z[:, :, lo_], b[:, :, hi_], rb[1], ALU.mult))
                            settle()
                            did(nc.vector.tensor_tensor(qs[:, t, 2 * NOPE:], qs[:, t, 2 * NOPE:], kr[:, t], ALU.add),
                                "qs", g, t)

                    def rest_oT(g):
                        need("dve", "oTh", g)
                        did(nc.vector.tensor_tensor(xTl[:, 2 * g:2 * g + 2, :],
                                                    bank[O_BANK[g]].rearrange("p (k n) -> p k n", k=2),
                                                    xTh[:, 2 * g:2 * g + 2, :].bitcast(F32), ALU.subtract), "oT", g)

                    rope_q(0)
                    rope_q(1)
                    fill = {s: [] for s in range(MLA_H + 2)}
                    for g in range(7):
                        fill[2 * g + 4].append(lambda g=g: rest_oT(g))
                    for g in range(2, 8):
                        fill[2 * g - 3].append(lambda g=g: rope_q(g))
                    fill[15] += [lambda t=t: add_chunk("mla_oa", 0, t, (2, 3), ALPHA) for t in range(T)]
                    fill[16].append(lambda: ahead("mla_oa1", 0))
                    fill[17] += [lambda t=t: add_chunk("mla_oa", 1, t, (2, 3), ALPHA) for t in range(T)]
                    fill[17].append(lambda: ahead("mla_oa1"))
                    attention("mla", MLA_H, lambda h, t: mlo[:, (h // 2) % 2, t, (h % 2) * VD:(h % 2 + 1) * VD], VD, fill)
                    rest_oT(7)
                    ahead("mla_ob0")
                    finish = update("mla_ob", 1.0, (4, 5))
                norm_and_turn(3 + 4 * l, finish, b0=4)
                need("dve", "pTh", l)
                did(nc.vector.tensor_tensor(cTl[:, 0:2, :], bank[2].rearrange("p (k n) -> p k n", k=2),
                                            cTh[:, 0:2, :].bitcast(F32), ALU.subtract), "pT", l)
                add_ffn = ffn(2 + 2 * l, ALPHA)

                def finish_ffn(t):
                    if t:
                        split_to(unit_at[f"ple_p{l}"][0] + 2)
                    add_ffn(t)

                norm_and_turn(4 + 4 * l, finish_ffn)
                ahead(f"ple_p{l}")
                dve.wait_ge(aux_loaded, (32, 80)[l])

                def ple_gate(c, t):
                    need("dve", "full", f"ple_g{l}{c}", t)
                    if c:
                        need("dve", "ptanh", l, 0, t)
                    did(nc.vector.tensor_tensor(pz[:, t], bank[2 * c + t], pb[:, c * CH:(c + 1) * CH], ALU.add),
                        "pz", l, c, t)
                    note(("ev", f"ple_g{l}{c}", t), "dve_done", counts["dve_done"])

                def ple_add(c, t):
                    cols = slice(c * CH, (c + 1) * CH)
                    need("dve", "ptanh", l, c, t)
                    need("dve", "ev", f"ple_p{l}", c, t)
                    did(nc.vector.scalar_tensor_tensor(out=tanh[:, t], in0=tanh[:, t], scalar=1.0,
                                                       in1=pp[:, t, cols], op0=ALU.add, op1=ALU.mult))
                    settle()
                    add(t, c, ALPHA, tanh[:, t])

                ahead(f"ple_g{l}0")
                for t in range(T):
                    ple_gate(0, t)
                for t in range(T):
                    ple_add(0, t)
                split_to(unit_at[f"ple_g{l}1"][1] + 2)
                ple_gate(1, 0)
                norm_and_turn(5 + 4 * l, lambda t: ple_add(1, t), middle=lambda: ple_gate(1, 1))
    return found


def kernel(**inputs):
    import concourse.bacc as bacc
    from concourse.bass_utils import run_bass_kernel_spmd

    a = {n: np.asarray(v) for n, v in inputs.items()}
    arrays = {"x": a["x"].reshape(S, D)}
    for n in ("norm1_w", "w_in", "q_norm_w", "k_norm_w", "w_ret_out", "w_moba_out", "w_o", "norm2_w", "w_ffn_gate",
              "w_ffn_up", "w_ffn_down"):
        arrays[n] = a[n][0]
    arrays["p"] = a["p_2"].reshape(2, S, PLE)
    for n in ("ffn1_w_in", "ffn1_w_out", "ffn2_w_in", "ffn2_w_out", "ln_g", "ln_b", "ple_w_gate", "ple_w_proj"):
        arrays[n] = a[n + "_2"]
    arrays["ple_b"] = a["ple_b_gate_2"]
    for n in ("fox_w_in", "fox_b_f", "fox_w_o", "mla_w_dq", "mla_w_o"):
        arrays[n] = a[n + "_2"][0]
    arrays["q_norm"] = a["mla_q_norm_2"][0]
    arrays["mla_w_uq"] = a["mla_w_uq_2"].reshape(QL, MLA_H * (NOPE + ROPE_D))
    arrays["kv_w_down"], arrays["kv_norm"] = a["kv_w_down_2"], a["kv_norm_2"]
    arrays["kv_w_up"] = a["kv_w_up_2"].reshape(KVL, MLA_H * (NOPE + VD))
    arrays.update(shape_constants())
    arrays = {f"in_{n}": np.ascontiguousarray(v) for n, v in arrays.items()}

    def program(marks):
        nc = bacc.Bacc("TRN2", target_bir_lowering=False, num_devices=1)
        dram = {n[3:]: nc.dram_tensor(n, v.shape, mybir.dt.from_np(v.dtype), kind="ExternalInput").ap()
                for n, v in arrays.items()}
        dram["out"] = nc.dram_tensor("out_x", (S, D), F32, kind="ExternalOutput").ap()
        return nc, build(nc, dram, marks)

    _, marks = program({})
    nc, again = program(marks)
    assert again == marks
    r = run_bass_kernel_spmd(nc, [arrays], core_ids=[0])
    return r.results[0]["out_x"].reshape(1, S, D)
```
